# Optimizing a Trainium2 kernel written in Bass

```python
import math
import jax, jax.numpy as jnp
from jax import lax
import numpy as np

D_MODEL = 1024
BATCH = 1
SEQ = 512
DEPTH = 1

CHUNK = 64
HEAD_DIM = 64
D_A = 384
HEADS_A = D_A // HEAD_DIM
D_B = 256
HEADS_B = D_B // HEAD_DIM
D_C = 384
HEADS_C = D_C // HEAD_DIM
D_MIX = D_A + D_B + D_C
IN_COLS = 2 * D_A + 3 * D_B + 2 * D_C
CONV_A_WIDTH = 31
CONV_B_WIDTH = 3
SG_BLOCK = 128
PEER_HEADS = 8
D_KEY = 256
N_KEYS = 128
N_EXPERTS = N_KEYS * N_KEYS
TOPK = 16
PEER_BLOCK = 128
PLE_DIM = 256
EPS = 1e-6


def rmsnorm(x, g):
    xf = x.astype(jnp.float32)
    y = xf * lax.rsqrt(jnp.mean(xf * xf, axis=-1, keepdims=True) + EPS)
    return (y * g.astype(jnp.float32)).astype(x.dtype)

def group_layernorm(x, g, b, heads):
    shp = x.shape
    xf = x.astype(jnp.float32).reshape(shp[:-1] + (heads, shp[-1] // heads))
    m = jnp.mean(xf, axis=-1, keepdims=True)
    var = jnp.mean(jnp.square(xf - m), axis=-1, keepdims=True)
    y = ((xf - m) * lax.rsqrt(var + EPS)).reshape(shp)
    return (y * g.astype(jnp.float32) + b.astype(jnp.float32)).astype(x.dtype)

def causal_dwconv(x, w):
    k = w.shape[0]
    return lax.conv_general_dilated(
        x, w.astype(x.dtype)[:, None, :], window_strides=(1,), padding=[(k - 1, 0)],
        dimension_numbers=("NWC", "WIO", "NWC"), feature_group_count=x.shape[-1])

def conformer_conv(za, conv_w, conv_b, ln_g, ln_b):
    val, gate = jnp.split(za, 2, axis=-1)
    y = val * jax.nn.sigmoid(gate)
    y = causal_dwconv(y, conv_w) + conv_b.astype(y.dtype)
    y = group_layernorm(y, ln_g, ln_b, HEADS_A)
    return jax.nn.silu(y)

def short_gated_conv(zb, conv_w):
    bg, cg, xb = jnp.split(zb, 3, axis=-1)
    return bg * causal_dwconv(cg * xb, conv_w)

def spatial_gating(zc, ln_g, ln_b, w_s, b_s):
    u, v = jnp.split(zc, 2, axis=-1)
    bsz, s, _ = v.shape
    v = group_layernorm(v, ln_g, ln_b, HEADS_C)
    vb = v.reshape(bsz, s // SG_BLOCK, SG_BLOCK, HEADS_C, HEAD_DIM)
    pos = jnp.arange(SG_BLOCK)
    mask = (pos[None, :] // CHUNK) <= (pos[:, None] // CHUNK)
    ws = jnp.where(mask[None], w_s, 0).astype(v.dtype)
    mixed = jnp.einsum("hij,bnjhc->bnihc", ws, vb) + b_s.T.astype(v.dtype)[None, None, :, :, None]
    return u * mixed.reshape(bsz, s, D_C)

def peer(n, w_q, sub_keys, expert_u, expert_v):
    bsz, s, d = n.shape
    t = bsz * s
    nf = n.reshape(t, d)
    q = (nf @ w_q).reshape(t, PEER_HEADS, D_KEY)
    q1, q2 = q[..., : D_KEY // 2], q[..., D_KEY // 2:]
    s1 = jnp.einsum("thd,hkd->thk", q1, sub_keys[:, 0])
    s2 = jnp.einsum("thd,hkd->thk", q2, sub_keys[:, 1])
    v1, i1 = lax.top_k(s1, TOPK)
    v2, i2 = lax.top_k(s2, TOPK)
    cand = (v1[..., :, None] + v2[..., None, :]).reshape(t, PEER_HEADS, TOPK * TOPK)
    vals, ci = lax.top_k(cand, TOPK)
    e1 = jnp.take_along_axis(i1, ci // TOPK, axis=-1)
    e2 = jnp.take_along_axis(i2, ci % TOPK, axis=-1)
    idx = (e1 * N_KEYS + e2).reshape(t, PEER_HEADS * TOPK)
    gates = jax.nn.softmax(vals.astype(jnp.float32), axis=-1).astype(n.dtype)
    gates = gates.reshape(t, PEER_HEADS * TOPK)
    nblk = t // PEER_BLOCK

    def block(args):
        xb, ib, gb = args
        ug = expert_u[ib]
        act = jax.nn.gelu(jnp.einsum("td,tkd->tk", xb, ug)) * gb
        vg = expert_v[ib]
        return jnp.einsum("tk,tkd->td", act, vg)

    out = lax.map(block, (nf.reshape(nblk, PEER_BLOCK, d),
                          idx.reshape(nblk, PEER_BLOCK, PEER_HEADS * TOPK),
                          gates.reshape(nblk, PEER_BLOCK, PEER_HEADS * TOPK)))
    return out.reshape(bsz, s, d)

def first_inputs(seed: int = 0) -> dict:
    key = jax.random.key(seed)
    ks = jax.random.split(key, 24)
    L, D = DEPTH, D_MODEL
    nrm = lambda k, shp, sc: jax.random.normal(k, shp, jnp.float32) * sc
    gain = lambda k, shp: 1.0 + 0.05 * jax.random.normal(k, shp, jnp.float32)
    return {
        "x": nrm(ks[0], (BATCH, SEQ, D), 1.0),
        "p": nrm(ks[1], (DEPTH, BATCH, SEQ, PLE_DIM), 1.0),
        "g_mix": gain(ks[2], (L, D)),
        "w_in": nrm(ks[3], (L, D, IN_COLS), D ** -0.5),
        "conv_a_w": nrm(ks[4], (L, CONV_A_WIDTH, D_A), CONV_A_WIDTH ** -0.5),
        "conv_a_b": nrm(ks[5], (L, D_A), 0.02),
        "ln_a_g": gain(ks[6], (L, D_A)),
        "ln_a_b": nrm(ks[7], (L, D_A), 0.02),
        "conv_b_w": nrm(ks[8], (L, CONV_B_WIDTH, D_B), CONV_B_WIDTH ** -0.5),
        "ln_c_g": gain(ks[9], (L, D_C)),
        "ln_c_b": nrm(ks[10], (L, D_C), 0.02),
        "w_s": nrm(ks[11], (L, HEADS_C, SG_BLOCK, SG_BLOCK), 0.5 * SG_BLOCK ** -0.5),
        "b_s": gain(ks[12], (L, HEADS_C, SG_BLOCK)),
        "w_out": nrm(ks[13], (L, D_MIX, D), D_MIX ** -0.5),
        "g_ffn": gain(ks[14], (L, D)),
        "w_q": nrm(ks[15], (L, D, PEER_HEADS * D_KEY), D ** -0.5),
        "sub_keys": nrm(ks[16], (L, PEER_HEADS, 2, N_KEYS, D_KEY // 2), (D_KEY // 2) ** -0.5),
        "expert_u": nrm(ks[17], (L, N_EXPERTS, D), D ** -0.5),
        "expert_v": nrm(ks[18], (L, N_EXPERTS, D), 0.1),
        "g_ple": gain(ks[19], (L, D)),
        "w_pe": nrm(ks[20], (L, PLE_DIM, D), PLE_DIM ** -0.5),
        "w_pg": nrm(ks[21], (L, D, D), D ** -0.5),
        "g_final": gain(ks[22], (D,)),
    }

def first_block(x, p, g_mix, w_in, conv_a_w, conv_a_b, ln_a_g, ln_a_b, conv_b_w, ln_c_g, ln_c_b,
              w_s, b_s, w_out, g_ffn, w_q, sub_keys, expert_u, expert_v, g_ple, w_pe, w_pg,
              g_final):
    h = x
    for i in range(DEPTH):
        a = rmsnorm(h, g_mix[i])
        z = a @ w_in[i]
        za = z[..., : 2 * D_A]
        zb = z[..., 2 * D_A: 2 * D_A + 3 * D_B]
        zc = z[..., 2 * D_A + 3 * D_B:]
        ya = conformer_conv(za, conv_a_w[i], conv_a_b[i], ln_a_g[i], ln_a_b[i])
        yb = short_gated_conv(zb, conv_b_w[i])
        yc = spatial_gating(zc, ln_c_g[i], ln_c_b[i], w_s[i], b_s[i])
        h = h + jnp.concatenate([ya, yb, yc], axis=-1) @ w_out[i]
        h = h + peer(rmsnorm(h, g_ffn[i]), w_q[i], sub_keys[i], expert_u[i], expert_v[i])
        gate = jax.nn.sigmoid(rmsnorm(h, g_ple[i]) @ w_pg[i])
        h = h + (p[i] @ w_pe[i]) * gate
    return rmsnorm(h, g_final)


DEPTH_2 = 2

N_A_LAYERS = DEPTH_2 // 2
N_B_LAYERS = DEPTH_2 - N_A_LAYERS
SSM_DIM = D_MODEL
SSM_GROUP_DIM = 16
SSM_GROUPS = SSM_DIM // SSM_GROUP_DIM
SSM_STATE = 64
SSM_CHUNK = 128
N_HEADS = 8
Q_BLOCK = 128
REL_BUCKETS = 32
REL_MAX_EXACT = REL_BUCKETS // 2
REL_MAX_DIST = 128
D_FF = 2816
CONV_WIDTH = 3
NEG_INF = -1e30


def rms_norm(x, g):
    xf = x.astype(jnp.float32)
    y = xf * lax.rsqrt(jnp.mean(xf * xf, axis=-1, keepdims=True) + EPS)
    return (y * g.astype(jnp.float32)).astype(x.dtype)

def _ssm_combine(e_i, e_j):
    ar_i, ai_i, br_i, bi_i = e_i
    ar_j, ai_j, br_j, bi_j = e_j
    return (ar_j * ar_i - ai_j * ai_i,
            ar_j * ai_i + ai_j * ar_i,
            ar_j * br_i - ai_j * bi_i + br_j,
            ar_j * bi_i + ai_j * br_i + bi_j)

def s5_mixer(h, w_in, log_dt, lam_re, lam_im, b_re, b_im, c_re, c_im, d_skip, w_glu):
    f32 = jnp.float32
    bsz, seqlen, _ = h.shape
    u = h @ w_in
    dt = jnp.exp(log_dt.astype(f32))[:, None]
    lr = lam_re.astype(f32)
    li = lam_im.astype(f32)
    mag = jnp.exp(lr * dt)
    ab_r = mag * jnp.cos(li * dt)
    ab_i = mag * jnp.sin(li * dt)
    den = lr * lr + li * li
    f_r = ((ab_r - 1.0) * lr + ab_i * li) / den
    f_i = (ab_i * lr - (ab_r - 1.0) * li) / den
    br = b_re.astype(f32)
    bi = b_im.astype(f32)
    bb_r = f_r[..., None] * br - f_i[..., None] * bi
    bb_i = f_r[..., None] * bi + f_i[..., None] * br
    cr = c_re.astype(f32)
    ci = c_im.astype(f32)
    n_chunks = seqlen // SSM_CHUNK
    uc = u.astype(f32).reshape(bsz, n_chunks, SSM_CHUNK, SSM_GROUPS, SSM_GROUP_DIM)
    uc = uc.transpose(1, 2, 0, 3, 4)
    a_shape = (SSM_CHUNK, bsz, SSM_GROUPS, SSM_STATE)
    a_r = jnp.broadcast_to(ab_r, a_shape)
    a_i = jnp.broadcast_to(ab_i, a_shape)

    def chunk_step(carry, u_chunk):
        x_r0, x_i0 = carry
        bu_r = jnp.einsum("tbgc,gpc->tbgp", u_chunk, bb_r)
        bu_i = jnp.einsum("tbgc,gpc->tbgp", u_chunk, bb_i)
        pw_r, pw_i, s_r, s_i = lax.associative_scan(
            _ssm_combine, (a_r, a_i, bu_r, bu_i), axis=0)
        x_r = s_r + pw_r * x_r0 - pw_i * x_i0
        x_i = s_i + pw_r * x_i0 + pw_i * x_r0
        y = (jnp.einsum("tbgp,gcp->tbgc", x_r, cr)
             - jnp.einsum("tbgp,gcp->tbgc", x_i, ci))
        return (x_r[-1], x_i[-1]), y

    zeros = jnp.zeros((bsz, SSM_GROUPS, SSM_STATE), f32)
    _, ys = lax.scan(chunk_step, (zeros, zeros), uc)
    y = ys.transpose(2, 0, 1, 3, 4).reshape(bsz, seqlen, SSM_DIM)
    y = y + d_skip.astype(f32) * u.astype(f32)
    g = jax.nn.gelu(y).astype(h.dtype)
    val, gate = jnp.split(g @ w_glu, 2, axis=-1)
    return val * jax.nn.sigmoid(gate)

def t5_causal_bucket(rel):
    n = jnp.maximum(-rel, 0)
    nf = jnp.maximum(n, REL_MAX_EXACT).astype(jnp.float32)
    large = REL_MAX_EXACT + (jnp.log(nf / REL_MAX_EXACT)
                             / math.log(REL_MAX_DIST / REL_MAX_EXACT)
                             * (REL_BUCKETS - REL_MAX_EXACT)).astype(jnp.int32)
    large = jnp.minimum(large, REL_BUCKETS - 1)
    return jnp.where(n < REL_MAX_EXACT, n, large)

def shared_kv(x, kv_norm, kv_w, k_norm):
    bsz, seqlen, _ = x.shape
    kv = rms_norm(x, kv_norm) @ kv_w
    nk = 2 * N_HEADS * HEAD_DIM
    k = rms_norm(kv[..., :nk].reshape(bsz, seqlen, N_HEADS, 2, HEAD_DIM), k_norm)
    v = kv[..., nk:].reshape(bsz, seqlen, N_HEADS, 2 * HEAD_DIM)
    return k, v

def diff_attention(h, k, v, rel_bias, w_q, q_norm, lq1, lk1, lq2, lk2, subln, w_o, lam_init):
    f32 = jnp.float32
    bsz, seqlen, _ = h.shape
    q = rms_norm((h @ w_q).reshape(bsz, seqlen, N_HEADS, 2, HEAD_DIM), q_norm)
    lam = (jnp.exp(jnp.sum(lq1.astype(f32) * lk1.astype(f32)))
           - jnp.exp(jnp.sum(lq2.astype(f32) * lk2.astype(f32))) + lam_init)
    scale = HEAD_DIM ** -0.5
    n_blocks = seqlen // Q_BLOCK
    qb = q.reshape(bsz, n_blocks, Q_BLOCK, N_HEADS, 2, HEAD_DIM).transpose(1, 0, 2, 3, 4, 5)
    k_pos = jnp.arange(seqlen)

    def block(args):
        idx, qc = args
        q_pos = idx * Q_BLOCK + jnp.arange(Q_BLOCK)
        rel = k_pos[None, :] - q_pos[:, None]
        bias = rel_bias[t5_causal_bucket(rel)].astype(f32).transpose(2, 0, 1)
        s = jnp.einsum("bqhcd,bkhcd->bhcqk", qc, k).astype(f32) * scale
        s = s + bias[None, :, None]
        s = jnp.where(rel <= 0, s, NEG_INF)
        pm = jax.nn.softmax(s, axis=-1)
        attn = pm[:, :, 0] - lam * pm[:, :, 1]
        return jnp.einsum("bhqk,bkhe->bqhe", attn.astype(v.dtype), v)

    o = lax.map(block, (jnp.arange(n_blocks), qb))
    o = o.transpose(1, 0, 2, 3, 4).reshape(bsz, seqlen, N_HEADS, 2 * HEAD_DIM)
    o = rms_norm(o, subln) * (1.0 - lam_init)
    return o.reshape(bsz, seqlen, N_HEADS * 2 * HEAD_DIM) @ w_o

def conv_ffn(h, w_up, conv_w, conv_b, w_down):
    up = h @ w_up
    seqlen = up.shape[1]
    padded = jnp.pad(up, ((0, 0), (CONV_WIDTH - 1, 0), (0, 0)))
    c = conv_b
    for j in range(CONV_WIDTH):
        c = c + conv_w[j] * padded[:, j:j + seqlen]
    g, val = jnp.split(c, 2, axis=-1)
    return (jax.nn.gelu(g) * val) @ w_down

def second_inputs(seed: int = 0) -> dict:
    key = jax.random.key(seed)
    ks = iter(jax.random.split(key, 40))
    f32 = jnp.float32

    def nrm(shape, scale):
        return jax.random.normal(next(ks), shape, f32) * scale

    def gain(shape):
        return 1.0 + nrm(shape, 0.05)

    na, nb = N_A_LAYERS, N_B_LAYERS
    lam_im = jnp.pi * jnp.arange(SSM_STATE, dtype=f32)
    return {
        "x": nrm((BATCH, SEQ, D_MODEL), 1.0),
        "p": nrm((DEPTH_2, BATCH, SEQ, PLE_DIM), 1.0),
        "ssm_norm": gain((na, D_MODEL)),
        "ssm_w_in": nrm((na, D_MODEL, SSM_DIM), D_MODEL ** -0.5),
        "ssm_log_dt": jax.random.uniform(next(ks), (na, SSM_GROUPS), f32,
                                         math.log(1e-3), math.log(1e-1)),
        "ssm_lambda_re": -0.5 + nrm((na, SSM_GROUPS, SSM_STATE), 0.01),
        "ssm_lambda_im": lam_im + nrm((na, SSM_GROUPS, SSM_STATE), 0.01),
        "ssm_b_re": nrm((na, SSM_GROUPS, SSM_STATE, SSM_GROUP_DIM), SSM_GROUP_DIM ** -0.5),
        "ssm_b_im": nrm((na, SSM_GROUPS, SSM_STATE, SSM_GROUP_DIM), SSM_GROUP_DIM ** -0.5),
        "ssm_c_re": nrm((na, SSM_GROUPS, SSM_GROUP_DIM, SSM_STATE), SSM_STATE ** -0.5),
        "ssm_c_im": nrm((na, SSM_GROUPS, SSM_GROUP_DIM, SSM_STATE), SSM_STATE ** -0.5),
        "ssm_d": nrm((na, SSM_DIM), 0.5),
        "ssm_w_glu": nrm((na, SSM_DIM, 2 * D_MODEL), SSM_DIM ** -0.5),
        "kv_norm": gain((D_MODEL,)),
        "kv_w": nrm((D_MODEL, 2 * N_HEADS * HEAD_DIM + N_HEADS * 2 * HEAD_DIM), D_MODEL ** -0.5),
        "k_norm": gain((HEAD_DIM,)),
        "attn_norm": gain((nb, D_MODEL)),
        "attn_w_q": nrm((nb, D_MODEL, 2 * N_HEADS * HEAD_DIM), D_MODEL ** -0.5),
        "q_norm": gain((nb, HEAD_DIM)),
        "lambda_q1": nrm((nb, HEAD_DIM), 0.1),
        "lambda_k1": nrm((nb, HEAD_DIM), 0.1),
        "lambda_q2": nrm((nb, HEAD_DIM), 0.1),
        "lambda_k2": nrm((nb, HEAD_DIM), 0.1),
        "subln": gain((nb, 2 * HEAD_DIM)),
        "attn_w_o": nrm((nb, N_HEADS * 2 * HEAD_DIM, D_MODEL), (N_HEADS * 2 * HEAD_DIM) ** -0.5),
        "rel_bias": nrm((REL_BUCKETS, N_HEADS), 0.5),
        "ffn_norm": gain((DEPTH_2, D_MODEL)),
        "ffn_w_up": nrm((DEPTH_2, D_MODEL, 2 * D_FF), D_MODEL ** -0.5),
        "ffn_conv_w": nrm((DEPTH_2, CONV_WIDTH, 2 * D_FF), CONV_WIDTH ** -0.5),
        "ffn_conv_b": nrm((DEPTH_2, 2 * D_FF), 0.02),
        "ffn_w_down": nrm((DEPTH_2, D_FF, D_MODEL), D_FF ** -0.5),
        "ple_norm": gain((DEPTH_2, D_MODEL)),
        "ple_w_gate": nrm((DEPTH_2, D_MODEL, D_MODEL), D_MODEL ** -0.5),
        "ple_w_proj": nrm((DEPTH_2, PLE_DIM, D_MODEL), PLE_DIM ** -0.5),
    }

def second_block(x, p, ssm_norm, ssm_w_in, ssm_log_dt, ssm_lambda_re, ssm_lambda_im,
              ssm_b_re, ssm_b_im, ssm_c_re, ssm_c_im, ssm_d, ssm_w_glu,
              kv_norm, kv_w, k_norm, attn_norm, attn_w_q, q_norm,
              lambda_q1, lambda_k1, lambda_q2, lambda_k2, subln, attn_w_o, rel_bias,
              ffn_norm, ffn_w_up, ffn_conv_w, ffn_conv_b, ffn_w_down,
              ple_norm, ple_w_gate, ple_w_proj):
    k = v = None
    for i in range(DEPTH_2):
        if i < N_A_LAYERS:
            h = rms_norm(x, ssm_norm[i])
            x = x + s5_mixer(h, ssm_w_in[i], ssm_log_dt[i], ssm_lambda_re[i], ssm_lambda_im[i],
                             ssm_b_re[i], ssm_b_im[i], ssm_c_re[i], ssm_c_im[i],
                             ssm_d[i], ssm_w_glu[i])
        else:
            if i == N_A_LAYERS:
                k, v = shared_kv(x, kv_norm, kv_w, k_norm)
            j = i - N_A_LAYERS
            lam_init = 0.8 - 0.6 * math.exp(-0.3 * i)
            h = rms_norm(x, attn_norm[j])
            x = x + diff_attention(h, k, v, rel_bias, attn_w_q[j], q_norm[j],
                                   lambda_q1[j], lambda_k1[j], lambda_q2[j], lambda_k2[j],
                                   subln[j], attn_w_o[j], lam_init)
        h = rms_norm(x, ffn_norm[i])
        x = x + conv_ffn(h, ffn_w_up[i], ffn_conv_w[i], ffn_conv_b[i], ffn_w_down[i])
        gate = jax.nn.sigmoid(rms_norm(x, ple_norm[i]) @ ple_w_gate[i])
        x = x + gate * (p[i] @ ple_w_proj[i])
    return x


def setup_inputs(seed=0):
    out = dict(first_inputs(seed))
    for name, value in second_inputs(seed + 1).items():
        if name != "x":
            out[name + "_2"] = value
    return out


def reference(
    x, p, g_mix, w_in, conv_a_w, conv_a_b, ln_a_g, ln_a_b, conv_b_w, ln_c_g, ln_c_b, w_s, b_s,
    w_out, g_ffn, w_q, sub_keys, expert_u, expert_v, g_ple, w_pe, w_pg, g_final, p_2,
    ssm_norm_2, ssm_w_in_2, ssm_log_dt_2, ssm_lambda_re_2, ssm_lambda_im_2, ssm_b_re_2,
    ssm_b_im_2, ssm_c_re_2, ssm_c_im_2, ssm_d_2, ssm_w_glu_2, kv_norm_2, kv_w_2, k_norm_2,
    attn_norm_2, attn_w_q_2, q_norm_2, lambda_q1_2, lambda_k1_2, lambda_q2_2, lambda_k2_2,
    subln_2, attn_w_o_2, rel_bias_2, ffn_norm_2, ffn_w_up_2, ffn_conv_w_2, ffn_conv_b_2,
    ffn_w_down_2, ple_norm_2, ple_w_gate_2, ple_w_proj_2,
):
    x = first_block(
        x, p, g_mix, w_in, conv_a_w, conv_a_b, ln_a_g, ln_a_b, conv_b_w, ln_c_g, ln_c_b, w_s,
        b_s, w_out, g_ffn, w_q, sub_keys, expert_u, expert_v, g_ple, w_pe, w_pg, g_final,
    )
    return second_block(
        x, p_2, ssm_norm_2, ssm_w_in_2, ssm_log_dt_2, ssm_lambda_re_2, ssm_lambda_im_2,
        ssm_b_re_2, ssm_b_im_2, ssm_c_re_2, ssm_c_im_2, ssm_d_2, ssm_w_glu_2, kv_norm_2, kv_w_2,
        k_norm_2, attn_norm_2, attn_w_q_2, q_norm_2, lambda_q1_2, lambda_k1_2, lambda_q2_2,
        lambda_k2_2, subln_2, attn_w_o_2, rel_bias_2, ffn_norm_2, ffn_w_up_2, ffn_conv_w_2,
        ffn_conv_b_2, ffn_w_down_2, ple_norm_2, ple_w_gate_2, ple_w_proj_2,
    )


_drawn_inputs = setup_inputs


def setup_inputs(seed=0):
    import zlib

    import numpy as np

    out = dict(_drawn_inputs(seed))
    spreads = {}
    factors = {'ln_a_b': 5.007,
     'ln_c_g': 4.753,
     'ln_c_b': 8.0,
     'g_ffn': 5.452,
     'g_ple': 6.415,
     'ssm_norm_2': 5.335,
     'ssm_lambda_re_2': 64.0,
     'k_norm_2': 9.032,
     'attn_norm_2': 2.739,
     'lambda_k1_2': 4.478,
     'lambda_k2_2': 5.076,
     'ple_norm_2': 5.181,
     'subln_2': 3.206,
     'ffn_conv_b_2': 3.332}
    for name, (base, spread) in spreads.items():
        noise = np.random.default_rng([zlib.crc32(name.encode()), seed]).standard_normal(out[name].shape)
        drawn = base * np.exp(spread * noise) if base else spread * noise
        out[name] = __import__('jax').numpy.asarray(drawn.astype(out[name].dtype))
    for name, factor in factors.items():
        out[name] = (out[name] * factor).astype(out[name].dtype)
    return out
```

```python
import math
from contextlib import ExitStack

import numpy as np
import concourse.bass as bass
from concourse import mybir

F32 = mybir.dt.float32
F16, BF16 = mybir.dt.float16, mybir.dt.bfloat16
U32 = mybir.dt.uint32
ALU = mybir.AluOpType
ACT = mybir.ActivationFunctionType
AX = mybir.AxisListType.X

P = 128
SEQ, D = 512, 1024
KT = D // P
NT = SEQ // P
EPS = 1e-6
D_A, D_B, D_C = 384, 256, 384
TA, TB, TC = D_A // P, D_B // P, D_C // P
HD = 64
HEADS_C = D_C // HD
CONV_A, CONV_B = 31, 3
HEADS, TOPK, NKEYS = 8, 16, 128
UNITS = NT * HEADS
RING = 8
GROUPS, GC, ST = 64, 16, 64
CH = 8
NCH = SEQ // CH
GT = P // GC
FF = 2816
FT = FF // P
LAM_INIT = 0.8 - 0.6 * math.exp(-0.3)
NEG = -1e30
LOWEST = -3.0e38
BUCKETS, MAX_DIST = 32, 128
SKEW = 3 * P

COLS = {}
_at = 0
for _name, _n in [("g_mix", KT), ("conv_a_w", CONV_A * TA), ("conv_a_b", TA), ("ln_a_g", TA), ("ln_a_b", TA),
                  ("conv_b_w", CONV_B * TB), ("g_ffn", KT), ("g_ple", KT), ("g_final", KT), ("ssm_norm", KT),
                  ("ssm_d", KT), ("kv_norm", KT), ("k_norm", 1), ("attn_norm", KT), ("q_norm", 1), ("subln", 1),
                  ("ffn_norm0", KT), ("ffn_norm1", KT), ("ffn_w0", 3 * 2 * FT), ("ffn_w1", 3 * 2 * FT),
                  ("ffn_b0", 2 * FT), ("ffn_b1", 2 * FT), ("ple_norm0", KT), ("ple_norm1", KT), ("far", HEADS)]:
    COLS[_name] = _at
    _at += _n
NCOLS = _at

WSLOT = 11 * P
NSLOT = NBANK = 4
NSPLIT = 2


LAYERS = [("w_in", 18, 8, 18), ("w_out", 8, 8, 8), ("w_q", 16, 8, 16), ("ple_a", 8, 10, 16), ("ssm_in", 8, 8, 8),
          ("glu", 16, 8, 16), ("up0", 44, 8, 44), ("down0", 16, 11, 8), ("ple0", 8, 10, 16), ("w_k", 8, 8, 8), ("w_v", 8, 8, 8),
          ("attn_q", 8, 8, 8), ("attn_o", 8, 8, 8), ("up1", 44, 8, 44), ("down1", 16, 11, 8), ("ple1", 8, 10, 16)]
STAGES = ["setup", "mixer", "w_out", "w_q", "peer", "ple_a", "final_a", "ssm_in", "ssm", "glu",
          "up0", "down0", "ple0", "kv", "attn", "attn_o", "up1", "down1", "ple1"]
LAYER_STAGE = {"w_in": "mixer", "w_k": "kv", "w_v": "kv", "attn_q": "kv"}


def build(nc, A, first=0, last=99):
    stages = [s for i, s in enumerate(STAGES) if i == 0 or first <= i <= last]
    SLAB0, TILE0, SLABS, KTILES, TILES = {}, {}, {}, {}, {}
    FIRST = 2 if "mixer" in stages else NSLOT
    s = t = FIRST
    for name, n, k, m in LAYERS:
        if LAYER_STAGE.get(name, name) in stages:
            SLAB0[name], TILE0[name], SLABS[name], KTILES[name], TILES[name] = s, t, n, k, m
            s += n
            t += m

    def used(s):
        return s - FIRST + 1

    def full(s):
        return s // NSLOT + (1 if s % NSLOT >= FIRST % NSLOT and FIRST < NSLOT else 0)

    NORM = {}
    for name in ("mixer", "w_q", "ple_a", "final_a", "ssm_in", "up0", "ple0", "kv", "up1", "ple1"):
        if name in stages:
            NORM[name] = len(NORM)
    PLES = [name for name in ("ple_a", "ple0", "ple1") if name in stages]
    ctx = ExitStack()
    with ctx:
        def sb(name, shape, dt=F32):
            return ctx.enter_context(nc.sbuf_tensor(name, shape, dt))

        def sem(name):
            return ctx.enter_context(nc.semaphore(name))

        hT = sb("hT", [P, KT, SEQ])
        aT = sb("aT", [P, KT, SEQ])
        wring = sb("wring", [P, NSLOT, WSLOT])
        cols = sb("cols", [P, NCOLS])
        rstd = sb("rstd", [P, 2, SEQ])
        sq = sb("sq", [P, 2, SEQ])
        consts = sb("consts", [P, 5 * P + 1])
        xt = sb("xt", [P, 2, SEQ])
        ident = consts[:, 0:P]
        onesD = consts[:, P:2 * P]
        blk64 = consts[:, 2 * P:3 * P]
        swap = consts[:, 3 * P:4 * P]
        ones128 = consts[:, 4 * P:5 * P]
        sgn = consts[:, 5 * P:5 * P + 1]
        eps = sb("eps", [P, 1])
        ones_row = sb("ones_row", [1, P])
        idx = sb("idx", [P, 2, TOPK], U32)
        Z = sb("Z", [P, FT * SEQ])
        R = sb("R", [P, 22528])
        banks = [ctx.enter_context(nc.psum_tensor(f"bank{i}", [P, SEQ], F32)) for i in range(8)]

        def view(arena, at, *shape):
            n = int(np.prod(shape))
            v = arena[:, at:at + n]
            if len(shape) == 2:
                v = v.rearrange("p (a b) -> p a b", b=shape[1])
            elif len(shape) == 3:
                v = v.rearrange("p (a b c) -> p a b c", b=shape[1], c=shape[2])
            elif len(shape) == 4:
                v = v.rearrange("p (a b c d) -> p a b c d", b=shape[1], c=shape[2], d=shape[3])
            return v

        def parts_of(arena, at, tiles, width):
            v = arena[:, at:at + tiles * width].bitcast(F16)
            return v.rearrange("p (k h n) -> p k h n", h=2, n=width)

        def low(ap):
            return ap.bitcast(BF16)

        xs = parts_of(R, 14848, KT, SEQ)
        wsp = parts_of(R, 18944, NSPLIT, WSLOT)

        def col(name, i=0, n=1):
            return cols[:, COLS[name] + i:COLS[name] + i + n]

        def row(ap):
            return ap.rearrange("p a b -> p (a b)")

        biasD = nc.dram_tensor("biasD", [P, HEADS * SKEW], F32, kind="Internal")
        uD = nc.dram_tensor("uD", [KT, P, SEQ], F32, kind="Internal")
        yD = nc.dram_tensor("yD", [KT, P, SEQ], F32, kind="Internal")

        stage_done = sem("stage_done")
        loaded = sem("loaded")
        w_full = [sem(f"w_full{i}") for i in range(NSLOT)]
        w_used = sem("w_used")
        mm_done = sem("mm_done")
        evac_done = sem("evac_done")
        sq_ready, sq_used, stat_ready = sem("sq_ready"), sem("sq_used"), sem("stat_ready")
        rs_ready, a_ready = sem("rs_ready"), sem("a_ready")
        setup_ready = sem("setup_ready")
        out_stored = sem("out_stored")

        zt = view(Z, 0, 18, SEQ)
        ypad = view(R, 0, TA, SEQ + CONV_A - 1)
        ca = view(R, 1632, TA, SEQ)
        mpad = view(R, 3168, TB, SEQ + CONV_B - 1)
        cb = view(R, 4208, TB, SEQ)
        y = view(R, 5232, KT, SEQ)
        vtok = view(R, 9328, NT, D_C)
        vtmp = view(R, 10864, NT, D_C)
        wsT = view(R, 12400, HEADS_C, P)
        vrows = view(R, 13168, 2, D_C)
        bs_row = R[0:1, 13936:13936 + HEADS_C * P]
        vstat = view(R, 14704, 2, NT * HEADS_C)
        vld, in_mm, in_ev = sem("vld"), sem("in_mm"), sem("in_ev")
        y_val, conv_ready = sem("y_val"), sem("conv_ready")
        m_ready, gm_mm, gm_used, g_c, g_sq, g_rs, g_out = [sem(n) for n in
            ("m_ready", "gm_mm", "gm_used", "g_c", "g_sq", "g_rs", "g_out")]
        v_mm, v_ev, v_act, v_norm, mix_mm, mix_used = [sem(n) for n in
            ("v_mm", "v_ev", "v_act", "v_norm", "mix_mm", "mix_used")]

        qT = view(Z, 0, 2 * HEADS, SEQ)
        keysT = view(Z, 2 * HEADS * SEQ, 2 * HEADS, P)
        iota16 = Z[:, 10240:10256]
        diag = view(Z, 10256, 4, P)
        uring = view(R, 0, RING, D)
        vring = view(R, RING * D, RING, D)
        ntok = view(R, 2 * RING * D, NT, D)
        acc = aT[:, :, :].rearrange("p k t -> p (k t)").rearrange("p (a b) -> p a b", b=D)
        s0 = 2 * RING * D + NT * D
        qcur = view(R, s0, 2, 2, P)
        rep = view(R, s0 + 512, 2, P)
        tv = view(R, s0 + 768, 2, TOPK)
        tif = view(R, s0 + 800, 2, TOPK)
        cv = R[:, s0 + 832:s0 + 848]
        e12 = view(R, s0 + 848, 2, TOPK)
        nmax = view(R, s0 + 880, 2, 1)
        act = view(R, s0 + 882, 2, TOPK)
        gel = view(R, s0 + 914, 2, TOPK)
        gex = view(R, s0 + 946, 2, TOPK)
        gsum = view(R, s0 + 978, 2, 1)
        grec = view(R, s0 + 980, 2, 1)
        actg = view(R, s0 + 982, 2, TOPK)
        cand = view(Z, 10768, TOPK, TOPK)
        cand2 = view(R, s0 + 1014, TOPK, TOPK)
        eqa = view(R, s0 + 1270, TOPK, TOPK)
        eqb = view(R, s0 + 1526, TOPK, TOPK)
        ti = sb("ti", [P, 2, TOPK], U32)
        ci = sb("ci", [P, TOPK], U32)
        cab = sb("cab", [P, 2, TOPK], U32)
        keys_loaded = sem("keys_loaded")
        u_full = [sem(f"u_full{i}") for i in range(RING)]
        v_full = [sem(f"v_full{i}") for i in range(RING)]
        u_used, v_used = sem("u_used"), sem("v_used")
        q_cur, sc_mm, sc_used, top_done, ex_done, dots_done, gelu_done, actg_done, diag_done, out_used, idx_ready = [
            sem(n) for n in ("q_cur", "sc_mm", "sc_used", "top_done", "ex_done", "dots_done", "gelu_done",
                             "actg_done", "diag_done", "out_used", "idx_ready")]
        nt_mm, nt_ev, back_mm, back_used = sem("nt_mm"), sem("nt_ev"), sem("back_mm"), sem("back_used")

        pT = view(R, 0, 2, SEQ)
        sg = view(R, 1024, 2, SEQ)
        pe_in = view(R, 2048, 2, SEQ)
        ps = parts_of(R, 3072, 2, SEQ)
        p_loaded, sg_ready, p_split = sem("p_loaded"), sem("sg_ready"), sem("p_split")
        split_done, x_split = sem("split_done"), sem("x_split")
        SPLITS = [name for name in ("w_out", "glu", "attn_o") if name in stages]
        beat, beats = sb("beat", [P, 3]), sem("beats")

        uperm = view(Z, 0, KT, SEQ)
        uall = view(Z, KT * SEQ, KT, SEQ)
        spar = view(Z, 8192, 3, GROUPS)
        kpow = Z[:, 8384:8384 + 2 * CH]
        jnum = Z[:, 8400:8400 + NCH]
        small = view(Z, 8464, 11, GROUPS)
        cosT = view(Z, 9216, 2, SEQ)
        ysb = view(Z, 10240, 2, SEQ)
        sbc = view(R, 0, 4, GROUPS, GC)
        bb, bbp, Cm, D2 = [sbc[:, i, :, :] for i in range(4)]
        AR, AI, AIs = [view(R, 4096 + 1024 * i, GROUPS, 2 * CH) for i in range(3)]
        gmat = view(R, 7168, 2, GT * CH * GC).rearrange("p b (g i c) -> p b g i c", i=CH, c=GC)
        shifts = R[:, 10240:10240 + (2 * CH - 1) * GC]
        hmat = R[:, 10496:10496 + P]
        emat = view(R, 11008, 2, GT * CH * GC).rearrange("p b (g i c) -> p b g i c", i=CH, c=GC)
        gtmp = view(R, 13056, GT, CH, GC)
        bT = view(R, 14080, GT, P)
        Tg = view(R, 15104, 2, GT, P)
        sinT = view(R, 17152, 2, SEQ)
        ph = R[:, 18176:18688]
        nn = R[:, 18688:19200]
        vs = R[:, 19200:19712]
        t1 = R[:, 19712:20224]
        yv = R[:, 20224:20736]
        xpad = view(R, 20736, GT, NCH + 1)
        decay = view(R, 21256, GT, NCH)
        t2 = R[:, 21768:22280]
        bigP, bigN, bigM = [view(R, 7168 + 1024 * i, GROUPS, 2 * CH) for i in range(3)]
        halfpi, nsgn = sb("halfpi", [P, 1]), sb("nsgn", [P, 1])
        [ssm_loaded, u_stored, u_back, powers_ready, g_ready, e_ready, h_mm, h_ev, bt_mm, t_mm, bt_ev, te_ev, s_v_mm, vs_ready, vp_mm,
         yv_ready, yp_mm, x_ready, y_mm, yo_ev, y_stored, y_back, y_total, ph_ready, tab_ready, prep] = [
            sem(n) for n in ("ssm_loaded", "u_stored", "u_back", "powers_ready", "g_ready", "e_ready", "h_mm", "h_ev", "bt_mm", "t_mm",
                             "bt_ev", "te_ev", "s_v_mm", "vs_ready", "vp_mm", "yv_ready", "yp_mm", "x_ready",
                             "y_mm", "yo_ev", "y_stored", "y_back", "y_total", "ph_ready", "tab_ready", "prep")]

        ffz = parts_of(Z, 0, FT, SEQ)
        conv = view(R, 0, 2, 2, SEQ)
        c_ready, g_conv, g_act, prod_done = [sem(n) for n in ("c_ready", "g_conv", "g_act", "prod_done")]

        KQ = view(Z, 0, 2 * HEADS, SEQ)
        vt = view(R, 0, NT, D)
        a2s = parts_of(R, 4096, KT, SEQ)
        vf = view(R, 8192, KT, SEQ)
        gs, gi = rstd, xt
        relb = R[0:BUCKETS + 1, 12288:12288 + HEADS * P]
        onehot = R[0:BUCKETS + 1, 13312:13312 + SKEW]
        lamv = view(R, 13696, 4, HD)
        lams = view(R, 13952, 8, 1)
        bias_sb = view(Z, 8192, HEADS, SKEW)
        near_bias = view(R, 20480, HEADS, 2 * P)
        nlam, sub1, lamt = sb("nlam", [P, 1]), sb("sub1", [P, 1]), sb("lamt", [P, 2, HD])
        qh = R[:, 4096:4608]
        kh = R[:, 10752:11264]
        vh = view(R, 4608, NT, P)
        ss = view(R, 5120, 2, SEQ)
        ee = view(R, 6144, 2, 2, SEQ)
        att = view(R, 8192, 2, SEQ)
        attT = view(R, 9216, 2, NT, P)
        nm = view(R, 10240, 2, 1)
        sm = view(R, 10242, 2, 2)
        rr = view(R, 10246, 2, 1)
        [kv_loaded, a2_ready, v2_mm, v2_ev, gq_ready, gq_mm, gq_sqrt, gq_out, lam_ready, lam_exp, b_mm, b_ev, b_stored,
         b_back, at_sc, rel_ready, sc_free, mx_ready, exp_done, cb_done, tr_mm, tr_ev, pv_mm, o_ev, qh_ready, vh_ready] = [
            sem(n) for n in ("kv_loaded", "a2_ready", "v2_mm", "v2_ev", "gq_ready", "gq_mm", "gq_sqrt", "gq_out",
                             "lam_ready", "lam_exp", "b_mm", "b_ev", "b_stored", "b_back", "at_sc", "rel_ready", "sc_free",
                             "mx_ready", "exp_done", "cb_done", "tr_mm", "tr_ev", "pv_mm", "o_ev", "qh_ready",
                             "vh_ready")]
        GATED = [name for name in ("ple_a", "glu", "ple0", "ple1") if name in stages]
        FFNS = [name for name in ("up0", "up1") if name in stages]

        TURN = 1.0 / (2.0 * math.pi)
        ROUND = 1.5 * 2.0 ** 23
        PI_HI, PI_LO = 6.28125, 2.0 * math.pi - 6.28125
        PI_MAX = 3.1415925

        block = ctx.enter_context(nc.Block())

        def stage(name):
            return name in stages

        def after(name):
            return 4 * len([s for s in stages if STAGES.index(s) <= STAGES.index(name)])

        def barrier(eng, name):
            eng.drain().then_inc(stage_done, 1)
            eng.wait_ge(stage_done, after(name))

        @block.sync
        def _(sp):
            def stream(name):
                s0, n = SLAB0[name], SLABS[name]
                k = KTILES[name] * P
                W = A[name]
                straight = n if s0 % NSLOT or n % NSLOT else NSLOT if s0 - NSLOT < FIRST else 0
                for i in range(straight):
                    s = s0 + i
                    if s - NSLOT >= FIRST:
                        sp.wait_ge(split_done, used(s - NSLOT))
                    sp.dma_start(wring[:, s % NSLOT, 0:k], W[i]).then_inc(w_full[s % NSLOT], 16)
                if straight == n:
                    return
                with sp.Fori(0, (n - straight) // NSLOT) as r:
                    for u in range(NSLOT):
                        sp.wait_ge(split_done, r * NSLOT + used(s0 + straight + u - NSLOT))
                        sp.dma_start(wring[:, u, 0:k], W[r * NSLOT + (straight + u)]).then_inc(w_full[u], 16)

            sp.dma_start(hT[:, :, :], A["xT"]).then_inc(loaded, 16)
            sp.dma_start(cols[:, :], A["cols"]).then_inc(loaded, 16)
            sp.dma_start(consts[:, :], A["consts"]).then_inc(loaded, 16)
            if stage("mixer"):
                stream("w_in")
                sp.dma_start(wsT, A["wsT"]).then_inc(vld, 16)
                sp.dma_start(vrows, A["vrows"]).then_inc(vld, 16)
                sp.dma_start(bs_row, A["b_s"]).then_inc(vld, 16)
            if stage("w_out"):
                stream("w_out")
            if stage("w_q"):
                sp.wait_ge(stage_done, after("mixer"))
                sp.dma_start(keysT, A["keysT"]).then_inc(keys_loaded, 16)
                sp.dma_start(iota16, A["iota16"]).then_inc(keys_loaded, 16)
                stream("w_q")
            def flat(t, n):
                return t.ap()[n].rearrange("a b -> (a b)")

            for name in stages:
                before = stages[stages.index(name) - 1]
                if name in ("glu", "up0", "down0", "attn_o", "up1", "down1"):
                    stream(name)
                if name in PLES:
                    sp.wait_ge(stage_done, after(before))
                    sp.dma_start(pT, A["p_" + name]).then_inc(p_loaded, 16)
                    stream(name)
                if name == "ssm_in":
                    sp.wait_ge(stage_done, after(before))
                    sp.dma_start(sbc, A["ssm_bc"]).then_inc(ssm_loaded, 16)
                    sp.dma_start(spar, A["ssm_par"]).then_inc(ssm_loaded, 16)
                    sp.dma_start(kpow, A["ssm_k"]).then_inc(ssm_loaded, 16)
                    sp.dma_start(jnum, A["ssm_j"]).then_inc(ssm_loaded, 16)
                    stream(name)
                    for n in range(KT):
                        sp.wait_ge(evac_done, used(TILE0[name] + n))
                        sp.dma_start(flat(uD, n).rearrange("(s p j) -> p s j", p=P, j=NCH),
                                     uperm[:, n, :].rearrange("p (s j) -> p s j", j=NCH)).then_inc(u_stored, 16)
                    for n in range(KT):
                        sp.wait_ge(u_stored, 16 * KT)
                        sp.dma_start(uall[:, n, :], uD.ap()[n]).then_inc(u_back, 16)
                if name == "ssm":
                    for n in range(KT):
                        sp.wait_ge(yo_ev, n + 1)
                        sp.dma_start(yD.ap()[n], ysb[:, n % 2, :]).then_inc(y_stored, 16)
                        sp.wait_ge(y_stored, 16 * (n + 1))
                        sp.dma_start(uall[:, n, :].rearrange("p (s j) -> p s j", j=NCH),
                                     flat(yD, n).rearrange("(s p j) -> p s j", p=P, j=NCH)).then_inc(y_back, 16)
                if name == "kv":
                    stream("w_k")
                    sp.wait_ge(stage_done, after(before))
                    sp.dma_start(relb[0:BUCKETS, :].rearrange("b (h p) -> b h p", p=P), A["relb"])\
                      .then_inc(kv_loaded, 16)
                    sp.dma_start(onehot, A["onehot"]).then_inc(kv_loaded, 16)
                    sp.dma_start(lamv, A["lam"]).then_inc(kv_loaded, 16)
                    stream("w_v")
                    stream("attn_q")
                    sp.wait_ge(b_ev, HEADS)
                    sp.dma_start(biasD.ap().rearrange("p (h m) -> p h m", m=SKEW), bias_sb).then_inc(b_stored, 16)
                    sp.wait_ge(b_stored, 16)
                    sp.dma_start(near_bias, bass.AP(biasD, P - 1, [[HEADS * SKEW - 1, P], [SKEW, HEADS], [1, 2 * P]]))\
                      .then_inc(b_back, 16)
            sp.wait_ge(stage_done, 4 * len(stages))
            sp.dma_start(A["outT"], hT[:, :, :]).then_inc(out_stored, 16)
            sp.wait_ge(out_stored, 16)
        @block.tensor
        def _(pe):
            def norm_stats(i):
                for k in range(KT):
                    pe.wait_ge(sq_ready, KT * i + k + 1)
                    pe.matmul(banks[5][:, :], onesD, sq[:, k % 2, :], start=(k == 0),
                              stop=(k == KT - 1)).then_inc(sq_used, 1)

            def free_bank(t, r, step):
                if step or t - NBANK >= FIRST:
                    pe.wait_ge(evac_done, r * step + used(t - NBANK))

            PARTS = ((0, 0), (0, 1), (1, 0))

            def product(bank, slot, k0, n, x, ready=None, base=0, start=True, stop=True, first_of_slab=True):
                for k in range(n):
                    if ready is not None:
                        pe.wait_ge(ready, base + k + 1)
                    for p, (i, j) in enumerate(PARTS):
                        w, v = wsp[:, slot, i, (k0 + k) * P:(k0 + k + 1) * P], x[:, k, j, :]
                        mm = pe.matmul(bank[:, :], low(w) if i else w, low(v) if j else v,
                                       start=(start and k == 0 and p == 0), stop=(stop and k == n - 1 and p == 2))
                        if k == 0 and p == 0 and first_of_slab:
                            mm.then_inc(w_used, 1)
                return mm

            def plain(name, x, ready=None, base=0):
                n, s0, t0, kt = SLABS[name], SLAB0[name], TILE0[name], KTILES[name]
                if s0 % NSLOT or n % NSLOT:
                    for i in range(n):
                        s, t = s0 + i, t0 + i
                        pe.wait_ge(split_done, used(s))
                        free_bank(t, 0, 0)
                        product(banks[t % NBANK], s % NSPLIT, 0, kt, x, ready if i == 0 else None, base)\
                            .then_inc(mm_done, 1)
                    return
                with pe.Fori(0, n // NSLOT) as r:
                    for u in range(NSLOT):
                        pe.wait_ge(split_done, r * NSLOT + used(s0 + u))
                        free_bank(t0 + u, r, NSLOT)
                        product(banks[u], u % NSPLIT, 0, kt, x, ready if u == 0 else None, base).then_inc(mm_done, 1)

            def paired(name, x, ready, base):
                n, s0, t0 = SLABS[name], SLAB0[name], TILE0[name]
                with pe.Fori(0, n // NSLOT) as r:
                    for u in range(NSLOT):
                        pe.wait_ge(split_done, r * NSLOT + used(s0 + u))
                        free_bank(t0 + 2 * u, r, 2 * NSLOT)
                        product(banks[2 * u % NBANK], u % NSPLIT, 0, KT, x, ready if u == 0 else None, base)\
                            .then_inc(mm_done, 1)
                        free_bank(t0 + 2 * u + 1, r, 2 * NSLOT)
                        product(banks[(2 * u + 1) % NBANK], u % NSPLIT, KT, 2, ps, first_of_slab=False)\
                            .then_inc(mm_done, 1)

            def halves(name, x):
                n, s0, t0, kt = SLABS[name], SLAB0[name], TILE0[name], KTILES[name]
                with pe.Fori(0, n // (2 * NSLOT)) as r:
                    for u in range(NBANK):
                        free_bank(t0 + u, r, NBANK)
                        for half in range(2):
                            v = 2 * u + half
                            pe.wait_ge(split_done, r * (2 * NSLOT) + used(s0 + v))
                            mm = product(banks[u], v % NSPLIT, 0, kt, x[:, half * kt:(half + 1) * kt, :, :],
                                         start=(half == 0), stop=(half == 1))
                        mm.then_inc(mm_done, 1)

            pe.wait_ge(loaded, 48)
            barrier(pe, "setup")
            if stage("mixer"):
                norm_stats(NORM["mixer"])
                plain("w_in", xs, a_ready, KT * NORM["mixer"])
                pe.wait_ge(evac_done, used(TILE0["w_in"] + 17))
                for T in range(NT):
                    if T >= 2:
                        pe.wait_ge(v_ev, T - 1)
                    for k in range(TC):
                        mm = pe.transpose(banks[6 + T % 2][:, k * P:(k + 1) * P], zt[:, 15 + k, T * P:(T + 1) * P],
                                          ident)
                    mm.then_inc(v_mm, 1)
                pe.wait_ge(conv_ready, 1)
                for i in range(TA):
                    if i:
                        pe.wait_ge(g_c, i)
                    pe.matmul(banks[4][:, :], blk64, ca[:, i, :], start=True, stop=True).then_inc(gm_mm, 1)
                    pe.wait_ge(g_sq, i + 1)
                    pe.matmul(banks[5][:, :], blk64, sq[:, i % 2, :], start=True, stop=True).then_inc(gm_mm, 1)
                pe.wait_ge(vld, 48)
                pe.wait_ge(v_norm, 1)
                for pr in range(TC):
                    if pr == 2:
                        pe.wait_ge(mix_used, 1)
                    for T in range(NT):
                        for hh in range(2):
                            h = 2 * pr + hh
                            out = banks[6 + pr % 2][hh * HD:(hh + 1) * HD, T * P:(T + 1) * P]
                            pe.matmul(out, vtok[:, T, h * HD:(h + 1) * HD], wsT[:, h, :], start=True, stop=False)
                            mm = pe.matmul(out, ones_row[0:1, 0:HD], bs_row[0:1, h * P:(h + 1) * P],
                                           start=False, stop=True, tile_position=(0, hh * HD))
                    mm.then_inc(mix_mm, 1)
                barrier(pe, "mixer")
            if stage("w_out"):
                plain("w_out", xs, x_split, KT * SPLITS.index("w_out"))
                barrier(pe, "w_out")
            if stage("w_q"):
                norm_stats(NORM["w_q"])
                plain("w_q", xs, a_ready, KT * NORM["w_q"])
                for T in range(NT):
                    if T >= 1:
                        pe.wait_ge(nt_ev, 2 * T)
                    for k in range(KT):
                        mm = pe.transpose(banks[6 + k // 4][:, (k % 4) * P:(k % 4 + 1) * P],
                                          aT[:, k, T * P:(T + 1) * P], ident)
                        if k % 4 == 3:
                            mm.then_inc(nt_mm, 1)
                barrier(pe, "w_q")
            if stage("peer"):
                def scores(n, par, h):
                    pe.wait_ge(q_cur, n + 1)
                    if not (isinstance(n, int) and n == 0):
                        pe.wait_ge(sc_used, n)
                    for half in range(2):
                        mm = pe.matmul(banks[4][:, half * P:(half + 1) * P], qcur[:, par, half, :],
                                       keysT[:, h * 2 + half, :], start=True, stop=True)
                    mm.then_inc(sc_mm, 1)

                def combine(n, par):
                    if not (isinstance(n, int) and n < 2):
                        pe.wait_ge(out_used, n - 1)
                    for k in range(TOPK):
                        slot = k % RING
                        pe.wait_ge(diag_done, n * TOPK + k + 1)
                        pe.wait_ge(v_full[slot], n * 32 + 16 * (k // RING + 1))
                        for c in range(2):
                            mm = pe.matmul(banks[2 * par + c][:, :], diag[:, k % 4, :],
                                           vring[:, slot, c * SEQ:(c + 1) * SEQ], start=(k == 0),
                                           stop=(k == TOPK - 1))
                        mm.then_inc(v_used, 1)

                pe.wait_ge(keys_loaded, 32)
                scores(0, 0, 0)
                scores(1, 1, 1)
                for n in range(2):
                    combine(n, n)
                    scores(n + 2, n, n + 2)
                with pe.Fori(0, UNITS // 2 - 2) as i:
                    for par in range(2):
                        n = i * 2 + (par + 2)
                        combine(n, par)
                        scores(n + 2, par, (n + 2) % HEADS)
                combine(UNITS - 2, 0)
                combine(UNITS - 1, 1)
                pe.wait_ge(out_used, UNITS)
                for k in range(KT):
                    if k >= 2:
                        pe.wait_ge(back_used, k - 1)
                    for T in range(NT):
                        mm = pe.transpose(banks[6 + k % 2][:, T * P:(T + 1) * P], acc[:, T, k * P:(k + 1) * P], ident)
                    mm.then_inc(back_mm, 1)
                barrier(pe, "peer")
            def ple(name):
                norm_stats(NORM[name])
                pe.wait_ge(p_split, PLES.index(name) + 1)
                paired(name, xs, a_ready, KT * NORM[name])
                barrier(pe, name)

            def feed_forward(i):
                if stage(f"up{i}"):
                    norm_stats(NORM[f"up{i}"])
                    plain(f"up{i}", xs, a_ready, KT * NORM[f"up{i}"])
                    barrier(pe, f"up{i}")
                if stage(f"down{i}"):
                    halves(f"down{i}", ffz)
                    barrier(pe, f"down{i}")

            def group_stat(m, mean):
                pe.wait_ge(gq_ready, m + 1)
                if m >= 2:
                    pe.wait_ge(gq_sqrt, m - 1)
                pe.matmul(banks[4 + m % 2][:, :], mean, sq[:, m % 2, :], start=True, stop=True).then_inc(gq_mm, 1)

            if stage("ple_a"):
                ple("ple_a")
            if stage("final_a"):
                norm_stats(NORM["final_a"])
                barrier(pe, "final_a")
            if stage("ssm_in"):
                norm_stats(NORM["ssm_in"])
                plain("ssm_in", xs, a_ready, KT * NORM["ssm_in"])
                barrier(pe, "ssm_in")
            if stage("ssm"):
                def input_matrices(n, par):
                    zero = isinstance(n, int) and n == 0
                    pe.wait_ge(g_ready, n + 1)
                    for half in range(2):
                        if not zero:
                            pe.wait_ge(bt_ev, n * 2 - (1 - half))
                        for g in range(4):
                            mm = pe.transpose(banks[half][:, g * P:(g + 1) * P], row(gmat[:, par, half * 4 + g, :, :]),
                                              ident)
                        mm.then_inc(bt_mm, 1)
                    if not zero:
                        pe.wait_ge(h_ev, n)
                    for g in range(GT):
                        mm = pe.matmul(banks[2][:, g * GC:(g + 1) * GC], row(gmat[:, par, g, :, :]),
                                       Cm[:, n * GT + g, :], start=True, stop=True)
                    mm.then_inc(h_mm, 1)

                def output_matrices(n):
                    pe.wait_ge(h_ev, n + 1)
                    for half in range(2):
                        if not (isinstance(n, int) and n == 0):
                            pe.wait_ge(te_ev, n * 2 - (1 - half))
                        for j in range(4):
                            at = (CH - 1 - half * 4 - j) * GC
                            mm = pe.matmul(banks[3 + 3 * half][:, j * P:(j + 1) * P], shifts[:, at:at + P], hmat,
                                           start=True, stop=True)
                        mm.then_inc(t_mm, 1)

                def recur(n, par, last=False):
                    zero = isinstance(n, int) and n == 0
                    pe.wait_ge(bt_ev, n * 2 + 2)
                    if not zero:
                        pe.wait_ge(vs_ready, n)
                    for g in range(GT):
                        mm = pe.matmul(banks[4][:, g * NCH:(g + 1) * NCH], bT[:, g, :],
                                       uall[:, n, g * NCH:(g + 1) * NCH], start=True, stop=True)
                    mm.then_inc(s_v_mm, 1)
                    pe.wait_ge(vs_ready, n + 1)
                    if not zero:
                        pe.wait_ge(x_ready, n)
                    pe.matmul(banks[5][:, :], swap, vs, start=True, stop=True).then_inc(vp_mm, 1)
                    if not last:
                        input_matrices(n + 1, 1 - par)
                    pe.wait_ge(yv_ready, n + 1)
                    pe.matmul(banks[5][:, :], swap, yv, start=True, stop=True).then_inc(yp_mm, 1)
                    if not last:
                        output_matrices(n + 1)
                    pe.wait_ge(te_ev, n * 2 + 2)
                    pe.wait_ge(e_ready, n + 1)
                    pe.wait_ge(x_ready, n + 1)
                    if not zero:
                        pe.wait_ge(yo_ev, n)
                    for g in range(GT):
                        out = banks[7][:, g * NCH:(g + 1) * NCH]
                        pe.matmul(out, Tg[:, par, g, :], uall[:, n, g * NCH:(g + 1) * NCH], start=True, stop=False)
                        mm = pe.matmul(out, row(emat[:, par, g, :, :]),
                                       xpad[:, g, 0:NCH], start=False, stop=True)
                    mm.then_inc(y_mm, 1)

                input_matrices(0, 0)
                output_matrices(0)
                pe.wait_ge(u_back, 16 * KT)
                recur(0, 0)
                recur(1, 1)
                with pe.Fori(0, KT // 2 - 2) as i:
                    for par in range(2):
                        recur(i * 2 + (par + 2), par)
                recur(KT - 2, 0)
                recur(KT - 1, 1, True)
                barrier(pe, "ssm")
            if stage("glu"):
                plain("glu", xs, x_split, KT * SPLITS.index("glu"))
                barrier(pe, "glu")
            feed_forward(0)
            if stage("ple0"):
                ple("ple0")
            if stage("kv"):
                norm_stats(NORM["kv"])
                plain("w_k", xs, a_ready, KT * NORM["kv"])
                plain("w_v", xs)
                plain("attn_q", a2s, a2_ready, 0)
                for T in range(NT):
                    for c in range(2):
                        b = 2 * T + c
                        if b >= 2:
                            pe.wait_ge(v2_ev, b - 1)
                        for k in range(4):
                            mm = pe.transpose(banks[6 + c][:, k * P:(k + 1) * P], vf[:, 4 * c + k, T * P:(T + 1) * P],
                                              ident)
                        mm.then_inc(v2_mm, 1)
                        group_stat(2 * b, blk64)
                        group_stat(2 * b + 1, blk64)
                pe.wait_ge(kv_loaded, 48)
                pe.wait_ge(rel_ready, 1)
                for h in range(HEADS):
                    if h >= 2:
                        pe.wait_ge(b_ev, h - 1)
                    pe.matmul(banks[h % 2][:, 0:SKEW], relb[:, h * P:(h + 1) * P], onehot,
                              start=True, stop=True).then_inc(b_mm, 1)
                barrier(pe, "kv")
            if stage("attn"):
                def head(h, first=False):
                    def scores2(qt):
                        w = (qt + 1) * P
                        for c in range(2):
                            pe.wait_ge(sc_free, h * 8 + (2 * qt + c + 1))
                            rows = slice(c * HD, (c + 1) * HD)
                            pe.matmul(banks[2 * (qt % 2) + c][:, 0:w], qh[rows, qt * P:(qt + 1) * P],
                                      kh[rows, 0:w], start=True, stop=True).then_inc(at_sc, 1)

                    pe.wait_ge(qh_ready, h + 1)
                    scores2(0)
                    scores2(1)
                    for qt in range(NT):
                        pe.wait_ge(cb_done, h * 4 + (qt + 1))
                        if qt or not first:
                            pe.wait_ge(tr_ev, h * 4 + qt)
                        for kt in range(qt + 1):
                            mm = pe.transpose(banks[4 + qt % 2][:, kt * P:(kt + 1) * P],
                                              att[:, qt % 2, kt * P:(kt + 1) * P], ident)
                        mm.then_inc(tr_mm, 1)
                        if qt + 2 < NT:
                            scores2(qt + 2)
                        if qt == 0:
                            pe.wait_ge(vh_ready, h + 1)
                            if not first:
                                pe.wait_ge(o_ev, h)
                        pe.wait_ge(tr_ev, h * 4 + (qt + 1))
                        for kt in range(qt + 1):
                            mm = pe.matmul(banks[6][:, qt * P:(qt + 1) * P], vh[:, kt, :],
                                           attT[:, qt % 2, kt, :], start=(kt == 0), stop=(kt == qt))
                        mm.then_inc(pv_mm, 1)

                head(0, True)
                with pe.Fori(0, HEADS - 1) as i:
                    head(i + 1)
                for h in range(HEADS):
                    group_stat(2 * HEADS + h, ones128)
                barrier(pe, "attn")
            if stage("attn_o"):
                plain("attn_o", xs, x_split, KT * SPLITS.index("attn_o"))
                barrier(pe, "attn_o")
            feed_forward(1)
            if stage("ple1"):
                ple("ple1")
        @block.scalar
        def _(ac):
            def norm_squares(i):
                for k in range(KT):
                    if KT * i + k >= 2:
                        ac.wait_ge(sq_used, KT * i + k - 1)
                    ac.activation(sq[:, k % 2, :], hT[:, k, :], ACT.Square).then_inc(sq_ready, 1)
                ac.wait_ge(sq_used, KT * (i + 1))
                ac.activation(rstd[:, 1, :], banks[5][:, :], ACT.Sqrt, bias=eps[:, :]).then_inc(rs_ready, 1)

            def copies(name, out):
                t0, n = TILE0[name], TILES[name]
                with ac.Fori(0, n // NBANK) as r:
                    for u in range(NBANK):
                        ac.wait_ge(mm_done, r * NBANK + used(t0 + u))
                        ac.activation(out[:, r * NBANK + u, :], banks[u][:, :], ACT.Copy).then_inc(evac_done, 1)

            ac.wait_ge(loaded, 48)
            barrier(ac, "setup")
            if stage("mixer"):
                norm_squares(NORM["mixer"])
                for i in range(TILES["w_in"]):
                    t = TILE0["w_in"] + i
                    ac.wait_ge(mm_done, used(t))
                    ac.activation(zt[:, i, :], banks[t % NBANK][:, :],
                                  ACT.Sigmoid if TA <= i < 2 * TA else ACT.Copy).then_inc(evac_done, 1)
                for T in range(NT):
                    ac.wait_ge(v_mm, T + 1)
                    ac.activation(vtok[:, T, :], banks[6 + T % 2][:, 0:D_C], ACT.Copy).then_inc(v_ev, 1)
                for i in range(TA):
                    ac.wait_ge(g_c, i + 1)
                    if i == 2:
                        ac.wait_ge(gm_mm, 2)
                    ac.activation(sq[:, i % 2, :], ca[:, i, :], ACT.Square).then_inc(g_sq, 1)
                    ac.wait_ge(gm_mm, 2 * i + 2)
                    if i:
                        ac.wait_ge(g_out, i)
                    ac.activation(rstd[:, 1, :], banks[5][:, :], ACT.Sqrt, bias=eps[:, :]).then_inc(g_rs, 1)
                ac.wait_ge(v_act, 1)
                ac.activation(vstat[:, 1, :], vstat[:, 1, :], ACT.Sqrt, bias=eps[:, :], scale=1.0 / HD)\
                  .then_inc(v_act, 1)
                for i in range(TA):
                    ac.wait_ge(g_out, i + 1)
                    ac.activation(y[:, i, :], ca[:, i, :], ACT.Silu, bias=col("ln_a_b", i), scale=col("ln_a_g", i))
                barrier(ac, "mixer")
            if stage("w_out"):
                barrier(ac, "w_out")
            if stage("w_q"):
                norm_squares(NORM["w_q"])
                copies("w_q", qT)
                for T in range(NT):
                    for c in range(2):
                        ac.wait_ge(nt_mm, 2 * T + c + 1)
                        ac.activation(ntok[:, T, c * SEQ:(c + 1) * SEQ], banks[6 + c][:, :], ACT.Copy)\
                          .then_inc(nt_ev, 1)
                barrier(ac, "w_q")
            if stage("peer"):
                def query(n, par, h, T):
                    if not (isinstance(n, int) and n < 2):
                        ac.wait_ge(sc_mm, n - 1)
                    ac.activation(qcur[:, par, :, :], qT[:, bass.ds(h * 2, 2), bass.ds(T * P, P)], ACT.Copy)\
                      .then_inc(q_cur, 1)

                def exps(n, par):
                    ac.wait_ge(top_done, n + 1)
                    ac.activation(gex[:, par, :], cv, ACT.Exp, bias=nmax[:, par, :],
                                  accum_out=gsum[:, par, :]).then_inc(ex_done, 1)

                def weights(n, par):
                    ac.wait_ge(dots_done, n + 1)
                    ac.activation(gel[:, par, :], act[:, par, :], ACT.Gelu_apprx_tanh).then_inc(gelu_done, 1)

                def diags(n, par):
                    ac.wait_ge(actg_done, n + 1)
                    for k in range(TOPK):
                        if not (isinstance(n, int) and n == 0 and k < 4):
                            ac.wait_ge(v_used, n * TOPK + k - 3)
                        ac.activation(diag[:, k % 4, :], ident, ACT.Copy, scale=actg[:, par, k:k + 1])\
                          .then_inc(diag_done, 1)

                query(0, 0, 0, 0)
                query(1, 1, 1, 0)
                exps(0, 0)

                def step(n, par):
                    weights(n, par)
                    diags(n, par)
                    exps(n + 1, 1 - par)
                    query(n + 2, par, (n + 2) % HEADS, (n + 2) // HEADS)

                step(0, 0)
                step(1, 1)
                with ac.Fori(0, UNITS // 2 - 2) as i:
                    for par in range(2):
                        step(i * 2 + (par + 2), par)
                weights(UNITS - 2, 0)
                diags(UNITS - 2, 0)
                exps(UNITS - 1, 1)
                weights(UNITS - 1, 1)
                diags(UNITS - 1, 1)
                barrier(ac, "peer")
            def sigmoids(name, gate):
                t0 = TILE0[name]
                for n in range(KT):
                    t = t0 + 2 * n + gate
                    ac.wait_ge(mm_done, used(t))
                    if n >= 2:
                        ac.wait_ge(evac_done, used(t0 + 2 * n - 3))
                    ac.activation(sg[:, n % 2, :], banks[t % NBANK][:, :], ACT.Sigmoid)\
                      .then_inc(sg_ready, 1)

            def ple(name):
                norm_squares(NORM[name])
                sigmoids(name, 0)
                barrier(ac, name)

            def feed_forward(i):
                if stage(f"up{i}"):
                    norm_squares(NORM[f"up{i}"])
                    t0, base = TILE0[f"up{i}"], FT * FFNS.index(f"up{i}")
                    w2, b = COLS[f"ffn_w{i}"] + 2, COLS[f"ffn_b{i}"]

                    def pair(u, r=None):
                        for gv in range(2):
                            f = u if r is None else r * 2 + (u + 2)
                            ac.wait_ge(mm_done, f * 2 + used(t0 + gv))
                            if r is not None or base:
                                ac.wait_ge(prod_done, f + base - 1)
                            at = f * 2 + gv
                            ac.activation(conv[:, u, gv, :], banks[(2 * u + gv) % NBANK][:, :], ACT.Identity,
                                          bias=cols[:, bass.ds(at + b, 1)], scale=cols[:, bass.ds(at * 3 + w2, 1)])\
                              .then_inc(c_ready, 1)
                        ac.wait_ge(g_conv, f + (base + 1))
                        ac.activation(conv[:, u, 0, :], conv[:, u, 0, :], ACT.Gelu_apprx_tanh).then_inc(g_act, 1)

                    pair(0)
                    pair(1)
                    with ac.Fori(0, FT // 2 - 1) as r:
                        pair(0, r)
                        pair(1, r)
                    barrier(ac, f"up{i}")
                if stage(f"down{i}"):
                    barrier(ac, f"down{i}")

            def group_square(m, x):
                if m >= 2:
                    ac.wait_ge(gq_mm, m - 1)
                ac.activation(sq[:, m % 2, :], x, ACT.Square).then_inc(gq_ready, 1)

            def group_sqrt(m):
                ac.wait_ge(gq_mm, m + 1)
                if m >= 2:
                    ac.wait_ge(gq_out, m - 1)
                ac.activation(gs[:, m % 2, :], banks[4 + m % 2][:, :], ACT.Sqrt, bias=eps[:, :]).then_inc(gq_sqrt, 1)

            if stage("ple_a"):
                ple("ple_a")
            if stage("final_a"):
                norm_squares(NORM["final_a"])
                barrier(ac, "final_a")
            if stage("ssm_in"):
                norm_squares(NORM["ssm_in"])
                ac.wait_ge(ssm_loaded, 64)
                ac.activation(small[:, 0, :], spar[:, 2, :], ACT.Exp).then_inc(prep, 1)
                for n in range(KT):
                    if n == NBANK:
                        ac.wait_ge(prep, 2)
                        ac.activation(bigM, bigM, ACT.Exp)
                        ac.activation(AI, bigP, ACT.Sin)
                        ac.activation(AR, bigP, ACT.Abs)
                        ac.drain()
                        ac.activation(AR, AR, ACT.Sin, bias=halfpi[:, :], scale=-1.0)
                        ac.drain().then_inc(prep, 1)
                    t = TILE0["ssm_in"] + n
                    ac.wait_ge(mm_done, used(t))
                    ac.activation(uperm[:, n, :].rearrange("p (s j) -> p j s", j=NCH),
                                  banks[t % NBANK][:, :].rearrange("p (j s) -> p j s", s=CH), ACT.Copy)\
                      .then_inc(evac_done, 1)
                barrier(ac, "ssm_in")
            if stage("ssm"):
                def tables(n, par):
                    ac.wait_ge(ph_ready, n + 1)
                    if not (isinstance(n, int) and n < 2):
                        ac.wait_ge(x_ready, n - 1)
                    ac.activation(sinT[:, par, :], ph, ACT.Sin, scale=nsgn[:, :])
                    ac.activation(cosT[:, par, :], ph, ACT.Abs)
                    ac.drain()
                    ac.activation(cosT[:, par, :], cosT[:, par, :], ACT.Sin, bias=halfpi[:, :], scale=-1.0)
                    ac.drain().then_inc(tab_ready, 1)

                def input_matrices(n, par):
                    for half in range(2):
                        ac.wait_ge(bt_mm, n * 2 + (half + 1))
                        ac.activation(row(bT[:, half * 4:half * 4 + 4, :]), banks[half][:, :], ACT.Copy)\
                          .then_inc(bt_ev, 1)
                    ac.wait_ge(h_mm, n + 1)
                    if not (isinstance(n, int) and n == 0):
                        ac.wait_ge(t_mm, n * 2)
                    ac.activation(hmat, banks[2][:, 0:P], ACT.Copy).then_inc(h_ev, 1)

                def output_matrices(n, par):
                    if not (isinstance(n, int) and n < 2):
                        ac.wait_ge(y_mm, n - 1)
                    for half in range(2):
                        ac.wait_ge(t_mm, n * 2 + (half + 1))
                        ac.activation(Tg[:, par, :, half * SEQ // 8:(half + 1) * SEQ // 8]
                                      .rearrange("p g (t c) -> p t g c", c=GC),
                                      banks[3 + 3 * half][:, :].rearrange("p (t g c) -> p t g c", g=GT, c=GC),
                                      ACT.Copy).then_inc(te_ev, 1)

                def recur(n, par, last=False):
                    ac.wait_ge(s_v_mm, n + 1)
                    if not (isinstance(n, int) and n == 0):
                        ac.wait_ge(yv_ready, n)
                    ac.activation(vs, banks[4][:, :], ACT.Copy).then_inc(vs_ready, 1)
                    if not last:
                        input_matrices(n + 1, 1 - par)
                        tables(n + 1, 1 - par)
                        output_matrices(n + 1, 1 - par)
                    ac.wait_ge(y_mm, n + 1)
                    if not (isinstance(n, int) and n < 2):
                        ac.wait_ge(y_stored, n * 16 - 16)
                    ac.activation(ysb[:, par, :], banks[7][:, :], ACT.Copy).then_inc(yo_ev, 1)

                input_matrices(0, 0)
                output_matrices(0, 0)
                tables(0, 0)
                recur(0, 0)
                recur(1, 1)
                with ac.Fori(0, KT // 2 - 2) as i:
                    for par in range(2):
                        recur(i * 2 + (par + 2), par)
                recur(KT - 2, 0)
                recur(KT - 1, 1, True)
                for n in range(KT):
                    ac.wait_ge(y_total, n + 1)
                    ac.activation(aT[:, n, :].rearrange("p (j s) -> p j s", s=CH),
                                  uperm[:, n, :].rearrange("p (s j) -> p j s", j=NCH), ACT.Gelu_apprx_tanh)
                barrier(ac, "ssm")
            if stage("glu"):
                sigmoids("glu", 1)
                barrier(ac, "glu")
            feed_forward(0)
            if stage("ple0"):
                ple("ple0")
            if stage("kv"):
                norm_squares(NORM["kv"])
                copies("w_k", KQ[:, 0:HEADS, :])
                copies("w_v", vf)
                copies("attn_q", KQ[:, HEADS:, :])
                ac.drain()
                for b in range(2 * NT):
                    group_square(2 * b, KQ[:, 2 * b, :])
                    group_square(2 * b + 1, KQ[:, 2 * b + 1, :])
                    ac.wait_ge(v2_mm, b + 1)
                    ac.activation(vt[:, b // 2, (b % 2) * SEQ:(b % 2 + 1) * SEQ], banks[6 + b % 2][:, :], ACT.Copy)\
                      .then_inc(v2_ev, 1)
                    group_sqrt(2 * b)
                    group_sqrt(2 * b + 1)
                ac.wait_ge(lam_ready, 1)
                ac.activation(lams[:, 2:4, :], lams[:, 0:2, :], ACT.Exp).then_inc(lam_exp, 1)
                for h in range(HEADS):
                    ac.wait_ge(b_mm, h + 1)
                    ac.activation(bias_sb[:, h, :], banks[h % 2][:, 0:SKEW], ACT.Copy).then_inc(b_ev, 1)
                barrier(ac, "kv")
            if stage("attn"):
                with ac.Fori(0, HEADS) as h:
                    def exps(qt):
                        w = (qt + 1) * P
                        for c in range(2):
                            ac.wait_ge(mx_ready, h * 8 + (2 * qt + c + 1))
                            ac.activation(ee[:, qt % 2, c, 0:w], ss[:, c, 0:w], ACT.Exp, bias=nm[:, c, :],
                                          accum_out=sm[:, qt % 2, c:c + 1]).then_inc(exp_done, 1)

                    exps(0)
                    exps(1)
                    for qt in range(NT):
                        ac.wait_ge(tr_mm, h * 4 + (qt + 1))
                        ac.activation(row(attT[:, qt % 2, 0:qt + 1, :]), banks[4 + qt % 2][:, 0:(qt + 1) * P], ACT.Copy)\
                          .then_inc(tr_ev, 1)
                        if qt + 2 < NT:
                            exps(qt + 2)
                    ac.wait_ge(pv_mm, h * 4 + 4)
                    ac.activation(aT[:, h, :], banks[6][:, :], ACT.Copy).then_inc(o_ev, 1)
                ac.drain()
                for h in range(HEADS):
                    group_square(2 * HEADS + h, aT[:, h, :])
                    group_sqrt(2 * HEADS + h)
                barrier(ac, "attn")
            if stage("attn_o"):
                barrier(ac, "attn_o")
            feed_forward(1)
            if stage("ple1"):
                ple("ple1")
        @block.vector
        def _(ve):
            def split_tile(dst, src):
                ve.drain()
                ve.tensor_copy(dst[:, 0, :], src)
                ve.drain()
                return ve.tensor_tensor(low(dst[:, 1, :]), src, dst[:, 0, :], ALU.subtract)

            def norm_scale(i):
                ve.wait_ge(rs_ready, i + 1)
                ve.reciprocal(rstd[:, 0, :], rstd[:, 1, :])
                ve.drain()

            def norm_tiles(gains, parts, ready, out=None):
                for k in range(KT):
                    t = xt[:, k % 2, :] if out is None else out[:, k, :]
                    ve.scalar_tensor_tensor(t, hT[:, k, :], col(gains, k), rstd[:, 0, :], ALU.mult, ALU.mult)
                    split_tile(parts[:, k, :, :], t).then_inc(ready, 1)

            def norm_apply(i, gains, out=None):
                norm_scale(i)
                norm_tiles(gains, xs, a_ready, out)

            def split_input(src):
                for k in range(KT):
                    split_tile(xs[:, k, :, :], src[:, k, :]).then_inc(x_split, 1)

            def residual(name):
                t0, n = TILE0[name], TILES[name]
                with ve.Fori(0, n // NBANK) as r:
                    for u in range(NBANK):
                        ve.wait_ge(mm_done, r * NBANK + used(t0 + u))
                        h = hT[:, r * NBANK + u, :]
                        ve.tensor_tensor(h, h, banks[u][:, :], ALU.add).then_inc(evac_done, 1)

            ve.memset(eps[:, :], EPS)
            ve.memset(ones_row[:, :], 1.0)
            ve.wait_ge(loaded, 48)
            barrier(ve, "setup")
            if stage("mixer"):
                norm_apply(NORM["mixer"], "g_mix")
                ve.memset(ypad[:, :, 0:CONV_A - 1], 0.0)
                ve.memset(mpad[:, :, 0:CONV_B - 1], 0.0)
                ve.wait_ge(evac_done, used(TILE0["w_in"] + 2 * TA - 1))
                for i in range(TA):
                    ve.tensor_tensor(ypad[:, i, CONV_A - 1:], zt[:, i, :], zt[:, TA + i, :], ALU.mult)
                ve.drain()
                for i in range(TA):
                    ve.tensor_scalar(ca[:, i, :], ypad[:, i, 0:SEQ], col("conv_a_w", i), col("conv_a_b", i),
                                     ALU.mult, ALU.add)
                ve.drain()
                with ve.Fori(1, CONV_A) as j:
                    for i in range(TA):
                        ve.scalar_tensor_tensor(ca[:, i, :], ypad[:, i, bass.ds(j, SEQ)],
                                                cols[:, bass.ds(j * TA + (COLS["conv_a_w"] + i), 1)], ca[:, i, :],
                                                ALU.mult, ALU.add)
                    ve.drain()
                ve.drain().then_inc(conv_ready, 1)
                ve.wait_ge(evac_done, used(TILE0["w_in"] + 11))
                for i in range(TB):
                    ve.tensor_tensor(mpad[:, i, CONV_B - 1:], zt[:, 8 + i, :], zt[:, 10 + i, :], ALU.mult)
                ve.drain()
                for i in range(TB):
                    ve.tensor_scalar(cb[:, i, :], mpad[:, i, 0:SEQ], col("conv_b_w", i), None, ALU.mult)
                for j in range(1, CONV_B):
                    ve.drain()
                    for i in range(TB):
                        ve.scalar_tensor_tensor(cb[:, i, :], mpad[:, i, j:j + SEQ], col("conv_b_w", j * TB + i),
                                                cb[:, i, :], ALU.mult, ALU.add)
                ve.drain()
                for i in range(TB):
                    ve.tensor_tensor(y[:, TA + i, :], cb[:, i, :], zt[:, 6 + i, :], ALU.mult)
                for i in range(TA):
                    ve.wait_ge(gm_mm, 2 * i + 1)
                    ve.tensor_tensor(ca[:, i, :], ca[:, i, :], banks[4][:, :], ALU.subtract).then_inc(g_c, 1)
                    ve.wait_ge(g_rs, i + 1)
                    ve.reciprocal(rstd[:, 0, :], rstd[:, 1, :])
                    ve.drain()
                    ve.tensor_tensor(ca[:, i, :], ca[:, i, :], rstd[:, 0, :], ALU.mult).then_inc(g_out, 1)
                G = NT * HEADS_C
                vg = vtok.rearrange("p t (h d) -> p (t h) d", d=HD)
                tg = vtmp.rearrange("p t (h d) -> p (t h) d", d=HD)
                ve.wait_ge(v_ev, NT)
                ve.tensor_reduce(vstat[:, 0, :], vg, AX, ALU.add)
                ve.drain()
                ve.tensor_scalar(vstat[:, 0, :], vstat[:, 0, :], -1.0 / HD, None, ALU.mult)
                ve.drain()
                ve.tensor_tensor(vg, vg, vstat[:, 0, :].unsqueeze(2).broadcast_to([P, G, HD]), ALU.add)
                ve.drain()
                ve.tensor_tensor(tg, vg, vg, ALU.mult)
                ve.drain()
                ve.tensor_reduce(vstat[:, 1, :], tg, AX, ALU.add).then_inc(v_act, 1)
                ve.wait_ge(v_act, 2)
                ve.reciprocal(vstat[:, 0, :], vstat[:, 1, :])
                ve.drain()
                ve.tensor_tensor(vg, vg, vstat[:, 0, :].unsqueeze(2).broadcast_to([P, G, HD]), ALU.mult)
                ve.drain()
                ve.wait_ge(vld, 48)
                ve.tensor_tensor(vtok, vtok, vrows[:, 0, :].unsqueeze(1).broadcast_to([P, NT, D_C]), ALU.mult)
                ve.drain()
                ve.tensor_tensor(vtok, vtok, vrows[:, 1, :].unsqueeze(1).broadcast_to([P, NT, D_C]), ALU.add)
                ve.memset(wsT[HD:P, :, 0:HD], 0.0)
                ve.drain().then_inc(v_norm, 1)
                for pr in range(TC):
                    ve.wait_ge(mix_mm, pr + 1)
                    ve.tensor_tensor(y[:, TA + TB + pr, :], banks[6 + pr % 2][:, :], zt[:, 12 + pr, :], ALU.mult)\
                      .then_inc(mix_used, 1)
                barrier(ve, "mixer")
            if stage("w_out"):
                split_input(y)
                residual("w_out")
                barrier(ve, "w_out")
            if stage("w_q"):
                norm_apply(NORM["w_q"], "g_ffn", aT)
                barrier(ve, "w_q")
            if stage("peer"):
                def top(n, par):
                    ve.wait_ge(sc_mm, n + 1)
                    ve.memset(e12, 0.0)
                    sc = [banks[4][:, half * P:(half + 1) * P] for half in range(2)]
                    for half in range(2):
                        ve.max(tv[:, half, 0:8], sc[half])
                    ve.drain()
                    for half in range(2):
                        ve.max_index(ti[:, half, 0:8], tv[:, half, 0:8], sc[half])
                        ve.match_replace(rep[:, half, :], tv[:, half, 0:8], sc[half], LOWEST)
                    ve.drain().then_inc(sc_used, 1)
                    for half in range(2):
                        ve.max(tv[:, half, 8:16], rep[:, half, :])
                    ve.drain()
                    for half in range(2):
                        ve.max_index(ti[:, half, 8:16], tv[:, half, 8:16], rep[:, half, :])
                    ve.tensor_tensor(cand, tv[:, 0, :].unsqueeze(2).broadcast_to([P, TOPK, TOPK]),
                                     tv[:, 1, :].unsqueeze(1).broadcast_to([P, TOPK, TOPK]), ALU.add)
                    ve.drain()
                    flat = cand.rearrange("p a b -> p (a b)")
                    flat2 = cand2.rearrange("p a b -> p (a b)")
                    if not (isinstance(n, int) and n < 1):
                        ve.wait_ge(ex_done, n)
                    ve.tensor_copy(tif, ti[:, :, :])
                    ve.max(cv[:, 0:8], flat)
                    ve.drain()
                    ve.max_index(ci[:, 0:8], cv[:, 0:8], flat)
                    ve.match_replace(flat2, cv[:, 0:8], flat, LOWEST)
                    ve.tensor_scalar(nmax[:, par, :], cv[:, 0:1], -1.0, None, ALU.mult)
                    ve.drain()
                    ve.max(cv[:, 8:16], flat2)
                    ve.drain().then_inc(top_done, 1)
                    ve.max_index(ci[:, 8:16], cv[:, 8:16], flat2)
                    ve.drain()
                    ve.tensor_scalar(cab[:, 0, :], ci[:, :], 4, None, ALU.logical_shift_right)
                    ve.tensor_scalar(cab[:, 1, :], ci[:, :], 15, None, ALU.bitwise_and)
                    ve.drain()
                    entries = iota16.unsqueeze(1).broadcast_to([P, TOPK, TOPK])
                    for half, eq in ((0, eqa), (1, eqb)):
                        ve.tensor_tensor(eq, cab[:, half, :].unsqueeze(2).broadcast_to([P, TOPK, TOPK]), entries,
                                         ALU.is_equal)
                    ve.drain()
                    for half, eq in ((0, eqa), (1, eqb)):
                        ve.tensor_tensor(eq, eq, tif[:, half, :].unsqueeze(1).broadcast_to([P, TOPK, TOPK]), ALU.mult)
                    ve.drain()
                    for half, eq in ((0, eqa), (1, eqb)):
                        ve.tensor_reduce(e12[:, half, :], eq, AX, ALU.add)
                    ve.drain()
                    ve.scalar_tensor_tensor(idx[:, par, :], e12[:, 0, :], float(NKEYS), e12[:, 1, :],
                                            ALU.mult, ALU.add).then_inc(idx_ready, 1)

                def dots(n, par, T):
                    for k in range(TOPK):
                        slot = k % RING
                        ve.wait_ge(u_full[slot], n * 32 + 16 * (k // RING + 1))
                        ve.scalar_tensor_tensor(uring[:, slot, :], uring[:, slot, :], 1.0, ntok[:, T, :],
                                                ALU.mult, ALU.mult, accum_out=act[:, par, k:k + 1])\
                          .then_inc(u_used, 1)
                    ve.drain().then_inc(dots_done, 1)
                    ve.wait_ge(ex_done, n + 1)
                    ve.reciprocal(grec[:, par, :], gsum[:, par, :])
                    ve.drain()
                    ve.wait_ge(gelu_done, n + 1)
                    ve.scalar_tensor_tensor(actg[:, par, :], gel[:, par, :], grec[:, par, :], gex[:, par, :],
                                            ALU.mult, ALU.mult).then_inc(actg_done, 1)

                def add_up(n, par, T):
                    ve.drain()
                    ve.wait_ge(v_used, n * TOPK + TOPK)
                    for c in range(2):
                        a = acc[:, T, c * SEQ:(c + 1) * SEQ]
                        add = ve.tensor_tensor(a, a, banks[2 * par + c][:, :], ALU.add)
                    add.then_inc(out_used, 1)

                ve.memset(acc, 0.0)
                top(0, 0)
                dots(0, 0, 0)
                top(1, 1)
                with ve.Fori(0, UNITS // 2 - 1) as i:
                    for par in range(2):
                        n = i * 2 + (par + 1)
                        dots(n, 1 - par, n // HEADS)
                        top(n + 1, par)
                        add_up(i * 2 + par, par, (i * 2 + par) // HEADS)
                dots(UNITS - 1, 1, NT - 1)
                add_up(UNITS - 2, 0, NT - 1)
                add_up(UNITS - 1, 1, NT - 1)
                for k in range(KT):
                    ve.wait_ge(back_mm, k + 1)
                    ve.tensor_tensor(hT[:, k, :], hT[:, k, :], banks[6 + k % 2][:, :], ALU.add).then_inc(back_used, 1)
                barrier(ve, "peer")
            def gated(name, gate):
                t0, base = TILE0[name], KT * GATED.index(name)
                for n in range(KT):
                    t = t0 + 2 * n
                    ve.wait_ge(mm_done, used(t + 1))
                    ve.wait_ge(sg_ready, base + n + 1)
                    ve.tensor_tensor(pe_in[:, n % 2, :], sg[:, n % 2, :], banks[(t + 1 - gate) % NBANK][:, :],
                                     ALU.mult).then_inc(evac_done, 2)
                    ve.drain()
                    ve.tensor_tensor(hT[:, n, :], hT[:, n, :], pe_in[:, n % 2, :], ALU.add)

            def ple(name, gains):
                norm_apply(NORM[name], gains)
                ve.wait_ge(p_loaded, 16 * (PLES.index(name) + 1))
                split_tile(ps[:, 0, :, :], pT[:, 0, :])
                split_tile(ps[:, 1, :, :], pT[:, 1, :])
                ve.drain().then_inc(p_split, 1)
                gated(name, 0)
                barrier(ve, name)

            def feed_forward(i):
                if stage(f"up{i}"):
                    norm_apply(NORM[f"up{i}"], f"ffn_norm{i}")
                    base = FT * FFNS.index(f"up{i}")
                    w0 = COLS[f"ffn_w{i}"]
                    with ve.Fori(0, FT // 2) as r:
                        for u in range(2):
                            for gv in range(2):
                                buf, bank = conv[:, u, gv, :], banks[(2 * u + gv) % NBANK]
                                at = (r * 4 + (2 * u + gv)) * 3 + w0
                                ve.wait_ge(c_ready, r * 4 + (2 * base + 2 * u + gv + 1))
                                ve.scalar_tensor_tensor(buf[:, 1:], bank[:, 0:SEQ - 1], cols[:, bass.ds(at + 1, 1)],
                                                        buf[:, 1:], ALU.mult, ALU.add)
                                ve.drain()
                                ve.scalar_tensor_tensor(buf[:, 2:], bank[:, 0:SEQ - 2], cols[:, bass.ds(at, 1)],
                                                        buf[:, 2:], ALU.mult, ALU.add).then_inc(evac_done, 1)
                                done = ve.drain()
                                if gv == 0:
                                    done.then_inc(g_conv, 1)
                            ve.wait_ge(g_act, r * 2 + (base + u + 1))
                            ve.tensor_tensor(xt[:, u, :], conv[:, u, 0, :], conv[:, u, 1, :],
                                             ALU.mult).then_inc(prod_done, 1)
                            split_tile(ffz[:, r * 2 + u, :, :], xt[:, u, :])
                    barrier(ve, f"up{i}")
                if stage(f"down{i}"):
                    residual(f"down{i}")
                    barrier(ve, f"down{i}")

            def group_scale(m, x, gain):
                ve.wait_ge(gq_sqrt, m + 1)
                ve.reciprocal(gi[:, m % 2, :], gs[:, m % 2, :])
                ve.drain()
                ve.scalar_tensor_tensor(x, x, gain, gi[:, m % 2, :], ALU.mult, ALU.mult).then_inc(gq_out, 1)

            def reduce_angle(x, n):
                ve.tensor_scalar(n, x, TURN, ROUND, ALU.mult, ALU.add)
                ve.drain()
                ve.tensor_scalar(n, n, ROUND, None, ALU.subtract)
                ve.drain()
                ve.scalar_tensor_tensor(x, n, -PI_HI, x, ALU.mult, ALU.add)
                ve.drain()
                ve.scalar_tensor_tensor(x, n, -PI_LO, x, ALU.mult, ALU.add)
                ve.drain()
                ve.tensor_scalar(x, x, -PI_MAX, PI_MAX, ALU.max, ALU.min)
                ve.drain()

            if stage("ple_a"):
                ple("ple_a", "g_ple")
            if stage("final_a"):
                norm_scale(NORM["final_a"])
                for k in range(KT):
                    ve.scalar_tensor_tensor(hT[:, k, :], hT[:, k, :], col("g_final", k), rstd[:, 0, :],
                                            ALU.mult, ALU.mult).then_inc(a_ready, 1)
                barrier(ve, "final_a")
            def mul(out, a, b):
                ve.tensor_tensor(out, a, b, ALU.mult)

            if stage("ssm_in"):
                norm_apply(NORM["ssm_in"], "ssm_norm")
                dt, ld, th, fr, fi, den, nr, ab, th8, decay8, tmp = [small[:, i, :] for i in range(11)]
                lr, li = spar[:, 0, :], spar[:, 1, :]
                G16 = [P, GROUPS, 2 * CH]

                def each(x, n):
                    return x.unsqueeze(2).broadcast_to([P, GROUPS, n])

                ve.wait_ge(ssm_loaded, 64)
                ve.wait_ge(prep, 1)
                mul(ld, lr, dt)
                mul(th, li, dt)
                ve.memset(halfpi[:, :], math.pi / 2)
                ve.tensor_scalar(nsgn[:, :], sgn, -1.0, None, ALU.mult)
                ve.drain()
                reduce_angle(th, tmp)
                powers = kpow.unsqueeze(1).broadcast_to(G16)
                mul(bigP, each(th, 2 * CH), powers)
                mul(bigM, each(ld, 2 * CH), powers)
                ve.drain()
                reduce_angle(bigP, bigN)
                ve.tensor_copy(th8, bigP[:, :, 2 * CH - 1])
                ve.drain().then_inc(prep, 1)
                ve.wait_ge(prep, 3)
                mul(AR, AR, bigM)
                mul(AI, AI, bigM)
                ve.tensor_copy(decay8, bigM[:, :, 2 * CH - 1])
                mul(den, lr, lr)
                mul(tmp, li, li)
                ve.drain()
                ve.tensor_scalar(row(AIs), row(AI), sgn, None, ALU.mult)
                ve.tensor_tensor(den, den, tmp, ALU.add)
                ve.tensor_scalar(ab, AR[:, :, CH], -1.0, None, ALU.add)
                ve.drain()
                mul(nr, ab, lr)
                mul(tmp, AI[:, :, CH], li)
                mul(fi, AI[:, :, CH], lr)
                mul(fr, ab, li)
                ve.reciprocal(den, den)
                ve.drain()
                ve.tensor_tensor(nr, nr, tmp, ALU.add)
                ve.tensor_tensor(fi, fi, fr, ALU.subtract)
                ve.drain()
                mul(fr, nr, den)
                ve.scalar_tensor_tensor(fi, fi, sgn, den, ALU.mult, ALU.mult)
                ve.drain()
                mul(bigP, each(fi, GC), bbp)
                mul(bigN, each(fi, GC), bb)
                ve.drain()
                mul(bb, each(fr, GC), bb)
                mul(bbp, each(fr, GC), bbp)
                ve.tensor_scalar(row(Cm), row(Cm), nsgn[:, :], None, ALU.mult)
                ve.drain()
                ve.tensor_tensor(bb, bb, bigP, ALU.add)
                ve.tensor_tensor(bbp, bbp, bigN, ALU.subtract)
                ve.drain()
                ve.tensor_copy(shifts[:, 0:P], ident)
                ve.memset(shifts[:, P:], 0.0)
                ve.drain().then_inc(powers_ready, 1)
                barrier(ve, "ssm_in")
            if stage("ssm"):
                th8, decay8 = small[:, 8, :], small[:, 9, :]

                def angles(n):
                    g = bass.ds(n * GT, GT)
                    ve.tensor_tensor(ph.rearrange("p (g j) -> p g j", j=NCH),
                                     th8[:, g].unsqueeze(2).broadcast_to([P, GT, NCH]),
                                     jnum.unsqueeze(1).broadcast_to([P, GT, NCH]), ALU.mult)
                    ve.tensor_copy(decay[:, :, 1:], decay8[:, g].unsqueeze(2).broadcast_to([P, GT, NCH - 1]))
                    ve.drain()
                    reduce_angle(ph, nn)
                    ve.drain().then_inc(ph_ready, 1)

                def recur(n, par, last=False):
                    ve.wait_ge(vs_ready, n + 1)
                    ve.wait_ge(tab_ready, n + 1)
                    mul(t1, vs, cosT[:, par, :])
                    ve.wait_ge(vp_mm, n + 1)
                    mul(t2, banks[5][:, :], sinT[:, par, :])
                    ve.drain()
                    ve.tensor_tensor(t1, t1, t2, ALU.add)
                    ve.drain()
                    ve.tensor_tensor_scan(yv, row(decay), t1, 0.0, ALU.mult, ALU.add)
                    ve.drain().then_inc(yv_ready, 1)
                    if not last:
                        angles(n + 1)
                    mul(t1, yv, cosT[:, par, :])
                    ve.wait_ge(yp_mm, n + 1)
                    mul(t2, banks[5][:, :], sinT[:, par, :])
                    ve.drain()
                    if not (isinstance(n, int) and n == 0):
                        ve.wait_ge(y_mm, n)
                    ve.tensor_tensor(xpad[:, :, 1:], t1.rearrange("p (g j) -> p g j", j=NCH),
                                     t2.rearrange("p (g j) -> p g j", j=NCH), ALU.subtract)
                    ve.drain().then_inc(x_ready, 1)

                ve.memset(xpad[:, :, 0:1], 0.0)
                ve.memset(decay[:, :, 0:1], 0.0)
                angles(0)
                recur(0, 0)
                recur(1, 1)
                with ve.Fori(0, KT // 2 - 2) as i:
                    for par in range(2):
                        recur(i * 2 + (par + 2), par)
                recur(KT - 2, 0)
                recur(KT - 1, 1, True)
                ve.wait_ge(y_back, 16 * KT)
                for n in range(KT):
                    ve.scalar_tensor_tensor(uperm[:, n, :], uperm[:, n, :], col("ssm_d", n), uall[:, n, :],
                                            ALU.mult, ALU.add).then_inc(y_total, 1)
                barrier(ve, "ssm")
            if stage("glu"):
                split_input(aT)
                gated("glu", 1)
                barrier(ve, "glu")
            feed_forward(0)
            if stage("ple0"):
                ple("ple0", "ple_norm0")
            if stage("kv"):
                norm_apply(NORM["kv"], "kv_norm")
                norm_tiles("attn_norm", a2s, a2_ready)
                ve.wait_ge(kv_loaded, 48)
                ve.memset(relb[BUCKETS:BUCKETS + 1, :], NEG)
                ve.tensor_tensor(lamt[:, :, :], lamv[:, 0:4:2, :], lamv[:, 1:4:2, :], ALU.mult)
                ve.tensor_scalar(sub1[:, :], col("subln"), 1.0 - LAM_INIT, None, ALU.mult)
                ve.drain().then_inc(rel_ready, 1)
                ve.tensor_reduce(lams[:, 0:2, 0], lamt[:, :, :], AX, ALU.add)
                ve.drain().then_inc(lam_ready, 1)
                for m in range(2 * HEADS):
                    group_scale(m, KQ[:, m, :], col("k_norm" if m < HEADS else "q_norm"))
                ve.wait_ge(lam_exp, 1)
                ve.scalar_tensor_tensor(nlam[:, :], lams[:, 3, :], -LAM_INIT, lams[:, 2, :],
                                        ALU.add, ALU.subtract)
                barrier(ve, "kv")
            if stage("attn"):
                ve.wait_ge(b_back, 16)
                ve.drain().then_inc(sc_free, NBANK)
                with ve.Fori(0, HEADS) as h:
                    def softmax(qt):
                        w = (qt + 1) * P
                        near = min(w, 2 * P)
                        for c in range(2):
                            bank = banks[2 * (qt % 2) + c]
                            ve.wait_ge(at_sc, h * 8 + (2 * qt + c + 1))
                            if qt:
                                ve.wait_ge(exp_done, h * 8 + (2 * qt + c - 1))
                            ve.scalar_tensor_tensor(ss[:, c, w - near:w], bank[:, w - near:w], HD ** -0.5,
                                                    near_bias[:, h, 2 * P - near:], ALU.mult, ALU.add)
                            if w > near:
                                ve.tensor_scalar(ss[:, c, 0:w - near], bank[:, 0:w - near], HD ** -0.5,
                                                 cols[:, bass.ds(h + COLS["far"], 1)], ALU.mult, ALU.add)
                            ve.drain().then_inc(sc_free, 1)
                            ve.tensor_reduce(nm[:, c, :], ss[:, c, 0:w], AX, ALU.max)
                            ve.drain()
                            ve.tensor_scalar(nm[:, c, :], nm[:, c, :], -1.0, None, ALU.mult)
                            ve.drain().then_inc(mx_ready, 1)

                    def combine(qt):
                        w, b = (qt + 1) * P, qt % 2
                        ve.drain()
                        ve.wait_ge(exp_done, h * 8 + (2 * qt + 2))
                        ve.reciprocal(rr[:, :, 0], sm[:, b, :])
                        ve.drain()
                        ve.tensor_scalar(rr[:, 1, :], rr[:, 1, :], nlam[:, :], None, ALU.mult)
                        ve.drain()
                        ve.tensor_scalar(ee[:, b, 1, 0:w], ee[:, b, 1, 0:w], rr[:, 1, :], None, ALU.mult)
                        ve.drain()
                        ve.scalar_tensor_tensor(att[:, b, 0:w], ee[:, b, 0, 0:w], rr[:, 0, :], ee[:, b, 1, 0:w],
                                                ALU.mult, ALU.add).then_inc(cb_done, 1)

                    softmax(0)
                    softmax(1)
                    combine(0)
                    softmax(2)
                    combine(1)
                    softmax(3)
                    combine(2)
                    combine(3)
                for h in range(HEADS):
                    group_scale(2 * HEADS + h, aT[:, h, :], sub1[:, :])
                barrier(ve, "attn")
            if stage("attn_o"):
                split_input(aT)
                residual("attn_o")
                barrier(ve, "attn_o")
            feed_forward(1)
            if stage("ple1"):
                ple("ple1", "ple_norm1")
        @block.gpsimd
        def _(po):
            def tick():
                po.tensor_tensor(beat[:, 0:1], beat[:, 1:2], beat[:, 1:2], ALU.add)
                po.drain()

            def split(name):
                s0, n, w = SLAB0[name], SLABS[name], KTILES[name] * P

                def slab(s, r=0):
                    src, slot = wring[:, s % NSLOT, 0:w], s % NSPLIT
                    po.wait_ge(w_full[s % NSLOT], r * 16 + 16 * full(s))
                    if not (isinstance(r, int) and s - NSPLIT < FIRST):
                        po.wait_ge(w_used, r * NSLOT + used(s - NSPLIT + 1))
                    po.tensor_tensor(wsp[:, slot, 0, 0:w], src, one.broadcast_to([P, w]), ALU.mult)
                    po.drain()
                    po.tensor_tensor(low(wsp[:, slot, 1, 0:w]), src, wsp[:, slot, 0, 0:w], ALU.subtract)
                    po.drain().then_inc(split_done, 1)

                straight = n if s0 % NSLOT or n % NSLOT else NSLOT if s0 - NSPLIT < FIRST else 0
                for i in range(straight):
                    slab(s0 + i)
                if straight < n:
                    with po.Fori(0, (n - straight) // NSLOT) as r:
                        for u in range(NSLOT):
                            slab(s0 + straight + u, r)

            one = beat[:, 2:3]
            po.memset(beat[:, 0:2], 0.0)
            po.memset(one, 1.0)
            po.drain()
            barrier(po, "setup")
            if stage("mixer"):
                split("w_in")
                barrier(po, "mixer")
            if stage("w_out"):
                split("w_out")
                barrier(po, "w_out")
            if stage("w_q"):
                split("w_q")
                barrier(po, "w_q")
            if stage("peer"):
                BEATS = 2 * TOPK // 4

                def gather(ring, table, arrived, used_up, n, par, i, at):
                    for k in range(TOPK):
                        slot = k % RING
                        if k % 4 == 0 and not (i is None and n == 0 and k < RING):
                            if i is not None:
                                po.wait_ge(beats, i * (2 * BEATS) + (par * BEATS + at + k // 4 + 1))
                            po.wait_ge(used_up, n * TOPK + (k - RING + 4))
                            if i is not None:
                                po.tensor_tensor(beat[:, 0:1], beat[:, 1:2], beat[:, 1:2], ALU.add)\
                                  .then_inc(beats, 1)
                        po.indirect_dma_start(ring[:, slot, :], None, table,
                                              bass.IndirectOffsetOnAxis(idx[:, par, k:k + 1], 0))\
                          .then_inc(arrived[slot], 16)

                def unit(n, par, i=None):
                    po.wait_ge(idx_ready, n + 1)
                    gather(uring, A["expert_u"], u_full, u_used, n, par, i, 0)
                    gather(vring, A["expert_v"], v_full, v_used, n, par, i, BEATS // 2)

                po.tensor_tensor(beat[:, 0:1], beat[:, 1:2], beat[:, 1:2], ALU.add).then_inc(beats, 1)
                unit(0, 0)
                unit(1, 1)
                with po.Fori(0, UNITS // 2 - 1) as i:
                    for par in range(2):
                        unit(i * 2 + (par + 2), par, i)
                po.wait_ge(beats, (UNITS - 2) * BEATS + 1)
                barrier(po, "peer")
            for name in stages[1 + stages.index("peer") if "peer" in stages else 1:]:
                if name in ("mixer", "w_out", "w_q", "peer"):
                    continue
                def matrices(n, par):
                    grp = bass.ds(n * GT, GT)
                    for dst, a1, b1, a2, b2, i0, op, used_up, count, ready in (
                            (gmat, AR, bb, AIs, bbp, 0, ALU.add, h_mm, n - 1, g_ready),
                            (emat, AR, Cm, AI, D2, CH, ALU.subtract, y_mm, n - 1, e_ready)):
                        if not isinstance(n, int):
                            po.wait_ge(used_up, count)
                            tick()
                        dst = dst[:, par, :, :, :]
                        po.tensor_tensor(dst, a1[:, grp, i0:i0 + CH].unsqueeze(3).broadcast_to([P, GT, CH, GC]),
                                         b1[:, grp, :].unsqueeze(2).broadcast_to([P, GT, CH, GC]), ALU.mult)
                        po.tensor_tensor(gtmp, a2[:, grp, i0:i0 + CH].unsqueeze(3).broadcast_to([P, GT, CH, GC]),
                                         b2[:, grp, :].unsqueeze(2).broadcast_to([P, GT, CH, GC]), ALU.mult)
                        po.drain()
                        po.tensor_tensor(dst, dst, gtmp, op)
                        po.drain().then_inc(ready, 1)

                if name in ("ple_a", "ssm_in", "glu", "up0", "down0", "ple0", "attn_o", "up1", "down1", "ple1"):
                    split(name)
                if name == "kv":
                    for layer in ("w_k", "w_v", "attn_q"):
                        split(layer)
                if name == "ssm_in":
                    po.wait_ge(powers_ready, 1)
                    matrices(0, 0)
                    matrices(1, 1)
                if name == "ssm":
                    with po.Fori(0, KT // 2 - 1) as i:
                        for par in range(2):
                            matrices(i * 2 + (par + 2), par)
                if name == "attn":
                    def head(h, first=False):
                        if not first:
                            po.wait_ge(at_sc, h * 8)
                            tick()
                        po.tensor_copy(qh, KQ[:, h + HEADS, :])
                        po.tensor_copy(kh, KQ[:, h, :])
                        po.drain().then_inc(qh_ready, 1)
                        if not first:
                            po.wait_ge(pv_mm, h * 4)
                            tick()
                        po.tensor_copy(vh, vt[:, :, bass.ds(h * P, P)])
                        po.drain().then_inc(vh_ready, 1)

                    head(0, True)
                    with po.Fori(0, HEADS - 1) as i:
                        head(i + 1)
                barrier(po, name)


def _ins():
    shapes = {"xT": (P, KT, SEQ), "cols": (P, NCOLS), "consts": (P, 5 * P + 1),
              "wsT": (P, HEADS_C, P), "vrows": (P, 2, D_C), "b_s": (1, HEADS_C * P), "keysT": (P, 2 * HEADS, P),
              "iota16": (P, TOPK), "expert_u": (NKEYS * NKEYS, D), "expert_v": (NKEYS * NKEYS, D)}
    for name, n, k, _ in LAYERS:
        shapes[name] = (n, P, k * P)
    for name in ("ple_a", "ple0", "ple1"):
        shapes["p_" + name] = (P, 2, SEQ)
    shapes.update({"ssm_par": (P, 3, GROUPS), "ssm_bc": (P, 4, GROUPS, GC),
                   "ssm_k": (P, 2 * CH), "ssm_j": (P, NCH), "lam": (P, 4, HD), "relb": (BUCKETS, HEADS, P),
                   "onehot": (BUCKETS + 1, SKEW)})
    return shapes


def _buckets():
    exact = BUCKETS // 2
    n = np.arange(2 * P)
    nf = np.maximum(n, exact).astype(np.float32)
    large = exact + (np.log(nf / np.float32(exact)) / np.float32(math.log(MAX_DIST / exact))
                     * np.float32(BUCKETS - exact)).astype(np.int32)
    return np.where(n < exact, n, np.minimum(large, BUCKETS - 1))


def _lay_out(inputs):
    f = np.float32
    g = {k: np.asarray(v) for k, v in inputs.items()}

    def slabs(w):
        k, m = w.shape
        return np.ascontiguousarray(w.reshape(k // P, P, m // P, P).transpose(2, 1, 0, 3).reshape(m // P, P, k))

    def tiles(x):
        return np.ascontiguousarray(x.reshape(x.shape[0] // P, P, -1).transpose(1, 0, 2))

    def column(v):
        return v.reshape(-1, P).T

    out = {"xT": tiles(g["x"][0].T)}
    w_in = g["w_in"][0]
    out["w_in"] = slabs(w_in)
    out["wsT"] = np.ascontiguousarray(g["w_s"][0].transpose(2, 0, 1))
    out["vrows"] = np.ascontiguousarray(np.broadcast_to(np.stack([g["ln_c_g"][0], g["ln_c_b"][0]]), (P, 2, D_C)))
    out["b_s"] = g["b_s"][0].reshape(1, -1)
    out["w_out"], out["w_q"] = slabs(g["w_out"][0]), slabs(g["w_q"][0])
    out["keysT"] = np.ascontiguousarray(g["sub_keys"][0].reshape(2 * HEADS, NKEYS, P).transpose(2, 0, 1))
    out["iota16"] = np.ascontiguousarray(np.broadcast_to(np.arange(TOPK, dtype=f), (P, TOPK)))
    out["expert_u"], out["expert_v"] = g["expert_u"][0], g["expert_v"][0]

    def gated(wg, wp):
        return np.concatenate([slabs(wg), slabs(wp)], axis=2)

    out["ple_a"] = gated(g["w_pg"][0], g["w_pe"][0])
    out["p_ple_a"] = tiles(g["p"][0, 0].T)
    for i in range(2):
        out[f"ple{i}"] = gated(g["ple_w_gate_2"][i], g["ple_w_proj_2"][i])
        out[f"p_ple{i}"] = tiles(g["p_2"][i, 0].T)
        up = slabs(g["ffn_w_up_2"][i])
        out[f"up{i}"] = np.ascontiguousarray(up.reshape(2, FT, P, D).transpose(1, 0, 2, 3).reshape(2 * FT, P, D))
        down = slabs(g["ffn_w_down_2"][i])
        out[f"down{i}"] = np.ascontiguousarray(
            down.reshape(KT, P, 2, FF // 2).transpose(0, 2, 1, 3).reshape(2 * KT, P, FF // 2))

    def permuted(w, axis):
        s = w.shape
        w = w.reshape(s[:axis] + (KT, GT, GC) + s[axis + 1:])
        return np.ascontiguousarray(np.swapaxes(w, axis + 1, axis + 2).reshape(s))

    out["ssm_in"] = slabs(permuted(g["ssm_w_in_2"][0], 1))
    glu = slabs(permuted(g["ssm_w_glu_2"][0], 0))
    out["glu"] = np.ascontiguousarray(glu.reshape(2, KT, P, D).transpose(1, 0, 2, 3).reshape(2 * KT, P, D))
    two = lambda a, b: np.concatenate([a, b], axis=0)
    lr, li = g["ssm_lambda_re_2"][0].T, g["ssm_lambda_im_2"][0].T
    out["ssm_par"] = np.ascontiguousarray(
        np.stack([two(lr, lr), two(li, li), np.broadcast_to(g["ssm_log_dt_2"][0], (P, GROUPS))], axis=1))
    br, bi = (g[f"ssm_b_{x}_2"][0].transpose(1, 0, 2) for x in ("re", "im"))
    cr, cim = (g[f"ssm_c_{x}_2"][0].transpose(2, 0, 1) for x in ("re", "im"))
    out["ssm_bc"] = np.ascontiguousarray(np.stack([two(br, bi), two(bi, br), two(cr, cim), two(cim, cr)], axis=1))
    powers = np.concatenate([np.arange(CH - 1, -1, -1), np.arange(1, CH + 1)]).astype(f)
    out["ssm_k"] = np.ascontiguousarray(np.broadcast_to(powers, (P, 2 * CH)))
    out["ssm_j"] = np.ascontiguousarray(np.broadcast_to(np.arange(NCH, dtype=f), (P, NCH)))

    nk = 2 * HEADS * HD
    out["w_k"] = slabs(g["kv_w_2"][:, :nk])
    out["w_v"] = slabs(g["kv_w_2"][:, nk:])
    out["attn_q"], out["attn_o"] = slabs(g["attn_w_q_2"][0]), slabs(g["attn_w_o_2"][0])
    lam = np.stack([g[f"lambda_{x}_2"][0] for x in ("q1", "k1", "q2", "k2")])
    out["lam"] = np.ascontiguousarray(np.broadcast_to(lam, (P, 4, HD)))
    rb = g["rel_bias_2"]
    out["relb"] = np.ascontiguousarray(np.broadcast_to(rb[:, :, None], (BUCKETS, HEADS, P)))
    onehot = np.zeros((BUCKETS + 1, SKEW), f)
    bucket = _buckets()
    for m in range(SKEW):
        n = 2 * P - 1 - m
        onehot[bucket[n] if n >= 0 else BUCKETS, m] = 1.0
    out["onehot"] = onehot

    half = np.arange(P) // HD
    consts = [np.eye(P), np.full((P, P), 1.0 / D), (half[:, None] == half[None]) / HD,
              np.roll(np.eye(P), HD, axis=0), np.full((P, P), 1.0 / P), np.where(half, 1.0, -1.0)[:, None]]
    out["consts"] = np.concatenate(consts, axis=1).astype(f)

    c = {"g_mix": g["g_mix"], "conv_a_w": g["conv_a_w"][0], "conv_a_b": g["conv_a_b"], "ln_a_g": g["ln_a_g"],
         "ln_a_b": g["ln_a_b"], "conv_b_w": g["conv_b_w"][0], "g_ffn": g["g_ffn"], "g_ple": g["g_ple"],
         "g_final": g["g_final"], "ssm_norm": g["ssm_norm_2"], "ssm_d": permuted(g["ssm_d_2"], 1),
         "kv_norm": g["kv_norm_2"], "k_norm": two(g["k_norm_2"], g["k_norm_2"]), "attn_norm": g["attn_norm_2"],
         "q_norm": two(g["q_norm_2"][0], g["q_norm_2"][0]), "subln": g["subln_2"]}
    for i in range(2):
        c[f"ffn_norm{i}"], c[f"ple_norm{i}"] = g["ffn_norm_2"][i], g["ple_norm_2"][i]
        w = g["ffn_conv_w_2"][i].reshape(3, 2, FT, P).transpose(2, 1, 0, 3)
        c[f"ffn_w{i}"] = w
        c[f"ffn_b{i}"] = g["ffn_conv_b_2"][i].reshape(2, FT, P).transpose(1, 0, 2)
    blocks = {k: column(np.ascontiguousarray(v)) for k, v in c.items()}
    blocks["far"] = np.broadcast_to(rb[BUCKETS - 1], (P, HEADS))
    out["cols"] = np.concatenate([blocks[k] for k in COLS], axis=1)
    return {k: np.ascontiguousarray(v) for k, v in out.items()}


def kernel(**inputs):
    import concourse.bacc as bacc
    from concourse.bass_utils import run_bass_kernel_spmd

    nc = bacc.Bacc("TRN2", target_bir_lowering=False, num_devices=1)
    arrays = _lay_out(inputs)
    A = {}
    for name, shape in _ins().items():
        assert arrays[name].shape == shape, (name, arrays[name].shape, shape)
        A[name] = nc.dram_tensor(name + "_dram", shape, F32, kind="ExternalInput").ap()
    A["outT"] = nc.dram_tensor("outT_dram", (P, KT, SEQ), F32, kind="ExternalOutput").ap()
    build(nc, A)
    r = run_bass_kernel_spmd(nc, [{name + "_dram": a for name, a in arrays.items()}], core_ids=[0])
    outT = r.results[0]["outT_dram"]
    return np.ascontiguousarray(outT.transpose(1, 0, 2).reshape(D, SEQ).T)[None]
```

```python
import math
from contextlib import ExitStack

import numpy as np
import concourse.bass as bass
from concourse import mybir

F32 = mybir.dt.float32
F16, BF16 = mybir.dt.float16, mybir.dt.bfloat16
U32 = mybir.dt.uint32
ALU = mybir.AluOpType
ACT = mybir.ActivationFunctionType
AX = mybir.AxisListType.X

P = 128
SEQ, D = 512, 1024
KT = D // P
NT = SEQ // P
EPS = 1e-6
D_A, D_B, D_C = 384, 256, 384
TA, TB, TC = D_A // P, D_B // P, D_C // P
HD = 64
HEADS_C = D_C // HD
CONV_A, CONV_B = 31, 3
HEADS, TOPK, NKEYS = 8, 16, 128
UNITS = NT * HEADS
RING = 8
GROUPS, GC, ST = 64, 16, 64
CH = 8
NCH = SEQ // CH
GT = P // GC
FF = 2816
FT = FF // P
LAM_INIT = 0.8 - 0.6 * math.exp(-0.3)
NEG = -1e30
LOWEST = -3.0e38
BUCKETS, MAX_DIST = 32, 128
SKEW = 3 * P

COLS = {}
_at = 0
for _name, _n in [("g_mix", KT), ("conv_a_w", CONV_A * TA), ("conv_a_b", TA), ("ln_a_g", TA), ("ln_a_b", TA),
                  ("conv_b_w", CONV_B * TB), ("g_ffn", KT), ("g_ple", KT), ("g_final", KT), ("ssm_norm", KT),
                  ("ssm_d", KT), ("kv_norm", KT), ("k_norm", 1), ("attn_norm", KT), ("q_norm", 1), ("subln", 1),
                  ("ffn_norm0", KT), ("ffn_norm1", KT), ("ffn_w0", 3 * 2 * FT), ("ffn_w1", 3 * 2 * FT),
                  ("ffn_b0", 2 * FT), ("ffn_b1", 2 * FT), ("ple_norm0", KT), ("ple_norm1", KT), ("far", HEADS)]:
    COLS[_name] = _at
    _at += _n
NCOLS = _at

WSLOT = 11 * P
NSLOT = NBANK = 4
NSPLIT = 2


LAYERS = [("w_in", 18, 8, 18), ("w_out", 8, 8, 8), ("ple_a", 8, 10, 16), ("ssm_in", 8, 8, 8),
          ("glu", 16, 8, 16), ("up0", 44, 8, 44), ("down0", 16, 11, 8), ("ple0", 8, 10, 16), ("w_k", 8, 8, 8),
          ("w_v", 8, 8, 8), ("attn_q", 8, 8, 8), ("attn_o", 8, 8, 8), ("up1", 44, 8, 44), ("down1", 16, 11, 8), ("ple1", 8, 10, 16)]
STAGES = ["setup", "mixer", "w_out", "w_q", "peer", "ple_a", "final_a", "ssm_in", "ssm", "glu",
          "up0", "down0", "ple0", "kv", "attn", "attn_o", "up1", "down1", "ple1"]
LAYER_STAGE = {"w_in": "mixer", "w_k": "kv", "w_v": "kv", "attn_q": "kv"}


def build(nc, A, first=0, last=99):
    stages = [s for i, s in enumerate(STAGES) if i == 0 or first <= i <= last]
    SLAB0, TILE0, SLABS, KTILES, TILES = {}, {}, {}, {}, {}
    FIRST = 2 if "mixer" in stages else NSLOT
    s = t = FIRST
    for name, n, k, m in LAYERS:
        if LAYER_STAGE.get(name, name) in stages:
            SLAB0[name], TILE0[name], SLABS[name], KTILES[name], TILES[name] = s, t, n, k, m
            s += n
            t += m

    def used(s):
        return s - FIRST + 1

    def full(s):
        return s // NSLOT + (1 if s % NSLOT >= FIRST % NSLOT and FIRST < NSLOT else 0)

    NORM = {}
    for name in ("mixer", "w_q", "ple_a", "final_a", "ssm_in", "up0", "ple0", "kv", "up1", "ple1"):
        if name in stages:
            NORM[name] = len(NORM)
    PLES = [name for name in ("ple_a", "ple0", "ple1") if name in stages]
    ctx = ExitStack()
    with ctx:
        def sb(name, shape, dt=F32):
            return ctx.enter_context(nc.sbuf_tensor(name, shape, dt))

        def sem(name):
            return ctx.enter_context(nc.semaphore(name))

        hT = sb("hT", [P, KT, SEQ])
        aT = sb("aT", [P, KT, SEQ])
        wring = sb("wring", [P, NSLOT, WSLOT])
        cols = sb("cols", [P, NCOLS])
        rstd = sb("rstd", [P, 2, SEQ])
        sq = sb("sq", [P, 2, SEQ])
        consts = sb("consts", [P, 5 * P + 1])
        xt = sb("xt", [P, 2, SEQ])
        ident = consts[:, 0:P]
        onesD = consts[:, P:2 * P]
        blk64 = consts[:, 2 * P:3 * P]
        swap = consts[:, 3 * P:4 * P]
        ones128 = consts[:, 4 * P:5 * P]
        sgn = consts[:, 5 * P:5 * P + 1]
        eps = sb("eps", [P, 1])
        ones_row = sb("ones_row", [1, P])
        idx = sb("idx", [P, 2, TOPK], U32)
        Z = sb("Z", [P, FT * SEQ])
        R = sb("R", [P, 22528])
        banks = [ctx.enter_context(nc.psum_tensor(f"bank{i}", [P, SEQ], F32)) for i in range(8)]

        def view(arena, at, *shape):
            n = int(np.prod(shape))
            v = arena[:, at:at + n]
            if len(shape) == 2:
                v = v.rearrange("p (a b) -> p a b", b=shape[1])
            elif len(shape) == 3:
                v = v.rearrange("p (a b c) -> p a b c", b=shape[1], c=shape[2])
            elif len(shape) == 4:
                v = v.rearrange("p (a b c d) -> p a b c d", b=shape[1], c=shape[2], d=shape[3])
            return v

        def parts_of(arena, at, tiles, width):
            v = arena[:, at:at + tiles * width].bitcast(F16)
            return v.rearrange("p (k h n) -> p k h n", h=2, n=width)

        def low(ap):
            return ap.bitcast(BF16)

        xs = parts_of(R, 14848, KT, SEQ)
        wsp = parts_of(R, 18944, NSPLIT, WSLOT)

        def col(name, i=0, n=1):
            return cols[:, COLS[name] + i:COLS[name] + i + n]

        def row(ap):
            return ap.rearrange("p a b -> p (a b)")

        biasD = nc.dram_tensor("biasD", [P, HEADS * SKEW], F32, kind="Internal")
        uD = nc.dram_tensor("uD", [KT, P, SEQ], F32, kind="Internal")
        yD = nc.dram_tensor("yD", [KT, P, SEQ], F32, kind="Internal")

        stage_done = sem("stage_done")
        loaded = sem("loaded")
        w_full = [sem(f"w_full{i}") for i in range(NSLOT)]
        w_used = sem("w_used")
        mm_done = sem("mm_done")
        evac_done = sem("evac_done")
        sumsq = sq[:, 0, :]
        sumsq2 = sb("sumsq2", [P, SEQ])
        ss_ready, stat_mm = sem("ss_ready"), sem("stat_mm")
        rs_ready, a_ready = sem("rs_ready"), sem("a_ready")
        out_stored = sem("out_stored")

        zt = view(Z, 0, 18, SEQ)
        ypad = view(R, 0, TA, SEQ + CONV_A - 1)
        ca = view(R, 1632, TA, SEQ)
        mpad = view(R, 3168, TB, SEQ + CONV_B - 1)
        cb = view(R, 4208, TB, SEQ)
        y = view(R, 5232, KT, SEQ)
        vtok = view(R, 9328, NT, D_C)
        vtmp = view(R, 10864, NT, D_C)
        wsT = view(R, 12400, HEADS_C, P)
        vrows = view(R, 13168, 2, D_C)
        bs_row = R[0:1, 13936:13936 + HEADS_C * P]
        vstat = view(R, 14704, 2, NT * HEADS_C)
        vld = sem("vld")
        conv_ready = sem("conv_ready")
        m_ready, gm_mm, gm_used, g_c, g_sq, g_rs, g_out = [sem(n) for n in
            ("m_ready", "gm_mm", "gm_used", "g_c", "g_sq", "g_rs", "g_out")]
        v_mm, v_ev, v_act, v_norm, mix_mm, mix_used = [sem(n) for n in
            ("v_mm", "v_ev", "v_act", "v_norm", "mix_mm", "mix_used")]

        qT = view(Z, 0, 2, SEQ)
        wq = view(Z, 6144, 2, D)
        keysT = view(Z, 2 * HEADS * SEQ, 2 * HEADS, P)
        iota16 = Z[:, 10240:10256]
        diag = view(Z, 10256, 4, P)
        uring = view(R, 0, RING, D)
        vring = view(R, RING * D, RING, D)
        ntok = view(R, 2 * RING * D, NT, D)
        acc = view(Z, 2048, NT, D)
        s0 = 2 * RING * D + NT * D
        qcur = view(R, s0, 2, 2, P)
        rep = view(R, s0 + 512, 2, P)
        tv = view(R, s0 + 768, 2, TOPK)
        tif = view(R, s0 + 800, 2, TOPK)
        cv = R[:, s0 + 832:s0 + 848]
        e12 = view(R, s0 + 848, 2, TOPK)
        nmax = view(R, s0 + 880, 2, 1)
        act = view(R, s0 + 882, 2, TOPK)
        gel = view(R, s0 + 914, 2, TOPK)
        gex = view(R, s0 + 946, 2, TOPK)
        gsum = view(R, s0 + 978, 2, 1)
        grec = view(R, s0 + 980, 2, 1)
        actg = view(R, s0 + 982, 2, TOPK)
        cand = view(Z, 10768, TOPK, TOPK)
        cand2 = view(R, s0 + 1014, TOPK, TOPK)
        eqa = view(R, s0 + 1270, TOPK, TOPK)
        eqb = view(R, s0 + 1526, TOPK, TOPK)
        ti = sb("ti", [P, 2, TOPK], U32)
        ci = sb("ci", [P, TOPK], U32)
        cab = sb("cab", [P, 2, TOPK], U32)
        keys_loaded = sem("keys_loaded")
        wq_full, q_mm, q_ev = sem("wq_full"), sem("q_mm"), sem("q_ev")
        u_full = [sem(f"u_full{i}") for i in range(RING)]
        v_full = [sem(f"v_full{i}") for i in range(RING)]
        u_used, v_used = sem("u_used"), sem("v_used")
        q_cur, sc_mm, sc_used, top_done, ex_done, dots_done, gelu_done, actg_done, diag_done, out_used, idx_ready = [
            sem(n) for n in ("q_cur", "sc_mm", "sc_used", "top_done", "ex_done", "dots_done", "gelu_done",
                             "actg_done", "diag_done", "out_used", "idx_ready")]
        nt_mm, nt_ev, back_mm, back_used = sem("nt_mm"), sem("nt_ev"), sem("back_mm"), sem("back_used")

        pT = view(R, 0, 2, SEQ)
        sg = view(R, 1024, 2, SEQ)
        pe_in = view(R, 2048, 2, SEQ)
        ps = parts_of(R, 3072, 2, SEQ)
        p_loaded, sg_ready, p_split = sem("p_loaded"), sem("sg_ready"), sem("p_split")
        split_done, x_split = sem("split_done"), sem("x_split")
        SPLITS = [name for name in ("w_out", "glu", "attn_o") if name in stages]
        beat, beats = sb("beat", [P, 3]), sem("beats")

        uperm = view(Z, 0, KT, SEQ)
        uall = view(Z, KT * SEQ, KT, SEQ)
        spar = view(Z, 8192, 3, GROUPS)
        kpow = Z[:, 8384:8384 + 2 * CH]
        jnum = Z[:, 8400:8400 + NCH]
        small = view(Z, 8464, 11, GROUPS)
        cosT = view(Z, 9216, 2, SEQ)
        ysb = view(Z, 10240, 2, SEQ)
        sbc = view(R, 0, 4, GROUPS, GC)
        bb, bbp, Cm, D2 = [sbc[:, i, :, :] for i in range(4)]
        AR, AI, AIs = [view(R, 4096 + 1024 * i, GROUPS, 2 * CH) for i in range(3)]
        gmat = view(R, 7168, 2, GT * CH * GC).rearrange("p b (g i c) -> p b g i c", i=CH, c=GC)
        shifts = R[:, 10240:10240 + (2 * CH - 1) * GC]
        hmat = R[:, 10496:10496 + P]
        emat = view(R, 11008, 2, GT * CH * GC).rearrange("p b (g i c) -> p b g i c", i=CH, c=GC)
        gtmp = view(R, 13056, GT, CH, GC)
        bT = view(R, 14080, GT, P)
        Tg = view(R, 15104, 2, GT, P)
        sinT = view(R, 17152, 2, SEQ)
        ph = R[:, 18176:18688]
        nn = R[:, 18688:19200]
        vs = R[:, 19200:19712]
        t1 = R[:, 19712:20224]
        yv = R[:, 20224:20736]
        xpad = view(R, 20736, GT, NCH + 1)
        decay = view(R, 21256, GT, NCH)
        t2 = R[:, 21768:22280]
        bigP, bigN, bigM = [view(R, 7168 + 1024 * i, GROUPS, 2 * CH) for i in range(3)]
        halfpi, nsgn = sb("halfpi", [P, 1]), sb("nsgn", [P, 1])
        [ssm_loaded, u_stored, u_back, powers_ready, g_ready, e_ready, h_mm, h_ev, bt_mm, t_mm, bt_ev, te_ev, s_v_mm, vs_ready, vp_mm,
         yv_ready, yp_mm, x_ready, y_mm, yo_ev, y_stored, y_total, ph_ready, tab_ready, prep] = [
            sem(n) for n in ("ssm_loaded", "u_stored", "u_back", "powers_ready", "g_ready", "e_ready", "h_mm", "h_ev", "bt_mm", "t_mm",
                             "bt_ev", "te_ev", "s_v_mm", "vs_ready", "vp_mm", "yv_ready", "yp_mm", "x_ready",
                             "y_mm", "yo_ev", "y_stored", "y_total", "ph_ready", "tab_ready", "prep")]

        y_back = [sem(f"y_back{n}") for n in range(KT)]

        ffz = parts_of(Z, 0, FT, SEQ)
        conv = view(R, 0, 2, 2, SEQ)
        c_ready, g_conv, g_act, prod_done = [sem(n) for n in ("c_ready", "g_conv", "g_act", "prod_done")]

        KQ = view(Z, 0, 2 * HEADS, SEQ)
        vt = view(R, 0, NT, D)
        a2s = parts_of(R, 4096, KT, SEQ)
        vf = view(R, 8192, KT, SEQ)
        gs, gi = rstd, xt
        relb = R[0:BUCKETS + 1, 12288:12288 + HEADS * P]
        onehot = R[0:BUCKETS + 1, 13312:13312 + SKEW]
        lamv = view(R, 13696, 4, HD)
        lams = view(R, 13952, 8, 1)
        bias_sb = view(Z, 8192, HEADS, SKEW)
        near_bias = view(R, 20480, HEADS, 2 * P)
        nlam, sub1, lamt = sb("nlam", [P, 1]), sb("sub1", [P, 1]), sb("lamt", [P, 2, HD])
        qh = R[:, 4096:4608]
        kh = R[:, 10752:11264]
        vh = view(R, 4608, NT, P)
        ss = view(R, 5120, 2, SEQ)
        ee = view(R, 6144, 2, 2, SEQ)
        att = view(R, 8192, 2, SEQ)
        attT = view(R, 9216, 2, NT, P)
        nm = view(R, 10240, 2, 1)
        sm = view(R, 10242, 2, 2)
        rr = view(R, 10246, 2, 1)
        [kv_loaded, a2_ready, v2_mm, v2_ev, gq_ready, gq_free, x_gelu, gq_mm, gq_sqrt, lam_ready, lam_exp, b_mm, b_ev, b_stored,
         b_back, at_sc, rel_ready, sc_free, mx_ready, exp_done, cb_done, tr_mm, tr_ev, pv_mm, o_ev, qh_ready, vh_ready] = [
            sem(n) for n in ("kv_loaded", "a2_ready", "v2_mm", "v2_ev", "gq_ready", "gq_free", "x_gelu", "gq_mm", "gq_sqrt",
                             "lam_ready", "lam_exp", "b_mm", "b_ev", "b_stored", "b_back", "at_sc", "rel_ready", "sc_free",
                             "mx_ready", "exp_done", "cb_done", "tr_mm", "tr_ev", "pv_mm", "o_ev", "qh_ready",
                             "vh_ready")]
        GATED = [name for name in ("ple_a", "glu", "ple0", "ple1") if name in stages]
        FFNS = [name for name in ("up0", "up1") if name in stages]

        TURN = 1.0 / (2.0 * math.pi)
        ROUND = 1.5 * 2.0 ** 23
        PI_HI, PI_LO = 6.28125, 2.0 * math.pi - 6.28125
        PI_MAX = 3.1415925

        block = ctx.enter_context(nc.Block())

        def stage(name):
            return name in stages

        def after(name):
            return 3 * len([s for s in stages if STAGES.index(s) <= STAGES.index(name)])

        def barrier(eng, name):
            eng.drain().then_inc(stage_done, 1)
            eng.wait_ge(stage_done, after(name))

        @block.sync
        def _(sp):
            def stream(name):
                s0, n = SLAB0[name], SLABS[name]
                k = KTILES[name] * P
                W = A[name]
                straight = n if s0 % NSLOT or n % NSLOT else NSLOT if s0 - NSLOT < FIRST else 0
                for i in range(straight):
                    s = s0 + i
                    if s - NSLOT >= FIRST:
                        sp.wait_ge(split_done, used(s - NSLOT))
                    sp.dma_start(wring[:, s % NSLOT, 0:k], W[i]).then_inc(w_full[s % NSLOT], 16)
                if straight == n:
                    return
                with sp.Fori(0, (n - straight) // NSLOT) as r:
                    for u in range(NSLOT):
                        sp.wait_ge(split_done, r * NSLOT + used(s0 + straight + u - NSLOT))
                        sp.dma_start(wring[:, u, 0:k], W[r * NSLOT + (straight + u)]).then_inc(w_full[u], 16)

            sp.dma_start(hT[:, :, :], A["xT"]).then_inc(loaded, 16)
            sp.dma_start(cols[:, :], A["cols"]).then_inc(loaded, 16)
            sp.dma_start(consts[:, :], A["consts"]).then_inc(loaded, 16)
            if stage("mixer"):
                stream("w_in")
                sp.dma_start(wsT, A["wsT"]).then_inc(vld, 16)
                sp.dma_start(vrows, A["vrows"]).then_inc(vld, 16)
                sp.dma_start(bs_row, A["b_s"]).then_inc(vld, 16)
            if stage("w_out"):
                stream("w_out")
            if stage("w_q"):
                sp.wait_ge(stage_done, after("mixer"))
                sp.dma_start(keysT, A["keysT"]).then_inc(keys_loaded, 16)
                sp.dma_start(iota16, A["iota16"]).then_inc(keys_loaded, 16)
                for h in range(HEADS if stage("peer") else 0):
                    if h:
                        sp.wait_ge(q_mm, 2 * h)
                    for half in range(2):
                        sp.dma_start(wq[:, half, :], A["w_q"][2 * h + half]).then_inc(wq_full, 16)
            def flat(t, n):
                return t.ap()[n].rearrange("a b -> (a b)")

            for name in stages:
                before = stages[stages.index(name) - 1]
                if name in ("glu", "up0", "down0", "attn_o", "up1", "down1"):
                    stream(name)
                if name in PLES:
                    up = {"ple0": "up0", "ple1": "up1"}.get(name, before)
                    sp.wait_ge(stage_done, after(up))
                    sp.dma_start(pT, A["p_" + name]).then_inc(p_loaded, 16)
                    stream(name)
                if name == "ssm_in":
                    sp.wait_ge(stage_done, after(before))
                    sp.dma_start(sbc, A["ssm_bc"]).then_inc(ssm_loaded, 16)
                    sp.dma_start(spar, A["ssm_par"]).then_inc(ssm_loaded, 16)
                    sp.dma_start(kpow, A["ssm_k"]).then_inc(ssm_loaded, 16)
                    sp.dma_start(jnum, A["ssm_j"]).then_inc(ssm_loaded, 16)
                    stream(name)
                    for n in range(KT):
                        sp.wait_ge(evac_done, used(TILE0[name] + n))
                        sp.dma_start(flat(uD, n).rearrange("(s p j) -> p s j", p=P, j=NCH),
                                     uperm[:, n, :].rearrange("p (s j) -> p s j", j=NCH)).then_inc(u_stored, 16)
                    for n in range(KT):
                        sp.wait_ge(u_stored, 16 * KT)
                        sp.dma_start(uall[:, n, :], uD.ap()[n]).then_inc(u_back, 16)
                if name == "ssm":
                    for n in range(KT):
                        sp.wait_ge(yo_ev, n + 1)
                        sp.dma_start(yD.ap()[n], ysb[:, n % 2, :]).then_inc(y_stored, 16)
                        sp.wait_ge(y_stored, 16 * (n + 1))
                        sp.dma_start(uall[:, n, :].rearrange("p (s j) -> p s j", j=NCH),
                                     flat(yD, n).rearrange("(s p j) -> p s j", p=P, j=NCH)).then_inc(y_back[n], 16)
                if name == "kv":
                    stream("w_k")
                    sp.wait_ge(stage_done, after(before))
                    sp.dma_start(relb[0:BUCKETS, :].rearrange("b (h p) -> b h p", p=P), A["relb"])\
                      .then_inc(kv_loaded, 16)
                    sp.dma_start(onehot, A["onehot"]).then_inc(kv_loaded, 16)
                    sp.dma_start(lamv, A["lam"]).then_inc(kv_loaded, 16)
                    stream("w_v")
                    stream("attn_q")
                    sp.wait_ge(b_ev, HEADS)
                    sp.dma_start(biasD.ap().rearrange("p (h m) -> p h m", m=SKEW), bias_sb).then_inc(b_stored, 16)
                    sp.wait_ge(b_stored, 16)
                    sp.dma_start(near_bias, bass.AP(biasD, P - 1, [[HEADS * SKEW - 1, P], [SKEW, HEADS], [1, 2 * P]]))\
                      .then_inc(b_back, 16)
            sp.wait_ge(stage_done, 3 * len(stages))
            sp.dma_start(A["outT"], hT[:, :, :]).then_inc(out_stored, 16)
            sp.wait_ge(out_stored, 16)
        @block.tensor
        def _(pe):
            def norm_stats(i):
                pe.wait_ge(ss_ready, i + 1)
                pe.matmul(banks[5][:, :], onesD, sumsq, start=True, stop=True).then_inc(stat_mm, 1)

            def free_bank(t, r, step):
                if step or t - NBANK >= FIRST:
                    pe.wait_ge(evac_done, r * step + used(t - NBANK))

            PARTS = ((0, 0), (0, 1), (1, 0))

            def product(bank, slot, k0, n, x, ready=None, base=0, start=True, stop=True, first_of_slab=True):
                for k in range(n):
                    if ready is not None:
                        pe.wait_ge(ready, base + k + 1)
                    for p, (i, j) in enumerate(PARTS):
                        w, v = wsp[:, slot, i, (k0 + k) * P:(k0 + k + 1) * P], x[:, k, j, :]
                        mm = pe.matmul(bank[:, :], low(w) if i else w, low(v) if j else v,
                                       start=(start and k == 0 and p == 0), stop=(stop and k == n - 1 and p == 2))
                        if k == 0 and p == 0 and first_of_slab:
                            mm.then_inc(w_used, 1)
                return mm

            def plain(name, x, ready=None, base=0):
                n, s0, t0, kt = SLABS[name], SLAB0[name], TILE0[name], KTILES[name]
                if s0 % NSLOT or n % NSLOT:
                    for i in range(n):
                        s, t = s0 + i, t0 + i
                        pe.wait_ge(split_done, used(s))
                        free_bank(t, 0, 0)
                        product(banks[t % NBANK], s % NSPLIT, 0, kt, x, ready if i == 0 else None, base)\
                            .then_inc(mm_done, 1)
                    return
                with pe.Fori(0, n // NSLOT) as r:
                    for u in range(NSLOT):
                        pe.wait_ge(split_done, r * NSLOT + used(s0 + u))
                        free_bank(t0 + u, r, NSLOT)
                        product(banks[u], u % NSPLIT, 0, kt, x, ready if u == 0 else None, base).then_inc(mm_done, 1)

            def paired(name, x, ready, base):
                n, s0, t0 = SLABS[name], SLAB0[name], TILE0[name]
                with pe.Fori(0, n // NSLOT) as r:
                    for u in range(NSLOT):
                        pe.wait_ge(split_done, r * NSLOT + used(s0 + u))
                        free_bank(t0 + 2 * u, r, 2 * NSLOT)
                        product(banks[2 * u % NBANK], u % NSPLIT, 0, KT, x, ready if u == 0 else None, base)\
                            .then_inc(mm_done, 1)
                        free_bank(t0 + 2 * u + 1, r, 2 * NSLOT)
                        if u == 0:
                            pe.wait_ge(p_split, PLES.index(name) + 1)
                        product(banks[(2 * u + 1) % NBANK], u % NSPLIT, KT, 2, ps, first_of_slab=False)\
                            .then_inc(mm_done, 1)

            def halves(name, x):
                n, s0, t0, kt = SLABS[name], SLAB0[name], TILE0[name], KTILES[name]
                with pe.Fori(0, n // (2 * NSLOT)) as r:
                    for u in range(NBANK):
                        free_bank(t0 + u, r, NBANK)
                        for half in range(2):
                            v = 2 * u + half
                            pe.wait_ge(split_done, r * (2 * NSLOT) + used(s0 + v))
                            mm = product(banks[u], v % NSPLIT, 0, kt, x[:, half * kt:(half + 1) * kt, :, :],
                                         start=(half == 0), stop=(half == 1))
                        mm.then_inc(mm_done, 1)

            pe.wait_ge(loaded, 48)
            barrier(pe, "setup")
            if stage("mixer"):
                norm_stats(NORM["mixer"])
                plain("w_in", xs, a_ready, KT * NORM["mixer"])
                pe.wait_ge(evac_done, used(TILE0["w_in"] + 17))
                for T in range(NT):
                    if T >= 2:
                        pe.wait_ge(v_ev, T - 1)
                    for k in range(TC):
                        mm = pe.transpose(banks[6 + T % 2][:, k * P:(k + 1) * P], zt[:, 15 + k, T * P:(T + 1) * P],
                                          ident)
                    mm.then_inc(v_mm, 1)
                pe.wait_ge(conv_ready, 1)
                for i in range(TA):
                    if i:
                        pe.wait_ge(g_c, i)
                    pe.matmul(banks[4][:, :], blk64, ca[:, i, :], start=True, stop=True).then_inc(gm_mm, 1)
                    pe.wait_ge(g_sq, i + 1)
                    pe.matmul(banks[5][:, :], blk64, sq[:, i % 2, :], start=True, stop=True).then_inc(gm_mm, 1)
                pe.wait_ge(vld, 48)
                pe.wait_ge(v_norm, 1)
                for pr in range(TC):
                    if pr == 2:
                        pe.wait_ge(mix_used, 1)
                    for T in range(NT):
                        for hh in range(2):
                            h = 2 * pr + hh
                            out = banks[6 + pr % 2][hh * HD:(hh + 1) * HD, T * P:(T + 1) * P]
                            pe.matmul(out, vtok[:, T, h * HD:(h + 1) * HD], wsT[:, h, :], start=True, stop=False)
                            mm = pe.matmul(out, ones_row[0:1, 0:HD], bs_row[0:1, h * P:(h + 1) * P],
                                           start=False, stop=True, tile_position=(0, hh * HD))
                    mm.then_inc(mix_mm, 1)
                barrier(pe, "mixer")
            if stage("w_out"):
                plain("w_out", xs, x_split, KT * SPLITS.index("w_out"))
                barrier(pe, "w_out")
            if stage("w_q"):
                norm_stats(NORM["w_q"])
                for T in range(NT):
                    if T >= 1:
                        pe.wait_ge(nt_ev, 2 * T)
                    for k in range(KT):
                        if T == 0:
                            pe.wait_ge(a_ready, KT * NORM["w_q"] + k + 1)
                        mm = pe.transpose(banks[6 + k // 4][:, (k % 4) * P:(k % 4 + 1) * P],
                                          aT[:, k, T * P:(T + 1) * P], ident)
                        if k % 4 == 3:
                            mm.then_inc(nt_mm, 1)
                barrier(pe, "w_q")
            if stage("peer"):
                def scores(n, par, h):
                    pe.wait_ge(q_cur, n + 1)
                    if not (isinstance(n, int) and n == 0):
                        pe.wait_ge(sc_used, n)
                    for half in range(2):
                        mm = pe.matmul(banks[4][:, half * P:(half + 1) * P], qcur[:, par, half, :],
                                       keysT[:, h * 2 + half, :], start=True, stop=True)
                    mm.then_inc(sc_mm, 1)

                def combine(n, par):
                    if not (isinstance(n, int) and n < 2):
                        pe.wait_ge(out_used, n - 1)
                    for k in range(TOPK):
                        slot = k % RING
                        pe.wait_ge(diag_done, n * TOPK + k + 1)
                        pe.wait_ge(v_full[slot], n * 32 + 16 * (k // RING + 1))
                        for c in range(2):
                            mm = pe.matmul(banks[2 * par + c][:, :], diag[:, k % 4, :],
                                           vring[:, slot, c * SEQ:(c + 1) * SEQ], start=(k == 0),
                                           stop=(k == TOPK - 1))
                        mm.then_inc(v_used, 1)

                def queries(h, half, first=False):
                    pe.wait_ge(wq_full, h * 32 + 32)
                    if not first:
                        pe.wait_ge(q_ev, h * 2)
                    for k in range(KT):
                        mm = pe.matmul(banks[6 + half][:, :], wq[:, half, k * P:(k + 1) * P], aT[:, k, :],
                                       start=(k == 0), stop=(k == KT - 1))
                    mm.then_inc(q_mm, 1)

                def head(h, last=False):
                    for T in range(NT):
                        n = h * NT + T
                        combine(n, T % 2)
                        if T < 2 and not last:
                            queries(h + 1, T)
                        if not (last and T >= 2):
                            scores(n + 2, T % 2, h + (T + 2) // NT)

                pe.wait_ge(keys_loaded, 32)
                queries(0, 0, True)
                queries(0, 1, True)
                scores(0, 0, 0)
                scores(1, 1, 0)
                head(0)
                with pe.Fori(0, HEADS - 2) as i:
                    head(i + 1)
                head(HEADS - 1, True)
                pe.wait_ge(out_used, UNITS)
                for k in range(KT):
                    if k >= 2:
                        pe.wait_ge(back_used, k - 1)
                    for T in range(NT):
                        mm = pe.transpose(banks[6 + k % 2][:, T * P:(T + 1) * P], acc[:, T, k * P:(k + 1) * P], ident)
                    mm.then_inc(back_mm, 1)
                barrier(pe, "peer")
            def ple(name):
                norm_stats(NORM[name])
                paired(name, xs, a_ready, KT * NORM[name])
                barrier(pe, name)

            def feed_forward(i):
                if stage(f"up{i}"):
                    norm_stats(NORM[f"up{i}"])
                    plain(f"up{i}", xs, a_ready, KT * NORM[f"up{i}"])
                    barrier(pe, f"up{i}")
                if stage(f"down{i}"):
                    halves(f"down{i}", ffz)
                    barrier(pe, f"down{i}")

            def group_stat(m, mean, u=None):
                b = (m if u is None else u) % 2
                pe.wait_ge(gq_ready, m + 1)
                pe.wait_ge(gq_free, m + 1)
                pe.matmul(banks[4 + b][:, :], mean, sq[:, b, :], start=True, stop=True).then_inc(gq_mm, 1)

            if stage("ple_a"):
                ple("ple_a")
            if stage("final_a"):
                norm_stats(NORM["final_a"])
                pe.matmul(banks[4][:, :], onesD, sumsq2[:, :], start=True, stop=True).then_inc(stat_mm, 1)
                barrier(pe, "final_a")
            if stage("ssm_in"):
                if not stage("final_a"):
                    norm_stats(NORM["ssm_in"])
                plain("ssm_in", xs, a_ready, KT * NORM["ssm_in"])
                barrier(pe, "ssm_in")
            if stage("ssm"):
                def input_matrices(n, par):
                    zero = isinstance(n, int) and n == 0
                    pe.wait_ge(g_ready, n + 1)
                    for half in range(2):
                        if not zero:
                            pe.wait_ge(bt_ev, n * 2 - (1 - half))
                        for g in range(4):
                            mm = pe.transpose(banks[half][:, g * P:(g + 1) * P], row(gmat[:, par, half * 4 + g, :, :]),
                                              ident)
                        mm.then_inc(bt_mm, 1)
                    if not zero:
                        pe.wait_ge(h_ev, n)
                    for g in range(GT):
                        mm = pe.matmul(banks[2][:, g * GC:(g + 1) * GC], row(gmat[:, par, g, :, :]),
                                       Cm[:, n * GT + g, :], start=True, stop=True)
                    mm.then_inc(h_mm, 1)

                def output_matrices(n):
                    pe.wait_ge(h_ev, n + 1)
                    for half in range(2):
                        if not (isinstance(n, int) and n == 0):
                            pe.wait_ge(te_ev, n * 2 - (1 - half))
                        for j in range(4):
                            at = (CH - 1 - half * 4 - j) * GC
                            mm = pe.matmul(banks[3 + 3 * half][:, j * P:(j + 1) * P], shifts[:, at:at + P], hmat,
                                           start=True, stop=True)
                        mm.then_inc(t_mm, 1)

                def recur(n, par, last=False):
                    zero = isinstance(n, int) and n == 0
                    pe.wait_ge(bt_ev, n * 2 + 2)
                    if not zero:
                        pe.wait_ge(vs_ready, n)
                    for g in range(GT):
                        mm = pe.matmul(banks[4][:, g * NCH:(g + 1) * NCH], bT[:, g, :],
                                       uall[:, n, g * NCH:(g + 1) * NCH], start=True, stop=True)
                    mm.then_inc(s_v_mm, 1)
                    pe.wait_ge(vs_ready, n + 1)
                    if not zero:
                        pe.wait_ge(x_ready, n)
                    pe.matmul(banks[5][:, :], swap, vs, start=True, stop=True).then_inc(vp_mm, 1)
                    if not last:
                        input_matrices(n + 1, 1 - par)
                    pe.wait_ge(yv_ready, n + 1)
                    pe.matmul(banks[5][:, :], swap, yv, start=True, stop=True).then_inc(yp_mm, 1)
                    if not last:
                        output_matrices(n + 1)
                    pe.wait_ge(te_ev, n * 2 + 2)
                    pe.wait_ge(e_ready, n + 1)
                    pe.wait_ge(x_ready, n + 1)
                    if not zero:
                        pe.wait_ge(yo_ev, n)
                    for g in range(GT):
                        out = banks[7][:, g * NCH:(g + 1) * NCH]
                        pe.matmul(out, Tg[:, par, g, :], uall[:, n, g * NCH:(g + 1) * NCH], start=True, stop=False)
                        mm = pe.matmul(out, row(emat[:, par, g, :, :]),
                                       xpad[:, g, 0:NCH], start=False, stop=True)
                    mm.then_inc(y_mm, 1)

                input_matrices(0, 0)
                output_matrices(0)
                pe.wait_ge(u_back, 16 * KT)
                recur(0, 0)
                recur(1, 1)
                with pe.Fori(0, KT // 2 - 2) as i:
                    for par in range(2):
                        recur(i * 2 + (par + 2), par)
                recur(KT - 2, 0)
                recur(KT - 1, 1, True)
                barrier(pe, "ssm")
            if stage("glu"):
                plain("glu", xs, x_split, KT * SPLITS.index("glu"))
                barrier(pe, "glu")
            feed_forward(0)
            if stage("ple0"):
                ple("ple0")
            if stage("kv"):
                norm_stats(NORM["kv"])
                plain("w_k", xs, a_ready, KT * NORM["kv"])
                with pe.Fori(0, SLABS["w_v"] // NSLOT) as r:
                    for u in range(NSLOT):
                        pe.wait_ge(split_done, r * NSLOT + used(SLAB0["w_v"] + u))
                        free_bank(TILE0["w_v"] + u, r, NSLOT)
                        product(banks[u], u % NSPLIT, 0, KT, xs).then_inc(mm_done, 1)
                        group_stat(r * NSLOT + u, blk64, u)
                plain("attn_q", a2s, a2_ready, 0)
                for T in range(NT):
                    for c in range(2):
                        b = 2 * T + c
                        if b >= 2:
                            pe.wait_ge(v2_ev, b - 1)
                        for k in range(4):
                            mm = pe.transpose(banks[6 + c][:, k * P:(k + 1) * P], vf[:, 4 * c + k, T * P:(T + 1) * P],
                                              ident)
                        mm.then_inc(v2_mm, 1)
                        group_stat(HEADS + b, blk64)
                pe.wait_ge(kv_loaded, 48)
                pe.wait_ge(rel_ready, 1)
                for h in range(HEADS):
                    if h >= 2:
                        pe.wait_ge(b_ev, h - 1)
                    pe.matmul(banks[h % 2][:, 0:SKEW], relb[:, h * P:(h + 1) * P], onehot,
                              start=True, stop=True).then_inc(b_mm, 1)
                barrier(pe, "kv")
            if stage("attn"):
                def scores2(h, qt):
                    w = (qt + 1) * P
                    for c in range(2):
                        pe.wait_ge(sc_free, h * 8 + (2 * qt + c + 1))
                        rows = slice(c * HD, (c + 1) * HD)
                        pe.matmul(banks[2 * (qt % 2) + c][:, 0:w], qh[rows, qt * P:(qt + 1) * P],
                                  kh[rows, 0:w], start=True, stop=True).then_inc(at_sc, 1)

                def values(h, qt, first=False):
                    pe.wait_ge(cb_done, h * 4 + (qt + 1))
                    if qt or not first:
                        pe.wait_ge(tr_ev, h * 4 + qt)
                    for kt in range(qt + 1):
                        mm = pe.transpose(banks[4 + qt % 2][:, kt * P:(kt + 1) * P],
                                          att[:, qt % 2, kt * P:(kt + 1) * P], ident)
                    mm.then_inc(tr_mm, 1)
                    if qt == 0:
                        pe.wait_ge(vh_ready, h + 1)
                        if not first:
                            pe.wait_ge(o_ev, h)
                    pe.wait_ge(tr_ev, h * 4 + (qt + 1))
                    for kt in range(qt + 1):
                        mm = pe.matmul(banks[6][:, qt * P:(qt + 1) * P], vh[:, kt, :],
                                       attT[:, qt % 2, kt, :], start=(kt == 0), stop=(kt == qt))
                    mm.then_inc(pv_mm, 1)

                def head(h, first=False, last=False):
                    scores2(h, 2)
                    values(h, 0, first)
                    scores2(h, 3)
                    values(h, 1, first)
                    if not last:
                        pe.wait_ge(qh_ready, h + 2)
                        scores2(h + 1, 0)
                    values(h, 2, first)
                    if not last:
                        scores2(h + 1, 1)
                    values(h, 3, first)

                pe.wait_ge(qh_ready, 1)
                scores2(0, 0)
                scores2(0, 1)
                head(0, first=True)
                with pe.Fori(0, (HEADS - 2) // 2) as i:
                    head(i * 2 + 1)
                    head(i * 2 + 2)
                head(HEADS - 1, last=True)
                for h in range(HEADS):
                    group_stat(2 * HEADS + h, ones128)
                barrier(pe, "attn")
            if stage("attn_o"):
                plain("attn_o", xs, x_split, KT * SPLITS.index("attn_o"))
                barrier(pe, "attn_o")
            feed_forward(1)
            if stage("ple1"):
                ple("ple1")
        @block.scalar
        def _(ac):
            def norm_root(i):
                ac.wait_ge(stat_mm, i + 1)
                ac.activation(rstd[:, 1, :], banks[5][:, :], ACT.Sqrt, bias=eps[:, :]).then_inc(rs_ready, 1)

            def copies(name, out):
                t0, n = TILE0[name], TILES[name]
                with ac.Fori(0, n // NBANK) as r:
                    for u in range(NBANK):
                        ac.wait_ge(mm_done, r * NBANK + used(t0 + u))
                        ac.activation(out[:, r * NBANK + u, :], banks[u][:, :], ACT.Copy).then_inc(evac_done, 1)

            ac.wait_ge(loaded, 48)
            barrier(ac, "setup")
            if stage("mixer"):
                norm_root(NORM["mixer"])
                for i in range(TILES["w_in"]):
                    t = TILE0["w_in"] + i
                    ac.wait_ge(mm_done, used(t))
                    ac.activation(zt[:, i, :], banks[t % NBANK][:, :],
                                  ACT.Sigmoid if TA <= i < 2 * TA else ACT.Copy).then_inc(evac_done, 1)
                for T in range(NT):
                    ac.wait_ge(v_mm, T + 1)
                    ac.activation(vtok[:, T, :], banks[6 + T % 2][:, 0:D_C], ACT.Copy).then_inc(v_ev, 1)
                for i in range(TA):
                    ac.wait_ge(g_c, i + 1)
                    if i == 2:
                        ac.wait_ge(gm_mm, 2)
                    ac.activation(sq[:, i % 2, :], ca[:, i, :], ACT.Square).then_inc(g_sq, 1)
                    ac.wait_ge(gm_mm, 2 * i + 2)
                    if i:
                        ac.wait_ge(g_out, i)
                    ac.activation(rstd[:, 1, :], banks[5][:, :], ACT.Sqrt, bias=eps[:, :]).then_inc(g_rs, 1)
                ac.wait_ge(v_act, 1)
                ac.activation(vstat[:, 1, :], vstat[:, 1, :], ACT.Sqrt, bias=eps[:, :], scale=1.0 / HD)\
                  .then_inc(v_act, 1)
                for i in range(TA):
                    ac.wait_ge(g_out, i + 1)
                    ac.activation(y[:, i, :], ca[:, i, :], ACT.Silu, bias=col("ln_a_b", i), scale=col("ln_a_g", i))
                barrier(ac, "mixer")
            if stage("w_out"):
                barrier(ac, "w_out")
            if stage("w_q"):
                norm_root(NORM["w_q"])
                for T in range(NT):
                    for c in range(2):
                        ac.wait_ge(nt_mm, 2 * T + c + 1)
                        ac.activation(ntok[:, T, c * SEQ:(c + 1) * SEQ], banks[6 + c][:, :], ACT.Copy)\
                          .then_inc(nt_ev, 1)
                barrier(ac, "w_q")
            if stage("peer"):
                def query(n, par, T):
                    if not (isinstance(n, int) and n < 2):
                        ac.wait_ge(sc_mm, n - 1)
                    ac.activation(qcur[:, par, :, :], qT[:, :, T * P:(T + 1) * P], ACT.Copy)\
                      .then_inc(q_cur, 1)

                def exps(n, par):
                    ac.wait_ge(top_done, n + 1)
                    ac.activation(gex[:, par, :], cv, ACT.Exp, bias=nmax[:, par, :],
                                  accum_out=gsum[:, par, :]).then_inc(ex_done, 1)

                def weights(n, par):
                    ac.wait_ge(dots_done, n + 1)
                    ac.activation(gel[:, par, :], act[:, par, :], ACT.Gelu_apprx_tanh).then_inc(gelu_done, 1)

                def diags(n, par):
                    ac.wait_ge(actg_done, n + 1)
                    for k in range(TOPK):
                        if not (isinstance(n, int) and n == 0 and k < 4):
                            ac.wait_ge(v_used, n * TOPK + k - 3)
                        ac.activation(diag[:, k % 4, :], ident, ACT.Copy, scale=actg[:, par, k:k + 1])\
                          .then_inc(diag_done, 1)

                def queries(h):
                    for half in range(2):
                        ac.wait_ge(q_mm, h * 2 + (half + 1))
                        ac.activation(qT[:, half, :], banks[6 + half][:, :], ACT.Copy).then_inc(q_ev, 1)
                    ac.drain()

                def head(h, last=False):
                    for T in range(NT):
                        n = h * NT + T
                        weights(n, T % 2)
                        diags(n, T % 2)
                        if not (last and T == NT - 1):
                            exps(n + 1, (T + 1) % 2)
                        if not (last and T >= 2):
                            query(n + 2, T % 2, (T + 2) % NT)
                        if T == 1 and not last:
                            ac.drain()
                            queries(h + 1)

                queries(0)
                query(0, 0, 0)
                query(1, 1, 1)
                exps(0, 0)
                head(0)
                with ac.Fori(0, HEADS - 2) as i:
                    head(i + 1)
                head(HEADS - 1, True)
                barrier(ac, "peer")
            def sigmoids(name, gate):
                t0 = TILE0[name]
                for n in range(KT):
                    t = t0 + 2 * n + gate
                    ac.wait_ge(mm_done, used(t))
                    if n >= 2:
                        ac.wait_ge(evac_done, used(t0 + 2 * n - 3))
                    ac.activation(sg[:, n % 2, :], banks[t % NBANK][:, :], ACT.Sigmoid)\
                      .then_inc(sg_ready, 1)

            def ple(name):
                norm_root(NORM[name])
                sigmoids(name, 0)
                barrier(ac, name)

            def feed_forward(i):
                if stage(f"up{i}"):
                    norm_root(NORM[f"up{i}"])
                    t0, base = TILE0[f"up{i}"], FT * FFNS.index(f"up{i}")
                    w2, b = COLS[f"ffn_w{i}"] + 2, COLS[f"ffn_b{i}"]

                    def pair(u, r=None):
                        for gv in range(2):
                            f = u if r is None else r * 2 + (u + 2)
                            ac.wait_ge(mm_done, f * 2 + used(t0 + gv))
                            if r is not None or base:
                                ac.wait_ge(prod_done, f + base - 1)
                            at = f * 2 + gv
                            ac.activation(conv[:, u, gv, :], banks[(2 * u + gv) % NBANK][:, :], ACT.Identity,
                                          bias=cols[:, bass.ds(at + b, 1)], scale=cols[:, bass.ds(at * 3 + w2, 1)])\
                              .then_inc(c_ready, 1)
                        ac.wait_ge(g_conv, f + (base + 1))
                        ac.activation(conv[:, u, 0, :], conv[:, u, 0, :], ACT.Gelu_apprx_tanh).then_inc(g_act, 1)

                    pair(0)
                    pair(1)
                    with ac.Fori(0, FT // 2 - 1) as r:
                        pair(0, r)
                        pair(1, r)
                    barrier(ac, f"up{i}")
                if stage(f"down{i}"):
                    barrier(ac, f"down{i}")

            def group_square(m, x, u=None):
                ac.wait_ge(gq_free, m + 1)
                ac.activation(sq[:, (m if u is None else u) % 2, :], x, ACT.Square).then_inc(gq_ready, 1)

            def group_sqrt(m, u=None):
                b = (m if u is None else u) % 2
                ac.wait_ge(gq_mm, m + 1)
                ac.activation(gs[:, b, :], banks[4 + b][:, :], ACT.Sqrt, bias=eps[:, :]).then_inc(gq_sqrt, 1)

            if stage("ple_a"):
                ple("ple_a")
            if stage("final_a"):
                norm_root(NORM["final_a"])
                ac.wait_ge(ss_ready, NORM["ssm_in"] + 1)
                ac.activation(rstd[:, 1, :], xt[:, 0, :], ACT.Sqrt, bias=eps[:, :]).then_inc(rs_ready, 1)
                barrier(ac, "final_a")
            if stage("ssm_in"):
                if not stage("final_a"):
                    norm_root(NORM["ssm_in"])
                ac.wait_ge(ssm_loaded, 64)
                ac.activation(small[:, 0, :], spar[:, 2, :], ACT.Exp).then_inc(prep, 1)
                for n in range(KT):
                    if n == NBANK:
                        ac.wait_ge(prep, 2)
                        ac.activation(bigM, bigM, ACT.Exp)
                        ac.activation(AI, bigP, ACT.Sin)
                        ac.activation(AR, bigP, ACT.Abs)
                        ac.drain()
                        ac.activation(AR, AR, ACT.Sin, bias=halfpi[:, :], scale=-1.0)
                        ac.drain().then_inc(prep, 1)
                    t = TILE0["ssm_in"] + n
                    ac.wait_ge(mm_done, used(t))
                    ac.activation(uperm[:, n, :].rearrange("p (s j) -> p j s", j=NCH),
                                  banks[t % NBANK][:, :].rearrange("p (j s) -> p j s", s=CH), ACT.Copy)\
                      .then_inc(evac_done, 1)
                barrier(ac, "ssm_in")
            if stage("ssm"):
                def tables(n, par):
                    ac.wait_ge(ph_ready, n + 1)
                    if not (isinstance(n, int) and n < 2):
                        ac.wait_ge(x_ready, n - 1)
                    ac.activation(sinT[:, par, :], ph, ACT.Sin, scale=nsgn[:, :])
                    ac.activation(cosT[:, par, :], ph, ACT.Abs)
                    ac.drain()
                    ac.activation(cosT[:, par, :], cosT[:, par, :], ACT.Sin, bias=halfpi[:, :], scale=-1.0)
                    ac.drain().then_inc(tab_ready, 1)

                def input_matrices(n, par):
                    for half in range(2):
                        ac.wait_ge(bt_mm, n * 2 + (half + 1))
                        ac.activation(row(bT[:, half * 4:half * 4 + 4, :]), banks[half][:, :], ACT.Copy)\
                          .then_inc(bt_ev, 1)
                    ac.wait_ge(h_mm, n + 1)
                    if not (isinstance(n, int) and n == 0):
                        ac.wait_ge(t_mm, n * 2)
                    ac.activation(hmat, banks[2][:, 0:P], ACT.Copy).then_inc(h_ev, 1)

                def output_matrices(n, par):
                    if not (isinstance(n, int) and n < 2):
                        ac.wait_ge(y_mm, n - 1)
                    for half in range(2):
                        ac.wait_ge(t_mm, n * 2 + (half + 1))
                        ac.activation(Tg[:, par, :, half * SEQ // 8:(half + 1) * SEQ // 8]
                                      .rearrange("p g (t c) -> p t g c", c=GC),
                                      banks[3 + 3 * half][:, :].rearrange("p (t g c) -> p t g c", g=GT, c=GC),
                                      ACT.Copy).then_inc(te_ev, 1)

                def recur(n, par, last=False):
                    ac.wait_ge(s_v_mm, n + 1)
                    if not (isinstance(n, int) and n == 0):
                        ac.wait_ge(yv_ready, n)
                    ac.activation(vs, banks[4][:, :], ACT.Copy).then_inc(vs_ready, 1)
                    if not last:
                        input_matrices(n + 1, 1 - par)
                        tables(n + 1, 1 - par)
                        output_matrices(n + 1, 1 - par)
                    ac.wait_ge(y_mm, n + 1)
                    if not (isinstance(n, int) and n < 2):
                        ac.wait_ge(y_stored, n * 16 - 16)
                    ac.activation(ysb[:, par, :], banks[7][:, :], ACT.Copy).then_inc(yo_ev, 1)

                input_matrices(0, 0)
                output_matrices(0, 0)
                tables(0, 0)
                recur(0, 0)
                recur(1, 1)
                with ac.Fori(0, KT // 2 - 2) as i:
                    for par in range(2):
                        recur(i * 2 + (par + 2), par)
                recur(KT - 2, 0)
                recur(KT - 1, 1, True)
                for n in range(KT):
                    ac.wait_ge(y_total, n + 1)
                    ac.activation(aT[:, n, :].rearrange("p (j s) -> p j s", s=CH),
                                  uperm[:, n, :].rearrange("p (s j) -> p j s", j=NCH), ACT.Gelu_apprx_tanh)\
                      .then_inc(x_gelu, 1)
                barrier(ac, "ssm")
            if stage("glu"):
                sigmoids("glu", 1)
                barrier(ac, "glu")
            feed_forward(0)
            if stage("ple0"):
                ple("ple0")
            if stage("kv"):
                norm_root(NORM["kv"])
                copies("w_k", KQ[:, 0:HEADS, :])
                ac.drain()
                with ac.Fori(0, HEADS // NBANK) as r:
                    for u in range(NBANK):
                        m = r * NBANK + u
                        group_square(m, KQ[:, m, :], u)
                        ac.wait_ge(mm_done, r * NBANK + used(TILE0["w_v"] + u))
                        ac.activation(vf[:, m, :], banks[u][:, :], ACT.Copy).then_inc(evac_done, 1)
                        group_sqrt(m, u)
                copies("attn_q", KQ[:, HEADS:, :])
                ac.drain()
                for b in range(2 * NT):
                    group_square(HEADS + b, KQ[:, HEADS + b, :])
                    ac.wait_ge(v2_mm, b + 1)
                    ac.activation(vt[:, b // 2, (b % 2) * SEQ:(b % 2 + 1) * SEQ], banks[6 + b % 2][:, :], ACT.Copy)\
                      .then_inc(v2_ev, 1)
                    group_sqrt(HEADS + b)
                ac.wait_ge(lam_ready, 1)
                ac.activation(lams[:, 2:4, :], lams[:, 0:2, :], ACT.Exp).then_inc(lam_exp, 1)
                for h in range(HEADS):
                    ac.wait_ge(b_mm, h + 1)
                    ac.activation(bias_sb[:, h, :], banks[h % 2][:, 0:SKEW], ACT.Copy).then_inc(b_ev, 1)
                barrier(ac, "kv")
            if stage("attn"):
                def queries(h):
                    ac.activation(qh, KQ[:, h + HEADS, :], ACT.Copy)
                    ac.activation(kh, KQ[:, h, :], ACT.Copy)
                    ac.drain().then_inc(qh_ready, 1)

                def head_values(h):
                    ac.activation(vh, vt[:, :, bass.ds(h * P, P)], ACT.Copy).then_inc(vh_ready, 1)

                def exps(h, qt):
                    w = (qt + 1) * P
                    for c in range(2):
                        ac.wait_ge(mx_ready, h * 8 + (2 * qt + c + 1))
                        ac.activation(ee[:, qt % 2, c, 0:w], ss[:, c, 0:w], ACT.Exp, bias=nm[:, c, :],
                                      accum_out=sm[:, qt % 2, c:c + 1]).then_inc(exp_done, 1)

                def turned(h, qt):
                    ac.wait_ge(tr_mm, h * 4 + (qt + 1))
                    ac.activation(row(attT[:, qt % 2, 0:qt + 1, :]), banks[4 + qt % 2][:, 0:(qt + 1) * P], ACT.Copy)\
                      .then_inc(tr_ev, 1)

                def head(h, last=False):
                    turned(h, 0)
                    exps(h, 2)
                    turned(h, 1)
                    exps(h, 3)
                    if not last:
                        queries(h + 1)
                    turned(h, 2)
                    if not last:
                        exps(h + 1, 0)
                    turned(h, 3)
                    ac.wait_ge(pv_mm, h * 4 + 4)
                    ac.activation(aT[:, h, :], banks[6][:, :], ACT.Copy).then_inc(o_ev, 1)
                    if not last:
                        head_values(h + 1)
                        exps(h + 1, 1)

                queries(0)
                head_values(0)
                exps(0, 0)
                exps(0, 1)
                head(0)
                with ac.Fori(0, (HEADS - 2) // 2) as i:
                    head(i * 2 + 1)
                    head(i * 2 + 2)
                head(HEADS - 1, last=True)
                ac.drain()
                for h in range(HEADS):
                    group_square(2 * HEADS + h, aT[:, h, :])
                    group_sqrt(2 * HEADS + h)
                barrier(ac, "attn")
            if stage("attn_o"):
                barrier(ac, "attn_o")
            feed_forward(1)
            if stage("ple1"):
                ple("ple1")
        @block.vector
        def _(ve):
            def split_tile(dst, src):
                ve.drain()
                ve.tensor_copy(dst[:, 0, :], src)
                ve.drain()
                return ve.tensor_tensor(low(dst[:, 1, :]), src, dst[:, 0, :], ALU.subtract)

            def add_square(x):
                ve.drain()
                ve.tensor_tensor(sq[:, 1, :], x, x, ALU.mult)
                ve.drain()
                ve.tensor_tensor(sumsq, sumsq, sq[:, 1, :], ALU.add)

            def squares_from_here(then):
                if then in NORM:
                    ve.memset(sumsq, 0.0)

            def squares_done(then):
                if then in NORM:
                    ve.drain().then_inc(ss_ready, 1)

            def all_squares(then):
                squares_from_here(then)
                for k in range(KT):
                    add_square(hT[:, k, :])
                squares_done(then)

            def norm_scale(i):
                ve.wait_ge(rs_ready, i + 1)
                ve.reciprocal(rstd[:, 0, :], rstd[:, 1, :])
                ve.drain()

            def norm_tiles(gains, parts, ready, out=None):
                for k in range(KT):
                    t = xt[:, k % 2, :] if out is None else out[:, k, :]
                    ve.scalar_tensor_tensor(t, hT[:, k, :], col(gains, k), rstd[:, 0, :], ALU.mult, ALU.mult)
                    split_tile(parts[:, k, :, :], t).then_inc(ready, 1)

            def norm_apply(i, gains, out=None):
                norm_scale(i)
                norm_tiles(gains, xs, a_ready, out)

            def split_input(src):
                for k in range(KT):
                    split_tile(xs[:, k, :, :], src[:, k, :]).then_inc(x_split, 1)

            def residual(name, then):
                t0, n = TILE0[name], TILES[name]
                squares_from_here(then)
                with ve.Fori(0, n // NBANK) as r:
                    for u in range(NBANK):
                        ve.wait_ge(mm_done, r * NBANK + used(t0 + u))
                        h = hT[:, r * NBANK + u, :]
                        ve.tensor_tensor(h, h, banks[u][:, :], ALU.add).then_inc(evac_done, 1)
                        if then in NORM:
                            add_square(h)
                squares_done(then)

            ve.memset(eps[:, :], EPS)
            ve.memset(ones_row[:, :], 1.0)
            ve.wait_ge(loaded, 48)
            if len(stages) > 1 and stages[1] in NORM:
                all_squares(stages[1])
            barrier(ve, "setup")
            if stage("mixer"):
                norm_apply(NORM["mixer"], "g_mix")
                ve.memset(ypad[:, :, 0:CONV_A - 1], 0.0)
                ve.memset(mpad[:, :, 0:CONV_B - 1], 0.0)
                ve.wait_ge(evac_done, used(TILE0["w_in"] + 2 * TA - 1))
                for i in range(TA):
                    ve.tensor_tensor(ypad[:, i, CONV_A - 1:], zt[:, i, :], zt[:, TA + i, :], ALU.mult)
                ve.drain()
                for i in range(TA):
                    ve.tensor_scalar(ca[:, i, :], ypad[:, i, 0:SEQ], col("conv_a_w", i), col("conv_a_b", i),
                                     ALU.mult, ALU.add)
                ve.drain()
                TAPS = 6
                with ve.Fori(0, (CONV_A - 1) // TAPS) as r:
                    for u in range(1, TAPS + 1):
                        j = r * TAPS + u
                        for i in range(TA):
                            ve.scalar_tensor_tensor(ca[:, i, :], ypad[:, i, bass.ds(j, SEQ)],
                                                    cols[:, bass.ds(j * TA + (COLS["conv_a_w"] + i), 1)], ca[:, i, :],
                                                    ALU.mult, ALU.add)
                        ve.drain()
                ve.drain().then_inc(conv_ready, 1)
                ve.wait_ge(evac_done, used(TILE0["w_in"] + 11))
                for i in range(TB):
                    ve.tensor_tensor(mpad[:, i, CONV_B - 1:], zt[:, 8 + i, :], zt[:, 10 + i, :], ALU.mult)
                ve.drain()
                for i in range(TB):
                    ve.tensor_scalar(cb[:, i, :], mpad[:, i, 0:SEQ], col("conv_b_w", i), None, ALU.mult)
                for j in range(1, CONV_B):
                    ve.drain()
                    for i in range(TB):
                        ve.scalar_tensor_tensor(cb[:, i, :], mpad[:, i, j:j + SEQ], col("conv_b_w", j * TB + i),
                                                cb[:, i, :], ALU.mult, ALU.add)
                ve.drain()
                for i in range(TB):
                    ve.tensor_tensor(y[:, TA + i, :], cb[:, i, :], zt[:, 6 + i, :], ALU.mult)
                G = NT * HEADS_C
                vg = vtok.rearrange("p t (h d) -> p (t h) d", d=HD)
                tg = vtmp.rearrange("p t (h d) -> p (t h) d", d=HD)
                for i in range(TA):
                    ve.wait_ge(gm_mm, 2 * i + 1)
                    ve.tensor_tensor(ca[:, i, :], ca[:, i, :], banks[4][:, :], ALU.subtract).then_inc(g_c, 1)
                    if i == 0:
                        ve.wait_ge(v_ev, NT)
                        ve.tensor_reduce(vstat[:, 0, :], vg, AX, ALU.add)
                        ve.drain()
                        ve.tensor_scalar(vstat[:, 0, :], vstat[:, 0, :], -1.0 / HD, None, ALU.mult)
                        ve.drain()
                        ve.tensor_tensor(vg, vg, vstat[:, 0, :].unsqueeze(2).broadcast_to([P, G, HD]), ALU.add)
                    if i == 1:
                        ve.drain()
                        ve.tensor_tensor(tg, vg, vg, ALU.mult)
                        ve.drain()
                        ve.tensor_reduce(vstat[:, 1, :], tg, AX, ALU.add).then_inc(v_act, 1)
                    ve.wait_ge(g_rs, i + 1)
                    ve.reciprocal(rstd[:, 0, :], rstd[:, 1, :])
                    ve.drain()
                    ve.tensor_tensor(ca[:, i, :], ca[:, i, :], rstd[:, 0, :], ALU.mult).then_inc(g_out, 1)
                ve.wait_ge(v_act, 2)
                ve.reciprocal(vstat[:, 0, :], vstat[:, 1, :])
                ve.drain()
                ve.tensor_tensor(vg, vg, vstat[:, 0, :].unsqueeze(2).broadcast_to([P, G, HD]), ALU.mult)
                ve.drain()
                ve.wait_ge(vld, 48)
                ve.tensor_tensor(vtok, vtok, vrows[:, 0, :].unsqueeze(1).broadcast_to([P, NT, D_C]), ALU.mult)
                ve.drain()
                ve.tensor_tensor(vtok, vtok, vrows[:, 1, :].unsqueeze(1).broadcast_to([P, NT, D_C]), ALU.add)
                ve.memset(wsT[HD:P, :, 0:HD], 0.0)
                ve.drain().then_inc(v_norm, 1)
                for pr in range(TC):
                    ve.wait_ge(mix_mm, pr + 1)
                    ve.tensor_tensor(y[:, TA + TB + pr, :], banks[6 + pr % 2][:, :], zt[:, 12 + pr, :], ALU.mult)\
                      .then_inc(mix_used, 1)
                barrier(ve, "mixer")
            if stage("w_out"):
                split_input(y)
                residual("w_out", "w_q")
                barrier(ve, "w_out")
            if stage("w_q"):
                norm_scale(NORM["w_q"])
                for k in range(KT):
                    ve.scalar_tensor_tensor(aT[:, k, :], hT[:, k, :], col("g_ffn", k), rstd[:, 0, :],
                                            ALU.mult, ALU.mult).then_inc(a_ready, 1)
                barrier(ve, "w_q")
            if stage("peer"):
                def top(n, par):
                    ve.wait_ge(sc_mm, n + 1)
                    ve.memset(e12, 0.0)
                    sc = [banks[4][:, half * P:(half + 1) * P] for half in range(2)]
                    for half in range(2):
                        ve.max(tv[:, half, 0:8], sc[half])
                    ve.drain()
                    for half in range(2):
                        ve.max_index(ti[:, half, 0:8], tv[:, half, 0:8], sc[half])
                        ve.match_replace(rep[:, half, :], tv[:, half, 0:8], sc[half], LOWEST)
                    ve.drain().then_inc(sc_used, 1)
                    for half in range(2):
                        ve.max(tv[:, half, 8:16], rep[:, half, :])
                    ve.drain()
                    for half in range(2):
                        ve.max_index(ti[:, half, 8:16], tv[:, half, 8:16], rep[:, half, :])
                    ve.tensor_tensor(cand, tv[:, 0, :].unsqueeze(2).broadcast_to([P, TOPK, TOPK]),
                                     tv[:, 1, :].unsqueeze(1).broadcast_to([P, TOPK, TOPK]), ALU.add)
                    ve.drain()
                    flat = cand.rearrange("p a b -> p (a b)")
                    flat2 = cand2.rearrange("p a b -> p (a b)")
                    if not (isinstance(n, int) and n < 1):
                        ve.wait_ge(ex_done, n)
                    ve.tensor_copy(tif, ti[:, :, :])
                    ve.max(cv[:, 0:8], flat)
                    ve.drain()
                    ve.max_index(ci[:, 0:8], cv[:, 0:8], flat)
                    ve.match_replace(flat2, cv[:, 0:8], flat, LOWEST)
                    ve.tensor_scalar(nmax[:, par, :], cv[:, 0:1], -1.0, None, ALU.mult)
                    ve.drain()
                    ve.max(cv[:, 8:16], flat2)
                    ve.drain().then_inc(top_done, 1)
                    ve.max_index(ci[:, 8:16], cv[:, 8:16], flat2)
                    ve.drain()
                    ve.tensor_scalar(cab[:, 0, :], ci[:, :], 4, None, ALU.logical_shift_right)
                    ve.tensor_scalar(cab[:, 1, :], ci[:, :], 15, None, ALU.bitwise_and)
                    ve.drain()
                    entries = iota16.unsqueeze(1).broadcast_to([P, TOPK, TOPK])
                    for half, eq in ((0, eqa), (1, eqb)):
                        ve.tensor_tensor(eq, cab[:, half, :].unsqueeze(2).broadcast_to([P, TOPK, TOPK]), entries,
                                         ALU.is_equal)
                    ve.drain()
                    for half, eq in ((0, eqa), (1, eqb)):
                        ve.tensor_tensor(eq, eq, tif[:, half, :].unsqueeze(1).broadcast_to([P, TOPK, TOPK]), ALU.mult)
                    ve.drain()
                    for half, eq in ((0, eqa), (1, eqb)):
                        ve.tensor_reduce(e12[:, half, :], eq, AX, ALU.add)
                    ve.drain()
                    ve.scalar_tensor_tensor(idx[:, par, :], e12[:, 0, :], float(NKEYS), e12[:, 1, :],
                                            ALU.mult, ALU.add).then_inc(idx_ready, 1)

                def dots(n, par, T):
                    for k in range(TOPK):
                        slot = k % RING
                        ve.wait_ge(u_full[slot], n * 32 + 16 * (k // RING + 1))
                        ve.scalar_tensor_tensor(uring[:, slot, :], uring[:, slot, :], 1.0, ntok[:, T, :],
                                                ALU.mult, ALU.mult, accum_out=act[:, par, k:k + 1])\
                          .then_inc(u_used, 1)
                    ve.drain().then_inc(dots_done, 1)
                    ve.wait_ge(ex_done, n + 1)
                    ve.reciprocal(grec[:, par, :], gsum[:, par, :])
                    ve.drain()
                    ve.wait_ge(gelu_done, n + 1)
                    ve.scalar_tensor_tensor(actg[:, par, :], gel[:, par, :], grec[:, par, :], gex[:, par, :],
                                            ALU.mult, ALU.mult).then_inc(actg_done, 1)

                def add_up(n, par, T):
                    ve.drain()
                    ve.wait_ge(v_used, n * TOPK + TOPK)
                    for c in range(2):
                        a = acc[:, T, c * SEQ:(c + 1) * SEQ]
                        add = ve.tensor_tensor(a, a, banks[2 * par + c][:, :], ALU.add)
                    add.then_inc(out_used, 1)

                ve.memset(acc, 0.0)
                top(0, 0)
                dots(0, 0, 0)
                top(1, 1)

                def head(h, last=False):
                    for T in range(NT):
                        n = h * NT + T
                        if not (last and T == NT - 1):
                            dots(n + 1, (T + 1) % 2, (T + 1) % NT)
                        if not (last and T >= NT - 2):
                            top(n + 2, T % 2)
                        add_up(n, T % 2, T)

                with ve.Fori(0, HEADS - 1) as h:
                    head(h)
                head(HEADS - 1, True)
                squares_from_here("ple_a")
                for k in range(KT):
                    ve.wait_ge(back_mm, k + 1)
                    ve.tensor_tensor(hT[:, k, :], hT[:, k, :], banks[6 + k % 2][:, :], ALU.add).then_inc(back_used, 1)
                    if "ple_a" in NORM:
                        add_square(hT[:, k, :])
                squares_done("ple_a")
                barrier(ve, "peer")
            def gated(name, gate, then):
                squares_from_here(then)
                if then == "final_a":
                    ve.memset(sumsq2[:, :], 0.0)
                t0, base = TILE0[name], KT * GATED.index(name)
                for n in range(KT):
                    t = t0 + 2 * n
                    ve.wait_ge(mm_done, used(t + 1))
                    ve.wait_ge(sg_ready, base + n + 1)
                    ve.tensor_tensor(pe_in[:, n % 2, :], sg[:, n % 2, :], banks[(t + 1 - gate) % NBANK][:, :],
                                     ALU.mult).then_inc(evac_done, 2)
                    ve.drain()
                    ve.tensor_tensor(hT[:, n, :], hT[:, n, :], pe_in[:, n % 2, :], ALU.add)
                    if then in NORM:
                        add_square(hT[:, n, :])
                    if then == "final_a":
                        ve.tensor_scalar(pe_in[:, n % 2, :], hT[:, n, :], col("g_final", n), None, ALU.mult)
                        ve.drain()
                        ve.tensor_tensor(pe_in[:, n % 2, :], pe_in[:, n % 2, :], pe_in[:, n % 2, :], ALU.mult)
                        ve.drain()
                        ve.tensor_tensor(sumsq2[:, :], sumsq2[:, :], pe_in[:, n % 2, :], ALU.add)
                squares_done(then)

            def ple(name, gains, then):
                ve.wait_ge(p_loaded, 16 * (PLES.index(name) + 1))
                split_tile(ps[:, 0, :, :], pT[:, 0, :])
                split_tile(ps[:, 1, :, :], pT[:, 1, :])
                ve.drain().then_inc(p_split, 1)
                norm_apply(NORM[name], gains)
                gated(name, 0, then)
                barrier(ve, name)

            def feed_forward(i):
                if stage(f"up{i}"):
                    norm_apply(NORM[f"up{i}"], f"ffn_norm{i}")
                    base = FT * FFNS.index(f"up{i}")
                    w0 = COLS[f"ffn_w{i}"]
                    with ve.Fori(0, FT // 2) as r:
                        for u in range(2):
                            for gv in range(2):
                                buf, bank = conv[:, u, gv, :], banks[(2 * u + gv) % NBANK]
                                at = (r * 4 + (2 * u + gv)) * 3 + w0
                                ve.wait_ge(c_ready, r * 4 + (2 * base + 2 * u + gv + 1))
                                ve.scalar_tensor_tensor(buf[:, 1:], bank[:, 0:SEQ - 1], cols[:, bass.ds(at + 1, 1)],
                                                        buf[:, 1:], ALU.mult, ALU.add)
                                ve.drain()
                                ve.scalar_tensor_tensor(buf[:, 2:], bank[:, 0:SEQ - 2], cols[:, bass.ds(at, 1)],
                                                        buf[:, 2:], ALU.mult, ALU.add).then_inc(evac_done, 1)
                                done = ve.drain()
                                if gv == 0:
                                    done.then_inc(g_conv, 1)
                            ve.wait_ge(g_act, r * 2 + (base + u + 1))
                            ve.tensor_tensor(xt[:, u, :], conv[:, u, 0, :], conv[:, u, 1, :],
                                             ALU.mult).then_inc(prod_done, 1)
                            split_tile(ffz[:, r * 2 + u, :, :], xt[:, u, :])
                    barrier(ve, f"up{i}")
                if stage(f"down{i}"):
                    residual(f"down{i}", f"ple{i}")
                    barrier(ve, f"down{i}")

            def group_scale(m, x, gain, u=None):
                b = (m if u is None else u) % 2
                ve.wait_ge(gq_sqrt, m + 1)
                ve.reciprocal(gi[:, b, :], gs[:, b, :])
                ve.drain().then_inc(gq_free, 1)
                ve.scalar_tensor_tensor(x, x, gain, gi[:, b, :], ALU.mult, ALU.mult)
                ve.drain()

            def reduce_angle(x, n):
                ve.tensor_scalar(n, x, TURN, ROUND, ALU.mult, ALU.add)
                ve.drain()
                ve.tensor_scalar(n, n, ROUND, None, ALU.subtract)
                ve.drain()
                ve.scalar_tensor_tensor(x, n, -PI_HI, x, ALU.mult, ALU.add)
                ve.drain()
                ve.scalar_tensor_tensor(x, n, -PI_LO, x, ALU.mult, ALU.add)
                ve.drain()
                ve.tensor_scalar(x, x, -PI_MAX, PI_MAX, ALU.max, ALU.min)
                ve.drain()

            if stage("ple_a"):
                ple("ple_a", "g_ple", "final_a")
            if stage("final_a"):
                norm_scale(NORM["final_a"])
                ve.wait_ge(stat_mm, NORM["final_a"] + 2)
                ve.tensor_tensor(xt[:, 0, :], banks[4][:, :], rstd[:, 0, :], ALU.mult)
                ve.drain()
                ve.tensor_tensor(xt[:, 0, :], xt[:, 0, :], rstd[:, 0, :], ALU.mult)
                ve.drain().then_inc(ss_ready, 1)
                for k in range(KT):
                    ve.scalar_tensor_tensor(hT[:, k, :], hT[:, k, :], col("g_final", k), rstd[:, 0, :],
                                            ALU.mult, ALU.mult).then_inc(a_ready, 1)
                barrier(ve, "final_a")
            def mul(out, a, b):
                ve.tensor_tensor(out, a, b, ALU.mult)

            if stage("ssm_in"):
                norm_apply(NORM["ssm_in"], "ssm_norm")
                dt, ld, th, fr, fi, den, nr, ab, th8, decay8, tmp = [small[:, i, :] for i in range(11)]
                lr, li = spar[:, 0, :], spar[:, 1, :]
                G16 = [P, GROUPS, 2 * CH]

                def each(x, n):
                    return x.unsqueeze(2).broadcast_to([P, GROUPS, n])

                ve.wait_ge(ssm_loaded, 64)
                ve.wait_ge(prep, 1)
                mul(ld, lr, dt)
                mul(th, li, dt)
                ve.memset(halfpi[:, :], math.pi / 2)
                ve.tensor_scalar(nsgn[:, :], sgn, -1.0, None, ALU.mult)
                ve.drain()
                reduce_angle(th, tmp)
                powers = kpow.unsqueeze(1).broadcast_to(G16)
                mul(bigP, each(th, 2 * CH), powers)
                mul(bigM, each(ld, 2 * CH), powers)
                ve.drain()
                reduce_angle(bigP, bigN)
                ve.tensor_copy(th8, bigP[:, :, 2 * CH - 1])
                ve.drain().then_inc(prep, 1)
                ve.wait_ge(prep, 3)
                mul(AR, AR, bigM)
                mul(AI, AI, bigM)
                ve.tensor_copy(decay8, bigM[:, :, 2 * CH - 1])
                mul(den, lr, lr)
                mul(tmp, li, li)
                ve.drain()
                ve.tensor_scalar(row(AIs), row(AI), sgn, None, ALU.mult)
                ve.tensor_tensor(den, den, tmp, ALU.add)
                ve.tensor_scalar(ab, AR[:, :, CH], -1.0, None, ALU.add)
                ve.drain()
                mul(nr, ab, lr)
                mul(tmp, AI[:, :, CH], li)
                mul(fi, AI[:, :, CH], lr)
                mul(fr, ab, li)
                ve.reciprocal(den, den)
                ve.drain()
                ve.tensor_tensor(nr, nr, tmp, ALU.add)
                ve.tensor_tensor(fi, fi, fr, ALU.subtract)
                ve.drain()
                mul(fr, nr, den)
                ve.scalar_tensor_tensor(fi, fi, sgn, den, ALU.mult, ALU.mult)
                ve.drain()
                mul(bigP, each(fi, GC), bbp)
                mul(bigN, each(fi, GC), bb)
                ve.drain()
                mul(bb, each(fr, GC), bb)
                mul(bbp, each(fr, GC), bbp)
                ve.tensor_scalar(row(Cm), row(Cm), nsgn[:, :], None, ALU.mult)
                ve.drain()
                ve.tensor_tensor(bb, bb, bigP, ALU.add)
                ve.tensor_tensor(bbp, bbp, bigN, ALU.subtract)
                ve.drain()
                ve.tensor_copy(shifts[:, 0:P], ident)
                ve.memset(shifts[:, P:], 0.0)
                ve.drain().then_inc(powers_ready, 1)
                barrier(ve, "ssm_in")
            if stage("ssm"):
                th8, decay8 = small[:, 8, :], small[:, 9, :]

                def angles(n):
                    g = bass.ds(n * GT, GT)
                    ve.tensor_tensor(ph.rearrange("p (g j) -> p g j", j=NCH),
                                     th8[:, g].unsqueeze(2).broadcast_to([P, GT, NCH]),
                                     jnum.unsqueeze(1).broadcast_to([P, GT, NCH]), ALU.mult)
                    ve.tensor_copy(decay[:, :, 1:], decay8[:, g].unsqueeze(2).broadcast_to([P, GT, NCH - 1]))
                    ve.drain()
                    reduce_angle(ph, nn)
                    ve.drain().then_inc(ph_ready, 1)

                def recur(n, par, last=False):
                    ve.wait_ge(vs_ready, n + 1)
                    ve.wait_ge(tab_ready, n + 1)
                    mul(t1, vs, cosT[:, par, :])
                    ve.wait_ge(vp_mm, n + 1)
                    mul(t2, banks[5][:, :], sinT[:, par, :])
                    ve.drain()
                    ve.tensor_tensor(t1, t1, t2, ALU.add)
                    ve.drain()
                    ve.tensor_tensor_scan(yv, row(decay), t1, 0.0, ALU.mult, ALU.add)
                    ve.drain().then_inc(yv_ready, 1)
                    if not last:
                        angles(n + 1)
                    mul(t1, yv, cosT[:, par, :])
                    ve.wait_ge(yp_mm, n + 1)
                    mul(t2, banks[5][:, :], sinT[:, par, :])
                    ve.drain()
                    if not (isinstance(n, int) and n == 0):
                        ve.wait_ge(y_mm, n)
                    ve.tensor_tensor(xpad[:, :, 1:], t1.rearrange("p (g j) -> p g j", j=NCH),
                                     t2.rearrange("p (g j) -> p g j", j=NCH), ALU.subtract)
                    ve.drain().then_inc(x_ready, 1)

                ve.memset(xpad[:, :, 0:1], 0.0)
                ve.memset(decay[:, :, 0:1], 0.0)
                angles(0)
                recur(0, 0)
                recur(1, 1)
                with ve.Fori(0, KT // 2 - 2) as i:
                    for par in range(2):
                        recur(i * 2 + (par + 2), par)
                recur(KT - 2, 0)
                recur(KT - 1, 1, True)

                def total(n):
                    ve.wait_ge(y_back[n], 16)
                    ve.scalar_tensor_tensor(uperm[:, n, :], uperm[:, n, :], col("ssm_d", n), uall[:, n, :],
                                            ALU.mult, ALU.add).then_inc(y_total, 1)

                for n in range(KT - 1):
                    total(n)
                ve.wait_ge(y_mm, KT)
                for n in range(KT - 1):
                    ve.wait_ge(x_gelu, n + 1)
                    split_tile(xs[:, n, :, :], aT[:, n, :]).then_inc(x_split, 1)
                total(KT - 1)
                ve.wait_ge(x_gelu, KT)
                split_tile(xs[:, KT - 1, :, :], aT[:, KT - 1, :]).then_inc(x_split, 1)
                barrier(ve, "ssm")
            if stage("glu"):
                gated("glu", 1, "up0")
                barrier(ve, "glu")
            feed_forward(0)
            if stage("ple0"):
                ple("ple0", "ple_norm0", "kv")
            if stage("kv"):
                norm_apply(NORM["kv"], "kv_norm")
                norm_tiles("attn_norm", a2s, a2_ready)
                ve.wait_ge(kv_loaded, 48)
                ve.memset(relb[BUCKETS:BUCKETS + 1, :], NEG)
                ve.tensor_tensor(lamt[:, :, :], lamv[:, 0:4:2, :], lamv[:, 1:4:2, :], ALU.mult)
                ve.tensor_scalar(sub1[:, :], col("subln"), 1.0 - LAM_INIT, None, ALU.mult)
                ve.drain().then_inc(rel_ready, 1)
                ve.tensor_reduce(lams[:, 0:2, 0], lamt[:, :, :], AX, ALU.add)
                ve.drain().then_inc(lam_ready, 1)
                ve.drain().then_inc(gq_free, 2)
                with ve.Fori(0, HEADS // NBANK) as r:
                    for u in range(NBANK):
                        group_scale(r * NBANK + u, KQ[:, r * NBANK + u, :], col("k_norm"), u)
                for m in range(HEADS, 2 * HEADS):
                    group_scale(m, KQ[:, m, :], col("q_norm"))
                ve.wait_ge(lam_exp, 1)
                ve.scalar_tensor_tensor(nlam[:, :], lams[:, 3, :], -LAM_INIT, lams[:, 2, :],
                                        ALU.add, ALU.subtract)
                barrier(ve, "kv")
            if stage("attn"):
                ve.wait_ge(b_back, 16)
                ve.drain().then_inc(sc_free, NBANK)
                def softmax(h, qt, first=False):
                    w = (qt + 1) * P
                    near = min(w, 2 * P)
                    for c in range(2):
                        bank = banks[2 * (qt % 2) + c]
                        ve.wait_ge(at_sc, h * 8 + (2 * qt + c + 1))
                        if not first:
                            ve.wait_ge(exp_done, h * 8 + (2 * qt + c - 1))
                        ve.scalar_tensor_tensor(ss[:, c, w - near:w], bank[:, w - near:w], HD ** -0.5,
                                                near_bias[:, h, 2 * P - near:], ALU.mult, ALU.add)
                        if w > near:
                            ve.tensor_scalar(ss[:, c, 0:w - near], bank[:, 0:w - near], HD ** -0.5,
                                             cols[:, bass.ds(h + COLS["far"], 1)], ALU.mult, ALU.add)
                        ve.drain().then_inc(sc_free, 1)
                        ve.tensor_reduce(nm[:, c, :], ss[:, c, 0:w], AX, ALU.max)
                        ve.drain()
                        ve.tensor_scalar(nm[:, c, :], nm[:, c, :], -1.0, None, ALU.mult)
                        ve.drain().then_inc(mx_ready, 1)

                def combine(h, qt):
                    w, b = (qt + 1) * P, qt % 2
                    ve.wait_ge(exp_done, h * 8 + (2 * qt + 2))
                    ve.reciprocal(rr[:, :, 0], sm[:, b, :])
                    ve.drain()
                    ve.tensor_scalar(rr[:, 1, :], rr[:, 1, :], nlam[:, :], None, ALU.mult)
                    ve.drain()
                    ve.tensor_scalar(ee[:, b, 1, 0:w], ee[:, b, 1, 0:w], rr[:, 1, :], None, ALU.mult)
                    ve.drain()
                    ve.scalar_tensor_tensor(att[:, b, 0:w], ee[:, b, 0, 0:w], rr[:, 0, :], ee[:, b, 1, 0:w],
                                            ALU.mult, ALU.add).then_inc(cb_done, 1)

                def head(h, last=False):
                    combine(h, 0)
                    softmax(h, 2)
                    combine(h, 1)
                    softmax(h, 3)
                    combine(h, 2)
                    if not last:
                        softmax(h + 1, 0)
                    else:
                        ve.drain()
                    combine(h, 3)
                    if not last:
                        softmax(h + 1, 1)

                softmax(0, 0, True)
                softmax(0, 1)
                head(0)
                with ve.Fori(0, (HEADS - 2) // 2) as i:
                    head(i * 2 + 1)
                    head(i * 2 + 2)
                head(HEADS - 1, last=True)
                for h in range(HEADS):
                    group_scale(2 * HEADS + h, aT[:, h, :], sub1[:, :])
                    if stage("attn_o"):
                        split_tile(xs[:, h, :, :], aT[:, h, :]).then_inc(x_split, 1)
                barrier(ve, "attn")
            if stage("attn_o"):
                residual("attn_o", "up1")
                barrier(ve, "attn_o")
            feed_forward(1)
            if stage("ple1"):
                ple("ple1", "ple_norm1", None)
        @block.gpsimd
        def _(po):
            def tick():
                po.tensor_tensor(beat[:, 0:1], beat[:, 1:2], beat[:, 1:2], ALU.add)
                po.drain()

            def split(name):
                s0, n, w = SLAB0[name], SLABS[name], KTILES[name] * P

                def slab(s, r=0):
                    src, slot = wring[:, s % NSLOT, 0:w], s % NSPLIT
                    po.wait_ge(w_full[s % NSLOT], r * 16 + 16 * full(s))
                    if not (isinstance(r, int) and s - NSPLIT < FIRST):
                        po.wait_ge(w_used, r * NSLOT + used(s - NSPLIT + 1))
                    po.tensor_tensor(wsp[:, slot, 0, 0:w], src, one.broadcast_to([P, w]), ALU.mult)
                    po.drain()
                    po.tensor_tensor(low(wsp[:, slot, 1, 0:w]), src, wsp[:, slot, 0, 0:w], ALU.subtract)
                    po.drain().then_inc(split_done, 1)

                straight = n if s0 % NSLOT or n % NSLOT else NSLOT if s0 - NSPLIT < FIRST else 0
                for i in range(straight):
                    slab(s0 + i)
                if straight < n:
                    with po.Fori(0, (n - straight) // NSLOT) as r:
                        for u in range(NSLOT):
                            slab(s0 + straight + u, r)

            one = beat[:, 2:3]
            po.memset(beat[:, 0:2], 0.0)
            po.memset(one, 1.0)
            po.drain()
            if stage("mixer"):
                split("w_in")
            if stage("w_out"):
                split("w_out")
            if stage("w_q"):
                po.wait_ge(stage_done, after("w_q"))
            if stage("peer"):
                PACE = 1
                BEATS = 2 * TOPK // PACE

                def gather(ring, table, arrived, used_up, n, par, i, at):
                    for k in range(TOPK):
                        slot = k % RING
                        if k % PACE == 0 and not (i is None and n == 0 and k < RING):
                            if i is not None:
                                po.wait_ge(beats, i * (2 * BEATS) + (par * BEATS + at + k // PACE + 1))
                            po.wait_ge(used_up, n * TOPK + (k - RING + PACE))
                            if i is not None:
                                po.tensor_tensor(beat[:, 0:1], beat[:, 1:2], beat[:, 1:2], ALU.add)\
                                  .then_inc(beats, 1)
                        po.indirect_dma_start(ring[:, slot, :], None, table,
                                              bass.IndirectOffsetOnAxis(idx[:, par, k:k + 1], 0))\
                          .then_inc(arrived[slot], 16)

                def unit(n, par, i=None):
                    po.wait_ge(idx_ready, n + 1)
                    gather(uring, A["expert_u"], u_full, u_used, n, par, i, 0)
                    gather(vring, A["expert_v"], v_full, v_used, n, par, i, BEATS // 2)

                po.tensor_tensor(beat[:, 0:1], beat[:, 1:2], beat[:, 1:2], ALU.add).then_inc(beats, 1)
                unit(0, 0)
                unit(1, 1)
                with po.Fori(0, UNITS // 2 - 1) as i:
                    for par in range(2):
                        unit(i * 2 + (par + 2), par, i)
                po.wait_ge(beats, (UNITS - 2) * BEATS + 1)
                po.wait_ge(stage_done, after("peer"))
            for name in stages[1 + stages.index("peer") if "peer" in stages else 1:]:
                if name in ("mixer", "w_out", "w_q", "peer"):
                    continue
                def matrices(n, par):
                    grp = bass.ds(n * GT, GT)
                    for dst, a1, b1, a2, b2, i0, op, used_up, count, ready in (
                            (gmat, AR, bb, AIs, bbp, 0, ALU.add, h_mm, n - 1, g_ready),
                            (emat, AR, Cm, AI, D2, CH, ALU.subtract, y_mm, n - 1, e_ready)):
                        if not isinstance(n, int):
                            po.wait_ge(used_up, count)
                            tick()
                        dst = dst[:, par, :, :, :]
                        po.tensor_tensor(dst, a1[:, grp, i0:i0 + CH].unsqueeze(3).broadcast_to([P, GT, CH, GC]),
                                         b1[:, grp, :].unsqueeze(2).broadcast_to([P, GT, CH, GC]), ALU.mult)
                        po.tensor_tensor(gtmp, a2[:, grp, i0:i0 + CH].unsqueeze(3).broadcast_to([P, GT, CH, GC]),
                                         b2[:, grp, :].unsqueeze(2).broadcast_to([P, GT, CH, GC]), ALU.mult)
                        po.drain()
                        po.tensor_tensor(dst, dst, gtmp, op)
                        po.drain().then_inc(ready, 1)

                if name in ("ple_a", "ssm_in", "glu", "up0", "down0", "ple0", "attn_o", "up1", "down1", "ple1"):
                    split(name)
                if name == "kv":
                    for layer in ("w_k", "w_v", "attn_q"):
                        split(layer)
                if name == "ssm_in":
                    po.wait_ge(powers_ready, 1)
                    matrices(0, 0)
                    matrices(1, 1)
                if name == "ssm":
                    with po.Fori(0, KT // 2 - 1) as i:
                        for par in range(2):
                            matrices(i * 2 + (par + 2), par)
                if name in ("ssm_in", "kv"):
                    po.wait_ge(stage_done, after(name))
                elif name == "ssm":
                    po.wait_ge(y_mm, KT)
                elif name == "attn":
                    po.wait_ge(mx_ready, 2 * NT * HEADS)


def _ins():
    shapes = {"xT": (P, KT, SEQ), "cols": (P, NCOLS), "consts": (P, 5 * P + 1),
              "wsT": (P, HEADS_C, P), "vrows": (P, 2, D_C), "b_s": (1, HEADS_C * P), "keysT": (P, 2 * HEADS, P),
              "iota16": (P, TOPK), "expert_u": (NKEYS * NKEYS, D), "expert_v": (NKEYS * NKEYS, D)}
    for name, n, k, _ in LAYERS:
        shapes[name] = (n, P, k * P)
    shapes["w_q"] = (2 * HEADS, P, D)
    for name in ("ple_a", "ple0", "ple1"):
        shapes["p_" + name] = (P, 2, SEQ)
    shapes.update({"ssm_par": (P, 3, GROUPS), "ssm_bc": (P, 4, GROUPS, GC),
                   "ssm_k": (P, 2 * CH), "ssm_j": (P, NCH), "lam": (P, 4, HD), "relb": (BUCKETS, HEADS, P),
                   "onehot": (BUCKETS + 1, SKEW)})
    return shapes


def _buckets():
    exact = BUCKETS // 2
    n = np.arange(2 * P)
    nf = np.maximum(n, exact).astype(np.float32)
    large = exact + (np.log(nf / np.float32(exact)) / np.float32(math.log(MAX_DIST / exact))
                     * np.float32(BUCKETS - exact)).astype(np.int32)
    return np.where(n < exact, n, np.minimum(large, BUCKETS - 1))


def _lay_out(inputs):
    f = np.float32
    g = {k: np.asarray(v) for k, v in inputs.items()}

    def slabs(w):
        k, m = w.shape
        return np.ascontiguousarray(w.reshape(k // P, P, m // P, P).transpose(2, 1, 0, 3).reshape(m // P, P, k))

    def tiles(x):
        return np.ascontiguousarray(x.reshape(x.shape[0] // P, P, -1).transpose(1, 0, 2))

    def column(v):
        return v.reshape(-1, P).T

    out = {"xT": tiles(g["x"][0].T)}
    w_in = g["w_in"][0]
    out["w_in"] = slabs(w_in)
    out["wsT"] = np.ascontiguousarray(g["w_s"][0].transpose(2, 0, 1))
    out["vrows"] = np.ascontiguousarray(np.broadcast_to(np.stack([g["ln_c_g"][0], g["ln_c_b"][0]]), (P, 2, D_C)))
    out["b_s"] = g["b_s"][0].reshape(1, -1)
    out["w_out"], out["w_q"] = slabs(g["w_out"][0]), slabs(g["w_q"][0])
    out["keysT"] = np.ascontiguousarray(g["sub_keys"][0].reshape(2 * HEADS, NKEYS, P).transpose(2, 0, 1))
    out["iota16"] = np.ascontiguousarray(np.broadcast_to(np.arange(TOPK, dtype=f), (P, TOPK)))
    out["expert_u"], out["expert_v"] = g["expert_u"][0], g["expert_v"][0]

    def gated(wg, wp):
        return np.concatenate([slabs(wg), slabs(wp)], axis=2)

    out["ple_a"] = gated(g["w_pg"][0], g["w_pe"][0])
    out["p_ple_a"] = tiles(g["p"][0, 0].T)
    for i in range(2):
        out[f"ple{i}"] = gated(g["ple_w_gate_2"][i], g["ple_w_proj_2"][i])
        out[f"p_ple{i}"] = tiles(g["p_2"][i, 0].T)
        up = slabs(g["ffn_w_up_2"][i])
        out[f"up{i}"] = np.ascontiguousarray(up.reshape(2, FT, P, D).transpose(1, 0, 2, 3).reshape(2 * FT, P, D))
        down = slabs(g["ffn_w_down_2"][i])
        out[f"down{i}"] = np.ascontiguousarray(
            down.reshape(KT, P, 2, FF // 2).transpose(0, 2, 1, 3).reshape(2 * KT, P, FF // 2))

    def permuted(w, axis):
        s = w.shape
        w = w.reshape(s[:axis] + (KT, GT, GC) + s[axis + 1:])
        return np.ascontiguousarray(np.swapaxes(w, axis + 1, axis + 2).reshape(s))

    out["ssm_in"] = slabs(permuted(g["ssm_w_in_2"][0], 1))
    glu = slabs(permuted(g["ssm_w_glu_2"][0], 0))
    out["glu"] = np.ascontiguousarray(glu.reshape(2, KT, P, D).transpose(1, 0, 2, 3).reshape(2 * KT, P, D))
    two = lambda a, b: np.concatenate([a, b], axis=0)
    lr, li = g["ssm_lambda_re_2"][0].T, g["ssm_lambda_im_2"][0].T
    out["ssm_par"] = np.ascontiguousarray(
        np.stack([two(lr, lr), two(li, li), np.broadcast_to(g["ssm_log_dt_2"][0], (P, GROUPS))], axis=1))
    br, bi = (g[f"ssm_b_{x}_2"][0].transpose(1, 0, 2) for x in ("re", "im"))
    cr, cim = (g[f"ssm_c_{x}_2"][0].transpose(2, 0, 1) for x in ("re", "im"))
    out["ssm_bc"] = np.ascontiguousarray(np.stack([two(br, bi), two(bi, br), two(cr, cim), two(cim, cr)], axis=1))
    powers = np.concatenate([np.arange(CH - 1, -1, -1), np.arange(1, CH + 1)]).astype(f)
    out["ssm_k"] = np.ascontiguousarray(np.broadcast_to(powers, (P, 2 * CH)))
    out["ssm_j"] = np.ascontiguousarray(np.broadcast_to(np.arange(NCH, dtype=f), (P, NCH)))

    nk = 2 * HEADS * HD
    out["w_k"] = slabs(g["kv_w_2"][:, :nk])
    out["w_v"] = slabs(g["kv_w_2"][:, nk:])
    out["attn_q"], out["attn_o"] = slabs(g["attn_w_q_2"][0]), slabs(g["attn_w_o_2"][0])
    lam = np.stack([g[f"lambda_{x}_2"][0] for x in ("q1", "k1", "q2", "k2")])
    out["lam"] = np.ascontiguousarray(np.broadcast_to(lam, (P, 4, HD)))
    rb = g["rel_bias_2"]
    out["relb"] = np.ascontiguousarray(np.broadcast_to(rb[:, :, None], (BUCKETS, HEADS, P)))
    onehot = np.zeros((BUCKETS + 1, SKEW), f)
    bucket = _buckets()
    for m in range(SKEW):
        n = 2 * P - 1 - m
        onehot[bucket[n] if n >= 0 else BUCKETS, m] = 1.0
    out["onehot"] = onehot

    half = np.arange(P) // HD
    consts = [np.eye(P), np.full((P, P), 1.0 / D), (half[:, None] == half[None]) / HD,
              np.roll(np.eye(P), HD, axis=0), np.full((P, P), 1.0 / P), np.where(half, 1.0, -1.0)[:, None]]
    out["consts"] = np.concatenate(consts, axis=1).astype(f)

    c = {"g_mix": g["g_mix"], "conv_a_w": g["conv_a_w"][0], "conv_a_b": g["conv_a_b"], "ln_a_g": g["ln_a_g"],
         "ln_a_b": g["ln_a_b"], "conv_b_w": g["conv_b_w"][0], "g_ffn": g["g_ffn"], "g_ple": g["g_ple"],
         "g_final": g["g_final"], "ssm_norm": g["ssm_norm_2"], "ssm_d": permuted(g["ssm_d_2"], 1),
         "kv_norm": g["kv_norm_2"], "k_norm": two(g["k_norm_2"], g["k_norm_2"]), "attn_norm": g["attn_norm_2"],
         "q_norm": two(g["q_norm_2"][0], g["q_norm_2"][0]), "subln": g["subln_2"]}
    for i in range(2):
        c[f"ffn_norm{i}"], c[f"ple_norm{i}"] = g["ffn_norm_2"][i], g["ple_norm_2"][i]
        w = g["ffn_conv_w_2"][i].reshape(3, 2, FT, P).transpose(2, 1, 0, 3)
        c[f"ffn_w{i}"] = w
        c[f"ffn_b{i}"] = g["ffn_conv_b_2"][i].reshape(2, FT, P).transpose(1, 0, 2)
    blocks = {k: column(np.ascontiguousarray(v)) for k, v in c.items()}
    blocks["far"] = np.broadcast_to(rb[BUCKETS - 1], (P, HEADS))
    out["cols"] = np.concatenate([blocks[k] for k in COLS], axis=1)
    return {k: np.ascontiguousarray(v) for k, v in out.items()}


def kernel(**inputs):
    import concourse.bacc as bacc
    from concourse.bass_utils import run_bass_kernel_spmd

    nc = bacc.Bacc("TRN2", target_bir_lowering=False, num_devices=1)
    arrays = _lay_out(inputs)
    A = {}
    for name, shape in _ins().items():
        assert arrays[name].shape == shape, (name, arrays[name].shape, shape)
        A[name] = nc.dram_tensor(name + "_dram", shape, F32, kind="ExternalInput").ap()
    A["outT"] = nc.dram_tensor("outT_dram", (P, KT, SEQ), F32, kind="ExternalOutput").ap()
    build(nc, A)
    r = run_bass_kernel_spmd(nc, [{name + "_dram": a for name, a in arrays.items()}], core_ids=[0])
    outT = r.results[0]["outT_dram"]
    return np.ascontiguousarray(outT.transpose(1, 0, 2).reshape(D, SEQ).T)[None]
```
